# Optimizing a Trainium2 kernel written in Bass

```python
import math
import functools
import jax
import jax.numpy as jnp
from jax import lax
import numpy as np

D_MODEL = 1024
BATCH = 1
SEQ = 1024
DEPTH = 1
DEC_BATCH = 8
DEC_SEQ = 4
PAST_LEN = 1024
PAGE_SIZE = 128

NSA_HEADS = 8
NSA_KV_HEADS = 2
NSA_HPG = NSA_HEADS // NSA_KV_HEADS
NSA_HEAD_DIM = 64
CMP_BLOCK = 32
SEL_BLOCK = 64
N_SELECT = 16
WINDOW = 512
SEL_Q_BLOCK = 64
WIN_Q_BLOCK = 128
FORCE_SCORE = 1e4
REL_BUCKETS = 32
REL_MAX_DIST = 128
LRU_WIDTH = 512
LRU_BLOCKS = 8
LRU_BLOCK_DIM = LRU_WIDTH // LRU_BLOCKS
CONV_WIDTH = 4
LRU_C = 8.0
GLA_HEADS = 4
GLA_DK = 64
GLA_DV = 128
GLA_RANK = 16
GLA_TAU = 16.0
GLA_CHUNK = 64
D_FF = 4 * D_MODEL
N_BRANCH = 3
BRANCH_WIDTH = 512
NORM_EPS = 1e-6

PROJ_SPLITS = (
    ('nsa_q', NSA_HEADS * NSA_HEAD_DIM),
    ('nsa_cmp_kv', 2 * NSA_KV_HEADS * NSA_HEAD_DIM),
    ('nsa_sel_kv', 2 * NSA_KV_HEADS * NSA_HEAD_DIM),
    ('nsa_win_kv', 2 * NSA_KV_HEADS * NSA_HEAD_DIM),
    ('nsa_gate', 3 * NSA_HEADS),
    ('lru_x', LRU_WIDTH),
    ('lru_gate', LRU_WIDTH),
    ('gla_q', GLA_HEADS * GLA_DK),
    ('gla_k', GLA_HEADS * GLA_DK),
    ('gla_v', GLA_HEADS * GLA_DV),
    ('gla_alpha', GLA_RANK),
    ('gla_gate', GLA_HEADS * GLA_DV),
    ('merge_gate', N_BRANCH * D_MODEL),
)
PROJ_WIDTH = (NSA_HEADS * NSA_HEAD_DIM + 6 * NSA_KV_HEADS * NSA_HEAD_DIM + 3 * NSA_HEADS
              + 2 * LRU_WIDTH + 2 * GLA_HEADS * GLA_DK + 2 * GLA_HEADS * GLA_DV + GLA_RANK
              + N_BRANCH * D_MODEL)

kernel_name = 'hybrid_nsa_rglru_gla_decoder_step'

def _rmsnorm(x, g):
    xf = x.astype(jnp.float32)
    y = xf * lax.rsqrt(jnp.mean(xf * xf, axis=-1, keepdims=True) + NORM_EPS)
    return (y * g.astype(jnp.float32)).astype(x.dtype)

def _split_proj(p):
    out = {}
    off = 0
    for name, w in PROJ_SPLITS:
        out[name] = p[..., off:off + w]
        off += w
    return out

def _rel_bucket(dist):
    max_exact = REL_BUCKETS // 2
    n = jnp.maximum(dist, 0)
    nf = jnp.maximum(n, 1).astype(jnp.float32)
    large = max_exact + (jnp.log(nf / max_exact) / math.log(REL_MAX_DIST / max_exact)
                         * (REL_BUCKETS - max_exact)).astype(jnp.int32)
    return jnp.where(n < max_exact, n, jnp.minimum(large, REL_BUCKETS - 1))

def _bias_table(rel_bias):
    return rel_bias.astype(jnp.float32).reshape(REL_BUCKETS, NSA_KV_HEADS, NSA_HPG)

def _masked_softmax(s, mask):
    s = jnp.where(mask, s.astype(jnp.float32), -jnp.inf)
    m = jnp.max(s, axis=-1, keepdims=True)
    m = jnp.where(jnp.isfinite(m), m, 0.0)
    p = jnp.exp(s - m)
    return p / jnp.maximum(jnp.sum(p, axis=-1, keepdims=True), 1e-30)

def _nsa_compress(rows, pe, w1, w2):
    B, Tk = rows.shape[:2]
    nc = Tk // CMP_BLOCK
    blk = rows.reshape(B, nc, CMP_BLOCK, 2, NSA_KV_HEADS, NSA_HEAD_DIM) + pe[:, :, None, :]
    flat = jnp.transpose(blk, (0, 1, 3, 4, 2, 5)).reshape(B, nc, 2, NSA_KV_HEADS, CMP_BLOCK * NSA_HEAD_DIM)
    hid = jax.nn.gelu(jnp.einsum('bnzgf,zfe->bnzge', flat, w1))
    out = jnp.einsum('bnzge,zef->bnzgf', hid, w2)
    return out[:, :, 0], out[:, :, 1]

def _sel_blocks(rows):
    B, Tk = rows.shape[:2]
    r = rows.reshape(B, Tk // SEL_BLOCK, SEL_BLOCK, 2, NSA_KV_HEADS, NSA_HEAD_DIM)
    k = jnp.transpose(r[:, :, :, 0], (0, 3, 1, 2, 4))
    v = jnp.transpose(r[:, :, :, 1], (0, 3, 1, 2, 4))
    return k, v

def _nsa_cmp_sel(q, pos_q, k_c, v_c, k_sb, v_sb, rel_bias):
    B, Tq = q.shape[:2]
    nc = k_c.shape[1]
    ns = k_sb.shape[2]
    tbl = _bias_table(rel_bias)
    scale = NSA_HEAD_DIM ** -0.5
    end_c = (jnp.arange(nc, dtype=jnp.int32) + 1) * CMP_BLOCK - 1
    dist_c = pos_q[:, None] - end_c[None, :]
    bias_c = jnp.transpose(tbl[_rel_bucket(dist_c)], (2, 3, 0, 1))
    s_c = jnp.einsum('btghd,bngd->bghtn', q, k_c) * scale + bias_c
    p_c = _masked_softmax(s_c, dist_c >= 0)
    o_c = jnp.einsum('bghtn,bngd->btghd', p_c.astype(v_c.dtype), v_c)
    imp = jnp.sum(p_c, axis=2).reshape(B, NSA_KV_HEADS, Tq, ns, SEL_BLOCK // CMP_BLOCK).sum(-1)
    blk = jnp.arange(ns, dtype=jnp.int32)[None, :]
    cur = (pos_q // SEL_BLOCK)[:, None]
    forced = (blk == 0) | (blk == cur) | (blk == cur - 1)
    imp = jnp.where(forced, FORCE_SCORE, jnp.where(blk <= cur, imp, -jnp.inf))
    _, idx = lax.top_k(imp, min(N_SELECT, ns))
    kk = idx.shape[-1]
    b_ix = jnp.arange(B)[:, None, None, None]
    g_ix = jnp.arange(NSA_KV_HEADS)[None, :, None, None]
    k_g = k_sb[b_ix, g_ix, idx]
    v_g = v_sb[b_ix, g_ix, idx]
    pos_k = idx[..., None] * SEL_BLOCK + jnp.arange(SEL_BLOCK, dtype=jnp.int32)
    dist_s = pos_q[None, None, :, None, None] - pos_k
    bias_s = jnp.moveaxis(tbl[_rel_bucket(dist_s), g_ix[..., None]], -1, 2)
    s_s = jnp.einsum('btghd,bgtkld->bghtkl', q, k_g) * scale + bias_s
    p_s = _masked_softmax(s_s.reshape(B, NSA_KV_HEADS, NSA_HPG, Tq, kk * SEL_BLOCK),
                          (dist_s >= 0).reshape(B, NSA_KV_HEADS, 1, Tq, kk * SEL_BLOCK))
    p_s = p_s.reshape(B, NSA_KV_HEADS, NSA_HPG, Tq, kk, SEL_BLOCK)
    o_s = jnp.einsum('bghtkl,bgtkld->btghd', p_s.astype(v_g.dtype), v_g)
    return o_c, o_s

def _nsa_window(q, pos_q, k, v, pos_k, rel_bias):
    tbl = _bias_table(rel_bias)
    dist = pos_q[:, None] - pos_k[None, :]
    mask = (dist >= 0) & (dist < WINDOW) & (pos_k[None, :] >= 0)
    bias = jnp.transpose(tbl[_rel_bucket(dist)], (2, 3, 0, 1))
    s = jnp.einsum('btghd,bsgd->bghts', q, k) * (NSA_HEAD_DIM ** -0.5) + bias
    p = _masked_softmax(s, mask)
    return jnp.einsum('bghts,bsgd->btghd', p.astype(v.dtype), v)

def _nsa_gate_merge(pr, o_c, o_s, o_w):
    B, T = o_c.shape[:2]
    g = jax.nn.sigmoid(pr['nsa_gate'].reshape(B, T, 3, NSA_KV_HEADS, NSA_HPG, 1))
    o = g[:, :, 0] * o_c + g[:, :, 1] * o_s + g[:, :, 2] * o_w
    return o.reshape(B, T, NSA_HEADS * NSA_HEAD_DIM)

def _unblock(o, B, T):
    return jnp.moveaxis(o, 0, 1).reshape(B, T, NSA_KV_HEADS, NSA_HPG, NSA_HEAD_DIM)

def _nsa_prompt(pr, lw, rel_bias):
    B, T = pr['nsa_q'].shape[:2]
    q = pr['nsa_q'].reshape(B, T, NSA_KV_HEADS, NSA_HPG, NSA_HEAD_DIM)
    cmp_rows = pr['nsa_cmp_kv'].reshape(B, T, 2, NSA_KV_HEADS, NSA_HEAD_DIM)
    sel_rows = pr['nsa_sel_kv'].reshape(B, T, 2, NSA_KV_HEADS, NSA_HEAD_DIM)
    win_rows = pr['nsa_win_kv'].reshape(B, T, 2, NSA_KV_HEADS, NSA_HEAD_DIM)
    k_c, v_c = _nsa_compress(cmp_rows, lw['cmp_pe'], lw['cmp_w1'], lw['cmp_w2'])
    k_sb, v_sb = _sel_blocks(sel_rows)

    def cmp_sel_block(i):
        start = i * SEL_Q_BLOCK
        qb = lax.dynamic_slice_in_dim(q, start, SEL_Q_BLOCK, axis=1)
        pos = start + jnp.arange(SEL_Q_BLOCK, dtype=jnp.int32)
        return _nsa_cmp_sel(qb, pos, k_c, v_c, k_sb, v_sb, rel_bias)

    o_c, o_s = lax.map(cmp_sel_block, jnp.arange(T // SEL_Q_BLOCK, dtype=jnp.int32))
    kvp = jnp.pad(win_rows, ((0, 0), (WINDOW, 0), (0, 0), (0, 0), (0, 0)))

    def win_block(i):
        start = i * WIN_Q_BLOCK
        qb = lax.dynamic_slice_in_dim(q, start, WIN_Q_BLOCK, axis=1)
        kvb = lax.dynamic_slice_in_dim(kvp, start, WIN_Q_BLOCK + WINDOW, axis=1)
        pos_q = start + jnp.arange(WIN_Q_BLOCK, dtype=jnp.int32)
        pos_k = start - WINDOW + jnp.arange(WIN_Q_BLOCK + WINDOW, dtype=jnp.int32)
        return _nsa_window(qb, pos_q, kvb[:, :, 0], kvb[:, :, 1], pos_k, rel_bias)

    o_w = lax.map(win_block, jnp.arange(T // WIN_Q_BLOCK, dtype=jnp.int32))
    o = _nsa_gate_merge(pr, _unblock(o_c, B, T), _unblock(o_s, B, T), _unblock(o_w, B, T))
    return o, (cmp_rows, sel_rows, win_rows[:, T - min(WINDOW, T):])

def _nsa_sample(pr, lw, rel_bias, cache_cmp, cache_sel, win_buf, page_table):
    DB, S = pr['nsa_q'].shape[:2]
    past_len = page_table.shape[1] * cache_cmp.shape[1]
    tk = -(-(past_len + S) // SEL_BLOCK) * SEL_BLOCK
    q = pr['nsa_q'].reshape(DB, S, NSA_KV_HEADS, NSA_HPG, NSA_HEAD_DIM)
    cmp_rows = pr['nsa_cmp_kv'].reshape(DB, S, 2, NSA_KV_HEADS, NSA_HEAD_DIM)
    sel_rows = pr['nsa_sel_kv'].reshape(DB, S, 2, NSA_KV_HEADS, NSA_HEAD_DIM)
    win_rows = pr['nsa_win_kv'].reshape(DB, S, 2, NSA_KV_HEADS, NSA_HEAD_DIM)

    def full_rows(cache, new):
        past = cache[page_table].reshape(DB, past_len, 2, NSA_KV_HEADS, NSA_HEAD_DIM).astype(new.dtype)
        rows = jnp.concatenate([past, new], axis=1)
        return jnp.pad(rows, ((0, 0), (0, tk - past_len - S), (0, 0), (0, 0), (0, 0)))

    k_c, v_c = _nsa_compress(full_rows(cache_cmp, cmp_rows), lw['cmp_pe'], lw['cmp_w1'], lw['cmp_w2'])
    k_sb, v_sb = _sel_blocks(full_rows(cache_sel, sel_rows))
    pos_q = past_len + jnp.arange(S, dtype=jnp.int32)
    o_c, o_s = _nsa_cmp_sel(q, pos_q, k_c, v_c, k_sb, v_sb, rel_bias)
    w_buf = win_buf.shape[1]
    kv_w = jnp.concatenate([win_buf.astype(win_rows.dtype), win_rows], axis=1)
    pos_k = past_len - w_buf + jnp.arange(w_buf + S, dtype=jnp.int32)
    o_w = _nsa_window(q, pos_q, kv_w[:, :, 0], kv_w[:, :, 1], pos_k, rel_bias)
    o = _nsa_gate_merge(pr, o_c, o_s, o_w)
    return o, (cmp_rows, sel_rows, kv_w[:, S:])

def _linear_combine(e1, e2):
    a1, b1 = e1
    a2, b2 = e2
    return a1 * a2, a2 * b1 + b2

def _rglru(xb, gb, conv0, h0, lw):
    B, T, R = xb.shape
    f32 = jnp.float32
    xin = jnp.concatenate([conv0.astype(xb.dtype), xb], axis=1)
    w = lw['lru_conv_w']
    xc = lw['lru_conv_b'] + xin[:, 0:T] * w[0]
    for j in range(1, CONV_WIDTH):
        xc = xc + xin[:, j:j + T] * w[j]
    gates = jnp.einsum('btnc,znce->zbtne', xc.reshape(B, T, LRU_BLOCKS, LRU_BLOCK_DIM),
                       lw['lru_gate_w']).reshape(2, B, T, R) + lw['lru_gate_b'][:, None, None, :]
    gates = gates.astype(f32)
    r = jax.nn.sigmoid(gates[0])
    i = jax.nn.sigmoid(gates[1])
    log_a = -LRU_C * r * jax.nn.softplus(-lw['lru_lambda'].astype(f32))
    a = jnp.exp(log_a)
    b = jnp.sqrt(-jnp.expm1(2.0 * log_a)) * (i * xc.astype(f32))
    a_cum, b_cum = lax.associative_scan(_linear_combine, (a, b), axis=1)
    h = a_cum * h0.astype(f32)[:, None, :] + b_cum
    out = (jax.nn.gelu(gb.astype(f32)) * h).astype(xb.dtype)
    return out, xin[:, T:], h[:, -1].astype(h0.dtype)

def _gla(q, k, v, alr, og, s0, lw):
    B, T = q.shape[:2]
    f32 = jnp.float32
    q = q.astype(f32).reshape(B, T, GLA_HEADS, GLA_DK) * (GLA_DK ** -0.5)
    k = k.astype(f32).reshape(B, T, GLA_HEADS, GLA_DK)
    v = v.astype(f32).reshape(B, T, GLA_HEADS, GLA_DV)
    g = jax.nn.log_sigmoid((jnp.einsum('btr,re->bte', alr, lw['gla_alpha_w'])
                            + lw['gla_alpha_b']).astype(f32)) / GLA_TAU
    g = g.reshape(B, T, GLA_HEADS, GLA_DK)
    c = GLA_CHUNK if T >= GLA_CHUNK else T
    tp = -(-T // c) * c
    n = tp // c
    pad = ((0, 0), (0, tp - T), (0, 0), (0, 0))
    q, k, v, g = [jnp.pad(t, pad).reshape(B, n, c, GLA_HEADS, t.shape[-1]) for t in (q, k, v, g)]
    bc = jnp.cumsum(g, axis=2)
    bl = bc[:, :, -1]
    qi = q * jnp.exp(bc)
    ki = k * jnp.exp(-bc)
    kd = k * jnp.exp(bl[:, :, None] - bc)
    att = jnp.einsum('bnthk,bnshk->bnhts', qi, ki)
    att = jnp.where(jnp.tril(jnp.ones((c, c), dtype=bool)), att, 0.0)
    o = jnp.einsum('bnhts,bnshv->bnthv', att, v)
    ds = jnp.einsum('bnshk,bnshv->bnhkv', kd, v)

    def step(s, inp):
        ds_c, dec_c = inp
        return dec_c[..., None] * s + ds_c, s

    s_fin, s_prev = lax.scan(step, s0.astype(f32), (jnp.moveaxis(ds, 1, 0), jnp.moveaxis(jnp.exp(bl), 1, 0)))
    o = o + jnp.einsum('bnthk,bnhkv->bnthv', qi, jnp.moveaxis(s_prev, 0, 1))
    o = o.reshape(B, tp, GLA_HEADS, GLA_DV)[:, :T]
    o = _rmsnorm(o, lw['gla_norm_g'].reshape(GLA_HEADS, GLA_DV))
    o = o * jax.nn.silu(og.astype(f32).reshape(B, T, GLA_HEADS, GLA_DV))
    return o.reshape(B, T, GLA_HEADS * GLA_DV).astype(og.dtype), s_fin.astype(s0.dtype)

def _merge(o_a, o_b, o_c, gate_pre, w_branch, w_out):
    B, T = o_a.shape[:2]
    u = jnp.einsum('btzc,zcd->btzd', jnp.stack([o_a, o_b, o_c], axis=2), w_branch)
    g = jax.nn.sigmoid(gate_pre.reshape(B, T, N_BRANCH, D_MODEL))
    return jnp.einsum('btd,de->bte', jnp.sum(g * u, axis=2), w_out)

def _mlp(h, w1, w2):
    a = jax.nn.relu(jnp.einsum('btd,df->btf', h, w1))
    return jnp.einsum('btf,fd->btd', a * a, w2)

def _layer(x, lw, rel_bias, nsa_fn, conv0, h0, s0):
    h = _rmsnorm(x, lw['norm_mix_g'])
    pr = _split_proj(jnp.einsum('btd,de->bte', h, lw['w_in']) + lw['b_in'])
    o_a, nsa_state = nsa_fn(pr, lw, rel_bias)
    o_b, conv_new, h_new = _rglru(pr['lru_x'], pr['lru_gate'], conv0, h0, lw)
    o_c, s_new = _gla(pr['gla_q'], pr['gla_k'], pr['gla_v'], pr['gla_alpha'], pr['gla_gate'], s0, lw)
    x = x + _merge(o_a, o_b, o_c, pr['merge_gate'], lw['w_branch'], lw['w_out'])
    x = x + _mlp(_rmsnorm(x, lw['norm_mlp_g']), lw['mlp_w1'], lw['mlp_w2'])
    return x, nsa_state[0], nsa_state[1], nsa_state[2], conv_new, h_new, s_new

def setup_inputs(seed: int = 0) -> dict:
    key = jax.random.key(seed)
    ks = jax.random.split(key, 32)
    d = NSA_HEAD_DIM
    G = NSA_KV_HEADS

    def nrm(k, shape, scale):
        return jax.random.normal(k, shape, jnp.float32) * scale

    n_pages = PAST_LEN // PAGE_SIZE
    n_used = DEC_BATCH * n_pages
    n_pool = (5 * n_used) // 4
    w_buf = min(WINDOW, PAST_LEN)
    page_table = jax.random.permutation(ks[8], n_pool)[:n_used].reshape(DEC_BATCH, n_pages).astype(jnp.int32)
    a0 = jax.random.uniform(ks[15], (DEPTH, LRU_WIDTH), jnp.float32, 0.9, 0.999)
    sig = a0 ** (1.0 / LRU_C)
    lru_lambda = jnp.log(sig) - jnp.log1p(-sig)
    return {
        'x_prompt': nrm(ks[0], (BATCH, SEQ, D_MODEL), 1.0),
        'x_sample': nrm(ks[1], (DEC_BATCH, DEC_SEQ, D_MODEL), 1.0),
        'cache_nsa_cmp_kv': nrm(ks[2], (DEPTH, n_pool, PAGE_SIZE, 2, G, d), 1.0),
        'cache_nsa_sel_kv': nrm(ks[3], (DEPTH, n_pool, PAGE_SIZE, 2, G, d), 1.0),
        'state_nsa_win_kv': nrm(ks[4], (DEPTH, DEC_BATCH, w_buf, 2, G, d), 1.0),
        'state_lru_conv': nrm(ks[5], (DEPTH, DEC_BATCH, CONV_WIDTH - 1, LRU_WIDTH), 1.0),
        'state_lru_h': nrm(ks[6], (DEPTH, DEC_BATCH, LRU_WIDTH), 0.5),
        'state_gla': nrm(ks[7], (DEPTH, DEC_BATCH, GLA_HEADS, GLA_DK, GLA_DV), 0.5),
        'page_table': page_table,
        'rel_bias': nrm(ks[9], (REL_BUCKETS, NSA_HEADS), 0.1),
        'norm_mix_g': 1.0 + nrm(ks[10], (DEPTH, D_MODEL), 0.02),
        'norm_mlp_g': 1.0 + nrm(ks[11], (DEPTH, D_MODEL), 0.02),
        'norm_final_g': 1.0 + nrm(ks[12], (D_MODEL,), 0.02),
        'w_in': nrm(ks[13], (DEPTH, D_MODEL, PROJ_WIDTH), D_MODEL ** -0.5),
        'b_in': nrm(ks[14], (DEPTH, PROJ_WIDTH), 0.01),
        'nsa_cmp_pe': nrm(ks[16], (DEPTH, CMP_BLOCK, 2, d), 0.1),
        'nsa_cmp_w1': nrm(ks[17], (DEPTH, 2, CMP_BLOCK * d, d), (CMP_BLOCK * d) ** -0.5),
        'nsa_cmp_w2': nrm(ks[18], (DEPTH, 2, d, d), d ** -0.5),
        'lru_gate_w': nrm(ks[19], (DEPTH, 2, LRU_BLOCKS, LRU_BLOCK_DIM, LRU_BLOCK_DIM), LRU_BLOCK_DIM ** -0.5),
        'lru_gate_b': nrm(ks[20], (DEPTH, 2, LRU_WIDTH), 0.01),
        'lru_lambda': lru_lambda,
        'lru_conv_w': nrm(ks[21], (DEPTH, CONV_WIDTH, LRU_WIDTH), CONV_WIDTH ** -0.5),
        'lru_conv_b': nrm(ks[22], (DEPTH, LRU_WIDTH), 0.01),
        'gla_alpha_w': nrm(ks[23], (DEPTH, GLA_RANK, GLA_HEADS * GLA_DK), GLA_RANK ** -0.5),
        'gla_alpha_b': nrm(ks[24], (DEPTH, GLA_HEADS * GLA_DK), 0.01),
        'gla_norm_g': 1.0 + nrm(ks[25], (DEPTH, GLA_HEADS * GLA_DV), 0.02),
        'w_branch': nrm(ks[26], (DEPTH, N_BRANCH, BRANCH_WIDTH, D_MODEL), BRANCH_WIDTH ** -0.5),
        'w_out': nrm(ks[27], (DEPTH, D_MODEL, D_MODEL), D_MODEL ** -0.5),
        'mlp_w1': nrm(ks[28], (DEPTH, D_MODEL, D_FF), D_MODEL ** -0.5),
        'mlp_w2': nrm(ks[29], (DEPTH, D_FF, D_MODEL), D_FF ** -0.5),
    }

def reference(x_prompt, x_sample, cache_nsa_cmp_kv, cache_nsa_sel_kv, state_nsa_win_kv, state_lru_conv,
              state_lru_h, state_gla, page_table, rel_bias, norm_mix_g, norm_mlp_g, norm_final_g, w_in, b_in,
              nsa_cmp_pe, nsa_cmp_w1, nsa_cmp_w2, lru_gate_w, lru_gate_b, lru_lambda, lru_conv_w, lru_conv_b,
              gla_alpha_w, gla_alpha_b, gla_norm_g, w_branch, w_out, mlp_w1, mlp_w2):
    B = x_prompt.shape[0]
    xp, xs = x_prompt, x_sample
    conv0_p = jnp.zeros((B, CONV_WIDTH - 1, LRU_WIDTH), state_lru_conv.dtype)
    h0_p = jnp.zeros((B, LRU_WIDTH), state_lru_h.dtype)
    s0_p = jnp.zeros((B, GLA_HEADS, GLA_DK, GLA_DV), state_gla.dtype)
    outs_p = [[] for _ in range(6)]
    outs_s = [[] for _ in range(6)]
    for l in range(DEPTH):
        lw = {
            'norm_mix_g': norm_mix_g[l], 'norm_mlp_g': norm_mlp_g[l], 'w_in': w_in[l], 'b_in': b_in[l],
            'cmp_pe': nsa_cmp_pe[l], 'cmp_w1': nsa_cmp_w1[l], 'cmp_w2': nsa_cmp_w2[l],
            'lru_gate_w': lru_gate_w[l], 'lru_gate_b': lru_gate_b[l], 'lru_lambda': lru_lambda[l],
            'lru_conv_w': lru_conv_w[l], 'lru_conv_b': lru_conv_b[l],
            'gla_alpha_w': gla_alpha_w[l], 'gla_alpha_b': gla_alpha_b[l], 'gla_norm_g': gla_norm_g[l],
            'w_branch': w_branch[l], 'w_out': w_out[l], 'mlp_w1': mlp_w1[l], 'mlp_w2': mlp_w2[l],
        }
        xp, *st_p = _layer(xp, lw, rel_bias, _nsa_prompt, conv0_p, h0_p, s0_p)
        nsa_s = functools.partial(_nsa_sample, cache_cmp=cache_nsa_cmp_kv[l], cache_sel=cache_nsa_sel_kv[l],
                                  win_buf=state_nsa_win_kv[l], page_table=page_table)
        xs, *st_s = _layer(xs, lw, rel_bias, nsa_s, state_lru_conv[l], state_lru_h[l], state_gla[l])
        for j in range(6):
            outs_p[j].append(st_p[j])
            outs_s[j].append(st_s[j])
    y_prompt = _rmsnorm(xp, norm_final_g)
    y_sample = _rmsnorm(xs, norm_final_g)
    cmp_kv_prompt = jnp.stack(outs_p[0])
    cmp_kv_sample = jnp.stack(outs_s[0])
    sel_kv_prompt = jnp.stack(outs_p[1])
    sel_kv_sample = jnp.stack(outs_s[1])
    win_kv_prompt = jnp.stack(outs_p[2])
    win_kv_sample = jnp.stack(outs_s[2])
    lru_conv_prompt = jnp.stack(outs_p[3])
    lru_conv_sample = jnp.stack(outs_s[3])
    lru_h_prompt = jnp.stack(outs_p[4])
    lru_h_sample = jnp.stack(outs_s[4])
    gla_state_prompt = jnp.stack(outs_p[5])
    gla_state_sample = jnp.stack(outs_s[5])
    return (y_prompt, y_sample, cmp_kv_prompt, cmp_kv_sample, sel_kv_prompt, sel_kv_sample,
            win_kv_prompt, win_kv_sample, lru_conv_prompt, lru_conv_sample, lru_h_prompt, lru_h_sample,
            gla_state_prompt, gla_state_sample)


_drawn_inputs = setup_inputs


def setup_inputs(seed=0):
    import zlib

    import numpy as np

    out = dict(_drawn_inputs(seed))
    spreads = {}
    factors = {'cache_nsa_sel_kv': 3.612,
     'rel_bias': 8.0,
     'norm_mlp_g': 3.237,
     'norm_final_g': 2.891,
     'nsa_cmp_pe': 3.677,
     'lru_gate_b': 8.0,
     'gla_alpha_b': 8.0,
     'gla_norm_g': 8.0}
    for name, (base, spread) in spreads.items():
        noise = np.random.default_rng([zlib.crc32(name.encode()), seed]).standard_normal(out[name].shape)
        drawn = base * np.exp(spread * noise) if base else spread * noise
        out[name] = jnp.asarray(drawn.astype(out[name].dtype))
    for name, factor in factors.items():
        out[name] = (out[name] * factor).astype(out[name].dtype)
    return out
```

```python
from contextlib import ExitStack

import numpy as np

import concourse.bass as bass
from concourse import mybir

F32 = mybir.dt.float32
F16 = mybir.dt.float16
I32 = mybir.dt.int32
ACT = mybir.ActivationFunctionType
ALU = mybir.AluOpType
AX = mybir.AxisListType.X

P = 128
D = 1024
KD = D // P
SEQ = 1024
NB = 8
NS = 4
TS = NB * NS
T = SEQ + TS
NT = SEQ // P
CH = T // 3
PAST = 1024
PAGES = PAST // P
H, G, HPG, DH = 8, 2, 4, 64
WIN = 512
CB = 32
NCB = SEQ // CB
SB = 64
NSB = PAST // SB
R = 512
GH, GK, GV = 4, 64, 128
GC = 64
FF = 4096
EPS = 1e-6
WS = 64.0
BIG = 1e30
COL = {}
_o = 0
for _n, _w in (('q', 512), ('cmp', 256), ('sel', 256), ('win', 256), ('ngate', 24), ('lx', 512),
               ('lg', 512), ('gq', 256), ('gk', 256), ('gv', 512), ('ga', 16), ('gg', 512),
               ('merge', 3072)):
    COL[_n] = _o
    _o += _w

CN = {}
_o = 0
for _n, _w in (('ident', 128), ('ones', 128), ('winmask', 128), ('gmask', 128), ('gmask_s', 32),
               ('headsum', 128), ('tokrow', 256), ('headhot', 24), ('seqcols', 256), ('seqrows', 8),
               ('winmask_s', 4), ('blk', 16), ('bucket', 384)):
    CN[_n] = (_o, _w)
    _o += _w
CW = _o


def shape_constants():
    c = np.zeros((P, CW), np.float32)

    def put(name, a):
        o, w = CN[name]
        c[:a.shape[0], o:o + w] = a

    i, j = np.arange(P)[:, None], np.arange(P)[None, :]
    put('ident', (i == j).astype(np.float32))
    put('ones', np.ones((P, P), np.float32))
    put('winmask', np.where(j <= i, -BIG, 0.0))
    put('gmask', ((i <= j) & (i // GC == j // GC)).astype(np.float32))
    s, t = np.arange(TS)[:, None], np.arange(TS)[None, :]
    put('gmask_s', ((s <= t) & (s // NS == t // NS)).astype(np.float32))
    seq, head, tok = np.arange(P) // 32, np.arange(P) % 32 // NS, np.arange(P) % NS
    grp = head // HPG
    put('headsum', ((seq[:, None] == seq) & (grp[:, None] == grp) & (tok[:, None] == tok)).astype(np.float32))
    put('tokrow', np.concatenate([(np.arange(TS)[:, None] == (4 * hf + seq) * NS + tok).astype(np.float32)
                                  for hf in range(2)], 1))
    put('headhot', (np.arange(24)[None] % 8 == head[:, None]).astype(np.float32))
    put('seqcols', np.broadcast_to((np.arange(NB)[:, None] == np.arange(TS)[None] // NS).reshape(1, -1), (P, 256)))
    put('seqrows', (np.arange(TS)[:, None] // NS == np.arange(NB)[None]).astype(np.float32))
    put('winmask_s', np.where(np.arange(NS)[None] <= tok[:, None], -BIG, 0.0))
    put('blk', np.broadcast_to(np.arange(16.0)[None], (P, 16)))
    b = np.zeros((33, 384), np.float32)
    for col in range(384):
        d = 255 - col
        if d < 0:
            b[32, col] = 1
            continue
        n = d if d < 16 else min(31, 16 + int(np.log(max(d, 1) / 16) / np.log(8) * 16 + 1e-9))
        b[n, col] += 1
        b[31, col] -= 1
    put('bucket', b)
    return c


class Prog:

    def __init__(self, nc, d):
        self.nc, self.d = nc, d
        self.stage, self.pool = [], list(nc.free_semaphores)

    def sem(self, name):
        self.stage.append(self.nc.alloc_semaphore(name, self.pool.pop(0)))
        return self.stage[-1]

    def end_stage(self):
        self.nc.clear_and_free_semaphores(self.stage)
        self.pool += [s.num for s in self.stage]
        self.stage = []


def flat(ap):
    return ap.rearrange("p a b -> p (a b)")



VB_Q, VB_CMP, VB_SEL, VB_WIN, VB_NG, VB_LX, VB_LG = 0, 4, 6, 8, 10, 11, 15
VB_GQ, VB_GK, VB_GV, VB_GA, VB_GG, VB_MG = 19, 21, 23, 27, 28, 32
VG1, VG2, VG3 = 56, 64, 72
V_LGB, V_LAM, V_CW, V_CB, V_GAB, V_GNG = 80, 88, 92, 108, 112, 114
NV = 118
V_BQ8, V_LRC = 120, 124


def load_constants(k):
    nc, d = k.nc, k.d
    loaded, table_loaded = k.sem("c_loaded"), k.sem("c_table")
    turned, cols_ready = k.sem("c_turned"), k.sem("c_cols")
    spread, rows_made, rows_out, skewed = k.sem("c_spread"), k.sem("c_rows"), k.sem("c_rowsout"), k.sem("c_skewed")
    table_set = k.sem("c_tset")
    with nc.sbuf_tensor("vrows", [P, P], F32) as vrows, nc.sbuf_tensor("tbl", [33, H], F32) as tbl, \
            nc.sbuf_tensor("tblb", [33, H, P], F32) as tblb, nc.sbuf_tensor("brow", [P, H, 384], F32) as brow, \
            nc.Block() as block:

        @block.sync
        def _(sp):
            sp.dma_start(k.cst[:, :], d['consts']).then_inc(loaded, 16)
            b = d['b_in']
            rows = [(0, b, 0, 10), (10, b, COL['ngate'], 1), (11, b, COL['lx'], 8), (19, b, COL['gq'], 8),
                    (27, b, COL['ga'], 1), (28, b, COL['gg'], 28), (56, d['norm_mix_g'], 0, 8),
                    (64, d['norm_mlp_g'], 0, 8), (72, d['norm_final_g'], 0, 8), (80, d['lru_gate_b'], 0, 8),
                    (88, d['lru_lambda'], 0, 4), (92, d['lru_conv_w'], 0, 16), (108, d['lru_conv_b'], 0, 4),
                    (112, d['gla_alpha_b'], 0, 2), (114, d['gla_norm_g'], 0, 4)]
            for r, src, off, n in rows:
                sp.dma_start(vrows[r:r + n, :], bass.AP(tensor=src.tensor, offset=off, ap=[[P, n], [1, P]])).then_inc(loaded, 16)
            sp.wait_ge(table_set, 1)
            sp.dma_start(tbl[0:32, :], d['rel_bias']).then_inc(table_loaded, 16)
            for h in range(H):
                sp.wait_ge(rows_made, h + 1)
                sp.dma_start(k.skew[h], brow[:, h, :]).then_inc(rows_out, 16)
            sp.wait_ge(rows_out, 16 * H)

        @block.tensor
        def _(pe):
            pe.wait_ge(loaded, 16 * 16)
            nc.tensor.transpose(k.ps[:, 0, 0:NV], vrows[0:NV, :], k.c('ident')[0:NV, 0:NV]).then_inc(turned, 1)
            pe.wait_ge(spread, 1)
            for h in range(H):
                if h >= 2:
                    pe.wait_ge(rows_made, h - 1)
                nc.tensor.matmul(k.ps[:, 2 + h % 2, 0:384], tblb[:, h, :], k.c('bucket', 33),
                                 start=True, stop=True).then_inc(turned, 1)

        @block.vector
        def _(dve):
            nc.vector.memset(tbl[32:33, :], -BIG).then_inc(table_set, 1)
            dve.wait_ge(turned, 1)
            nc.vector.tensor_copy(k.vec[:, 0:NV], k.ps[:, 0, 0:NV]).then_inc(cols_ready, 1)
            dve.wait_ge(cols_ready, 1)
            nc.vector.tensor_scalar(k.vec[:, V_BQ8:V_BQ8 + 4], k.vec[:, VB_Q:VB_Q + 4], DH ** -0.5, None, ALU.mult)
            dve.wait_ge(table_set, 1)
            dve.wait_ge(table_loaded, 16)
            nc.vector.tensor_copy(tblb[:, :, :], tbl[:, :].unsqueeze(2).broadcast_to([33, H, P])).then_inc(spread, 1)

        @block.scalar
        def _(act):
            for h in range(H):
                act.wait_ge(turned, h + 2)
                nc.scalar.copy(brow[:, h, :], k.ps[:, 2 + h % 2, 0:384]).then_inc(rows_made, 1)


def load_x(k):
    nc, d = k.nc, k.d
    xl = [k.sem(f"x_loaded{i}") for i in range(3)]
    turned, copied, saved = k.sem("x_turned"), k.sem("x_copied"), k.sem("x_saved")
    xp = d['x_prompt'].rearrange("b (n p) c -> (b n) p c", p=P)
    xs = d['x_sample'].rearrange("b t c -> (b t) c")
    with nc.sbuf_tensor("xn", [P, 3, D], F32) as xn, nc.Block() as block:

        @block.sync
        def _(sp):
            for t in range(NT + 1):
                if t >= 3:
                    sp.wait_ge(turned, 2 * (t - 2))
                if t < NT:
                    sp.dma_start(xn[:, t % 3, :], xp[t]).then_inc(xl[t % 3], 16)
                else:
                    sp.dma_start(xn[0:TS, t % 3, :], xs).then_inc(xl[t % 3], 16)
            sp.wait_ge(copied, 2 * (NT + 1))
            sp.dma_start(k.xTd, flat(k.xT[:, :, :])).then_inc(saved, 16)
            sp.wait_ge(saved, 16)

        def half(u):
            t, hf = u // 2, u % 2
            n = P if t < NT else TS
            return t, hf, n

        @block.tensor
        def _(pe):
            for u in range(2 * (NT + 1)):
                t, hf, n = half(u)
                if hf == 0:
                    pe.wait_ge(xl[t % 3], 16 * (t // 3 + 1))
                if u >= 4:
                    pe.wait_ge(copied, u - 3)
                for j in range(4):
                    ins = nc.tensor.transpose(k.ps[:, u % 4, j * P:j * P + n], xn[0:n, t % 3, (4 * hf + j) * P:(4 * hf + j + 1) * P],
                                              k.c('ident')[0:n, 0:n])
                ins.then_inc(turned, 1)

        @block.scalar
        def _(act):
            for u in range(2 * (NT + 1)):
                t, hf, n = half(u)
                act.wait_ge(turned, u + 1)
                nc.scalar.copy(k.xT[:, 4 * hf:4 * hf + 4, t * P:t * P + n],
                               k.ps[:, u % 4, :].rearrange("p (j n) -> p j n", j=4)[:, :, 0:n]).then_inc(copied, 1)


def dense_out(ps, b, w=CH):
    return ps[:, 3 * b:3 * b + 3, 0:w]


def cols3(ap):
    return ap.rearrange("p (c n) -> p c n", c=3)


def norm(k, name, gcol, last=False):
    nc, xT = k.nc, k.xT
    squared, summed = k.sem(name + "_sq"), k.sem(name + "_sum")
    ms_ready, root_ready, rb_ready = k.sem(name + "_ms"), k.sem(name + "_root"), k.sem(name + "_rb")
    scaled, hi_ready, lo_ready = k.sem(name + "_scaled"), k.sem(name + "_hi"), k.sem(name + "_lo")
    with nc.sbuf_tensor(name + "sq", [P, 2, T], F32) as sq, nc.sbuf_tensor(name + "rb", [P, T], F32) as rb, \
            nc.sbuf_tensor(name + "tmp", [P, 2, T], F32) as tmp, nc.Block() as block:

        @block.scalar
        def _(act):
            for kt in range(KD):
                if kt >= 2:
                    act.wait_ge(summed, kt - 1)
                nc.scalar.activation(sq[:, kt % 2, :], xT[:, kt, :], ACT.Square).then_inc(squared, 1)
            act.wait_ge(ms_ready, 1)
            nc.scalar.activation(rb[:, :], rb[:, :], ACT.Sqrt).then_inc(root_ready, 1)
            for kt in range(0 if last else KD):
                act.wait_ge(scaled, kt + 1)
                nc.scalar.copy(k.hH[:, kt, :], tmp[:, kt % 2, :]).then_inc(hi_ready, 1)

        @block.tensor
        def _(pe):
            for kt in range(KD):
                pe.wait_ge(squared, kt + 1)
                for c in range(3):
                    ins = nc.tensor.matmul(k.ps[:, c, 0:CH], k.c('ones'), sq[:, kt % 2, c * CH:(c + 1) * CH],
                                           start=(kt == 0), stop=(kt == KD - 1))
                ins.then_inc(summed, 1)

        @block.vector
        def _(dve):
            dve.wait_ge(summed, KD)
            nc.vector.tensor_scalar(cols3(rb[:, :]), dense_out(k.ps, 0), 1.0 / D, EPS, ALU.mult, ALU.add).then_inc(ms_ready, 1)
            dve.wait_ge(root_ready, 1)
            nc.vector.reciprocal(rb[:, :], rb[:, :]).then_inc(rb_ready, 1)
            dve.wait_ge(rb_ready, 1)
            for kt in range(KD):
                if kt >= 2 and not last:
                    dve.wait_ge(lo_ready, kt - 1)
                nc.vector.scalar_tensor_tensor(xT[:, kt, :] if last else tmp[:, kt % 2, :], xT[:, kt, :], k.vec[:, gcol + kt:gcol + kt + 1],
                                               rb[:, :], ALU.mult, ALU.mult).then_inc(scaled, 1)

        @block.gpsimd
        def _(pool):
            for kt in range(0 if last else KD):
                pool.wait_ge(hi_ready, kt + 1)
                nc.gpsimd.tensor_tensor(k.hL[:, kt, :], tmp[:, kt % 2, :], k.hH[:, kt, :], ALU.subtract).then_inc(lo_ready, 1)


class Dense:

    def __init__(self, k, name, n):
        self.k, self.n = k, n
        self.loaded = [k.sem(f"{name}_w{i}") for i in range(4)]
        self.hi, self.lo = k.sem(name + "_hi"), k.sem(name + "_lo")
        self.multiplied, self.evacuated = k.sem(name + "_mult"), k.sem(name + "_evac")

    def load(self, sp, i, slot, src, first=False):
        if not first:
            sp.wait_ge(self.lo, i - 3)
        sp.dma_start(self.k.w32[:, slot, :, :], src).then_inc(self.loaded[slot], 16)

    def start_pe(self, pe):
        pe.sem_inc(self.multiplied, 2)

    def start_evac(self, eng):
        eng.sem_inc(self.evacuated, 2)

    def split_hi(self, act, i, slot, turn):
        act.wait_ge(self.loaded[slot], turn * 16 + 16)
        act.wait_ge(self.multiplied, i + 1)
        self.k.nc.scalar.activation(self.k.wH[:, slot % 2, :, :], self.k.w32[:, slot, :, :], ACT.Copy,
                                    scale=WS).then_inc(self.hi, 1)

    def split_lo(self, dve, i, slot):
        dve.wait_ge(self.hi, i + 1)
        self.k.nc.vector.scalar_tensor_tensor(self.k.wL[:, slot % 2, :, :], self.k.w32[:, slot, :, :], WS,
                                              self.k.wH[:, slot % 2, :, :], ALU.mult, ALU.subtract).then_inc(self.lo, 1)

    def multiply(self, pe, i, parity, inH, inL, ready=None):
        k, nc = self.k, self.k.nc
        pe.wait_ge(self.lo, i + 1)
        pe.wait_ge(self.evacuated, i + 1)
        wH, wL = k.wH[:, parity], k.wL[:, parity]
        for kt in range(KD):
            if ready is not None:
                ready(pe, kt)
            for w, x in ((wH, inH), (wH, inL), (wL, inH)):
                for c in range(3):
                    ins = nc.tensor.matmul(k.ps[:, 3 * parity + c, 0:CH], w[:, kt, :], x[:, kt, c * CH:(c + 1) * CH],
                                           start=(kt == 0 and x is inH and w is wH), stop=(kt == KD - 1 and w is wL))
        ins.then_inc(self.multiplied, 1)

    def multiply_all(self, pe, inH, inL):
        self.start_pe(pe)
        if self.n >= 4:
            with pe.Fori(0, self.n // 2) as j:
                self.multiply(pe, j * 2, 0, inH, inL)
                self.multiply(pe, j * 2 + 1, 1, inH, inL)
        else:
            self.multiply(pe, 0, 0, inH, inL)
            self.multiply(pe, 1, 1, inH, inL)
        if self.n % 2:
            self.multiply(pe, self.n - 1, 0, inH, inL)

    def wait_tile(self, eng, i):
        eng.wait_ge(self.multiplied, i + 3)


def w_tile(w, col, k0=0):
    return w[k0:k0 + D, bass.ds(col, P)].rearrange("(kt p) n -> p kt n", p=P)


def compress(k):
    nc, d = k.nc, k.d
    cmpT = k.cmpT
    dn = Dense(k, "cp", 2)
    with nc.Block() as block:

        @block.sync
        def _(sp):
            for i in range(2):
                dn.load(sp, i, i, w_tile(d['w_in'], COL['cmp'] + i * P), first=True)

        @block.scalar
        def _(act):
            dn.start_evac(act)
            for i in range(2):
                dn.split_hi(act, i, i, 0)
            for i in range(2):
                dn.wait_tile(act, i)
                nc.scalar.activation(cols3(cmpT[:, i, :]), dense_out(k.ps, i), ACT.Identity,
                                     bias=k.vec[:, VB_CMP + i:VB_CMP + i + 1], scale=1 / WS).then_inc(dn.evacuated, 1)

        @block.vector
        def _(dve):
            for i in range(2):
                dn.split_lo(dve, i, i)

        @block.tensor
        def _(pe):
            dn.multiply_all(pe, k.hH, k.hL)

    cleared, w_in, table_in = k.sem("cb_cleared"), k.sem("cb_win"), k.sem("cb_table")
    page_in = [k.sem(f"cb_page{s}") for s in range(PAGES)]
    page_turned, key_out, val_out = k.sem("cb_turned"), k.sem("cb_keyout"), k.sem("cb_valout")
    hid_done, hid_out, prompt_copied = k.sem("cb_hid"), k.sem("cb_hidout"), k.sem("cb_prompt")
    pe_turned, pe_copied, gelu_done, out_done, copied = (k.sem("cb_peturn"), k.sem("cb_pecopy"), k.sem("cb_gelu"),
                                                         k.sem("cb_out"), k.sem("cb_copied"))
    NBLK = NB * NCB + NCB
    with nc.sbuf_tensor("w1bd", [P, 2, CB, P], F32) as w1bd, nc.sbuf_tensor("w2bd", [P, 2, P], F32) as w2bd, \
            nc.sbuf_tensor("xc", [P, 2, 2, 2048], F32) as xc, \
            nc.sbuf_tensor("pen", [CB, 2, G, DH], F32) as pen, \
            nc.sbuf_tensor("ptab", [1, NB * PAGES], I32) as ptab, nc.Block() as block:
        cache = d['cache_nsa_cmp_kv'].rearrange("n p z g c -> p n (z g c)")
        spare = flat(k.oH[:, :, :]).bitcast(F32)
        pages = spare[:, 0:2048].rearrange("p (s n) -> p s n", s=PAGES)
        xp = spare[:, 2048:2048 + 2 * (SEQ + CB)].rearrange("p (z n) -> p z n", z=2)
        hraw = spare[:, 4160:4160 + 2 * (NBLK + 1)].rearrange("p (z n) -> p z n", z=2)
        hid = spare[:, 4738:4738 + 2 * NBLK].rearrange("p (z n) -> p z n", z=2)

        def load_page(sp, b, s):
            page = sp.value_load(ptab[0:1, bass.ds(b * PAGES + s, 1)], min_val=0, max_val=cache.shape[1] - 1)
            sp.dma_start(pages[:, s, :], cache[:, bass.ds(page, 1), :].rearrange("p o c -> p (o c)")).then_inc(page_in[s], 16)

        @block.sync
        def _(sp):
            sp.dma_start(ptab[:, :], d['page_table'].rearrange("(o a) b -> o (a b)", o=1)).then_inc(table_in, 16)
            sp.wait_ge(table_in, 16)
            for s in range(PAGES):
                load_page(sp, 0, s)
            with sp.Fori(1, NB) as b:
                for s in range(PAGES):
                    sp.wait_ge(page_turned, (b - 1) * PAGES + s + 1)
                    load_page(sp, b, s)

        @block.gpsimd
        def _(pool):
            nc.gpsimd.memset(w2bd[:, :, :], 0.0).then_inc(cleared, 1)
            nc.gpsimd.memset(w1bd[:, 0, :, :], 0.0).then_inc(cleared, 1)
            pool.wait_ge(cleared, 3)
            for g in range(G):
                r = slice(g * DH, (g + 1) * DH)
                pool.dma_start(pen[:, :, g, :], d['nsa_cmp_pe'].rearrange("l z c -> l z c")).then_inc(w_in, 16)
                for z in range(2):
                    pool.dma_start(w1bd[r, z, :, r], d['nsa_cmp_w1'][z].rearrange("(l c) e -> c l e", c=DH)).then_inc(w_in, 16)
                    pool.dma_start(w2bd[r, z, r], d['nsa_cmp_w2'][z]).then_inc(w_in, 16)

        @block.tensor
        def _(pe):
            pe.sem_inc(hid_done, 4)
            with pe.Fori(0, 2) as it:
                for pr in range(2):
                    pair = it * 2 + pr
                    for q in range(4):
                        quad = it * 8 + (pr * 4 + q)
                        pe.wait_ge(key_out, quad + 1)
                        pe.wait_ge(val_out, quad + 1)
                        for j in range(4):
                            s = (4 * q + j) % PAGES
                            pe.wait_ge(page_in[s], it * 64 + (16 * (pr * 2 + q // 2) + 16))
                            for z in range(2):
                                ins = nc.tensor.transpose(k.ps[:, 2 * (q % 2) + z, j * P:(j + 1) * P],
                                                          pages[:, s, z * P:(z + 1) * P], k.c('ident'))
                            ins.then_inc(page_turned, 1)
                    if pr == 0:
                        pe.wait_ge(w_in, 16 * 10)
                    for z in range(2):
                        n = it * 4 + (pr * 2 + z)
                        pe.wait_ge(val_out if z else key_out, it * 8 + (pr * 4 + 4 + 2))
                        pe.wait_ge(hid_out, n + 1)
                        for l in range(CB):
                            ins = nc.tensor.matmul(k.ps[:, 4 + pr * 2 + z, 0:64], w1bd[:, z, l, :], xc[:, pr, z, l:2048:CB],
                                                   start=(l == 0), stop=(l == CB - 1))
                        ins.then_inc(hid_done, 1)
            pe.wait_ge(key_out, 18)
            for z in range(2):
                ins = nc.tensor.transpose(k.ps[:, 0, z * CB:(z + 1) * CB], pen[:, z, :, :].rearrange("l g c -> l (g c)"),
                                          k.c('ident')[0:CB, 0:CB])
            ins.then_inc(pe_turned, 1)
            pe.wait_ge(pe_copied, 1)
            pe.wait_ge(prompt_copied, 1)
            for z in range(2):
                pe.wait_ge(hid_out, 8 + z + 1)
                for l in range(CB):
                    ins = nc.tensor.matmul(k.ps[:, 4 + z, 0:NCB + 1], w1bd[:, z, l, :], xp[:, z, l:SEQ + CB:CB],
                                           start=(l == 0), stop=(l == CB - 1))
                ins.then_inc(hid_done, 1)
            pe.wait_ge(gelu_done, 2)
            nc.tensor.matmul(k.ps[:, 0, 0:NBLK], w2bd[:, 0, :], hid[:, 0, :], start=True, stop=True).then_inc(out_done, 1)
            for s in range(9):
                ins = nc.tensor.matmul(k.ps[0:NCB, 1 + s // 4, (s % 4) * P:(s % 4 + 1) * P], hid[:, 1, s * NCB:(s + 1) * NCB],
                                       w2bd[:, 1, :], start=True, stop=True)
            ins.then_inc(out_done, 1)

        def quads_out(eng, copy, z, out):
            eng.sem_inc(out, 2)
            with eng.Fori(0, 2) as it:
                for pr in range(2):
                    eng.wait_ge(hid_done, it * 4 + (2 * pr + 2))
                    for q in range(4):
                        eng.wait_ge(page_turned, it * 32 + (16 * pr + 4 * q + 4))
                        copy(xc[:, pr, z, q * 512:(q + 1) * 512], k.ps[:, 2 * (q % 2) + z, :]).then_inc(out, 1)
                    if z == 0:
                        for zz in range(2):
                            eng.wait_ge(hid_done, it * 4 + (pr * 2 + zz + 5))
                            nc.scalar.copy(hraw[:, zz, bass.ds(it * 128 + pr * 64, 64)], k.ps[:, 4 + pr * 2 + zz, 0:64]).then_inc(hid_out, 1)

        @block.scalar
        def _(act):
            act.sem_inc(hid_out, 4)
            quads_out(act, nc.scalar.copy, 0, key_out)
            for z in range(2):
                act.wait_ge(hid_done, 4 + 8 + z + 1)
                nc.scalar.copy(hraw[:, z, NB * NCB:], k.ps[:, 4 + z, 0:NCB + 1]).then_inc(copied, 1)
            act.wait_ge(copied, 2)
            act.wait_ge(hid_out, 4 + 8)
            for z in range(2):
                nc.scalar.activation(hid[:, z, :], hraw[:, z, 0:NBLK], ACT.Gelu_apprx_tanh, bias=hraw[:, z, NBLK:NBLK + 1]).then_inc(gelu_done, 1)
            act.wait_ge(out_done, 1)
            nc.scalar.copy(k.kcT[:, :, :].rearrange("p s n -> p (s n)"), k.ps[:, 0, 0:NBLK])

        @block.vector
        def _(dve):
            nc.vector.memset(w1bd[:, 1, :, :], 0.0).then_inc(cleared, 1)
            quads_out(dve, nc.vector.tensor_copy, 1, val_out)
            nc.vector.tensor_copy(xp[:, :, 0:SEQ], cmpT[:, :, 0:SEQ]).then_inc(prompt_copied, 1)
            dve.wait_ge(pe_turned, 1)
            nc.vector.tensor_copy(xp[:, :, SEQ:SEQ + CB], k.ps[:, 0, 0:2 * CB].rearrange("p (z l) -> p z l", z=2)).then_inc(pe_copied, 1)
            dve.wait_ge(out_done, 2)
            nc.vector.tensor_copy(k.vcN[:, 0:8, :], k.ps[0:NCB, 1:3, :].rearrange("p b (s n) -> p (b s) n", n=P))
            nc.vector.tensor_copy(k.vcN[:, 8, :], k.ps[0:NCB, 3, 0:P])


def project_nsa(k):
    nc, d = k.nc, k.d
    cols = [COL['q'] + m * P for m in range(4)] + [COL['sel'], COL['sel'] + P, COL['win'], COL['win'] + P, COL['ngate']]
    n = len(cols)
    dn = Dense(k, "pn", n)
    with nc.sbuf_tensor("vT", [P, 2, T], F32) as vT, nc.sbuf_tensor("gT", [24, T], F32) as gT, \
            nc.sbuf_tensor("nat", [P, 3, 768], F32) as nat:
        with nc.Block() as block:

            @block.sync
            def _(sp):
                for i in range(n):
                    dn.load(sp, i, i % 4, w_tile(d['w_in'], cols[i]), first=i < 4)

            @block.scalar
            def _(act):
                dn.start_evac(act)
                dn.split_hi(act, 0, 0, 0)
                for i in range(n):
                    if i + 1 < n:
                        dn.split_hi(act, i + 1, (i + 1) % 4, (i + 1) // 4)
                    dn.wait_tile(act, i)
                    ps = dense_out(k.ps, i % 2)
                    if i < 4:
                        for u in range(2):
                            g, hh = i // 2, (2 * i + u) % HPG
                            r = slice(u * DH, (u + 1) * DH)
                            ins = nc.scalar.activation(cols3(k.qT[g * DH:(g + 1) * DH, hh, :]), ps[r], ACT.Identity,
                                                       bias=k.vec[r, V_BQ8 + i:V_BQ8 + i + 1], scale=DH ** -0.5 / WS)
                    elif i < 8:
                        out = (k.kT[:, 0, :], vT[:, 0, :], k.kT[:, 1, :], vT[:, 1, :])[i - 4]
                        b = VB_SEL + i - 4
                        ins = nc.scalar.activation(cols3(out), ps, ACT.Identity, bias=k.vec[:, b:b + 1], scale=1 / WS)
                    else:
                        ins = nc.scalar.activation(cols3(gT[:, :]), ps[0:24], ACT.Sigmoid, bias=k.vec[0:24, VB_NG:VB_NG + 1],
                                                   scale=1 / WS)
                    ins.then_inc(dn.evacuated, 1)

            @block.vector
            def _(dve):
                for i in range(n):
                    dn.split_lo(dve, i, i % 4)

            @block.tensor
            def _(pe):
                dn.multiply_all(pe, k.hH, k.hL)

        turned, first_out, second_out, vals_kept = k.sem("na_turned"), k.sem("na_out1"), k.sem("na_out2"), k.sem("na_kept")
        stored = [k.sem(f"na_stored{i}") for i in range(3)]
        other, new_turned = k.sem("na_other"), k.sem("na_new")
        with nc.Block() as block:
            rows = [P] * NT + [TS]
            outs = [(d['out_cmp_p'], d['out_cmp_s']), (d['out_sel_p'], d['out_sel_s']), (d['out_win_p'], d['out_win_s'])]

            def stores(t):
                if t == NT:
                    return [(outs[j][1][0], j) for j in range(3)]
                return [(outs[j][0][0, 0], j) for j in range(3) if j < 2 or t >= (SEQ - WIN) // P]

            @block.tensor
            def _(pe):
                for t in range(NT + 1):
                    m = rows[t]
                    if t >= 4:
                        pe.wait_ge(first_out, t - 3)
                        pe.wait_ge(second_out, t - 3)
                    for j, src in enumerate((k.cmpT[:, 0], k.cmpT[:, 1], k.kT[:, 0], vT[:, 0], k.kT[:, 1], vT[:, 1])):
                        nc.tensor.transpose(k.ps[0:m, 2 * (t % 4) + j // 4, (j % 4) * P:(j % 4 + 1) * P],
                                            src[:, t * P:t * P + m], k.c('ident'))
                    nc.tensor.transpose(k.ps[0:m, 2 * (t % 4) + 1, 256:280], gT[:, t * P:t * P + m],
                                        k.c('ident')[0:24, 0:24]).then_inc(turned, 1)
                pe.wait_ge(first_out, 8)
                pe.wait_ge(second_out, 8)
                for b in range(NB):
                    for z in range(2):
                        c = (2 * b + z) * P
                        ins = nc.tensor.transpose(k.ps[0:NS, 2 + c // 512, c % 512:c % 512 + P],
                                                  vT[:, z, SEQ + b * NS:SEQ + (b + 1) * NS], k.c('ident'))
                ins.then_inc(new_turned, 1)

            @block.scalar
            def _(act):
                for t in range(NT + 1):
                    act.wait_ge(turned, t + 1)
                    if t >= 3:
                        act.wait_ge(stored[t % 3], 16 * sum(len(stores(u)) for u in range(t % 3, t, 3)))
                        act.wait_ge(vals_kept, t - 2)
                    nc.scalar.copy(nat[0:rows[t], t % 3, 0:512], k.ps[0:rows[t], 2 * (t % 4), :]).then_inc(first_out, 1)

            @block.vector
            def _(dve):
                for t in range(NT + 1):
                    dve.wait_ge(turned, t + 1)
                    if t >= 3:
                        dve.wait_ge(stored[t % 3], 16 * sum(len(stores(u)) for u in range(t % 3, t, 3)))
                        dve.wait_ge(vals_kept, t - 2)
                    m, b = rows[t], 2 * (t % 4) + 1
                    nc.vector.tensor_copy(nat[0:m, t % 3, 512:768], k.ps[0:m, b, 0:256])
                    nc.vector.tensor_copy(k.gN[0:m, t, :], k.ps[0:m, b, 256:280]).then_inc(second_out, 1)
                dve.wait_ge(new_turned, 1)
                nc.vector.tensor_copy(k.vS[:, :, :, :].rearrange("t b z n -> t (b z n)"),
                                      k.ps[0:NS, 2:6, :].rearrange("t b n -> t (b n)"))

            @block.sync
            def _(sp):
                sp.dma_start(k.toep[:, :, :], bass.AP(tensor=k.skew.tensor, offset=P - 1,
                                                      ap=[[383, P], [384 * P, H], [1, 256]])).then_inc(other, 16)
                win_state = d['state_nsa_win_kv'].rearrange("b s z g c -> b (s z g c)")
                win_out = d['out_win_s'][0].rearrange("b s z g c -> b (s z g c)")
                sp.dma_start(win_out[:, 0:(WIN - NS) * 256], win_state[:, NS * 256:]).then_inc(other, 16)
                for t in range(NT + 1):
                    sp.wait_ge(first_out, t + 1)
                    sp.wait_ge(second_out, t + 1)
                    for out, j in stores(t):
                        src = nat[0:rows[t], t % 3, j * 256:(j + 1) * 256]
                        if t < NT:
                            r = t * P - (SEQ - WIN if j == 2 else 0)
                            sp.dma_start(out.rearrange("s z g c -> s (z g c)")[r:r + P], src).then_inc(stored[t % 3], 16)
                        elif j < 2:
                            sp.dma_start(out.rearrange("b s z g c -> (b s) (z g c)"), src).then_inc(stored[t % 3], 16)
                        else:
                            new = out.rearrange("b s z g c -> b s (z g c)")
                            for b in range(NB):
                                sp.dma_start(new[b, WIN - NS:WIN], nat[b * NS:(b + 1) * NS, t % 3, 512:768]).then_inc(other, 16)
                for r in range(3):
                    n_st = sum(len(stores(u)) - (u == NT) for u in range(r, NT + 1, 3))
                    sp.wait_ge(stored[r], 16 * n_st)
                sp.wait_ge(other, 16 * (2 + NB))

            @block.gpsimd
            def _(pool):
                for t in range(NT):
                    pool.wait_ge(first_out, t + 1)
                    pool.wait_ge(second_out, t + 1)
                    nc.gpsimd.tensor_copy(k.vN[:, t, 0, :], nat[:, t % 3, 384:512])
                    nc.gpsimd.tensor_copy(k.vN[:, t, 1, :], nat[:, t % 3, 640:768]).then_inc(vals_kept, 1)


def sample_attention(k):
    nc, d = k.nc, k.d
    HS = 4
    WT = WIN // P
    NK = PAST + NS
    names = ("q", "bias", "kturn", "kcopy", "score", "gate", "csoft", "imp", "drop", "sprep", "smax", "wprep", "wmax",
             "exp", "pturn", "pcopy", "o", "fac", "comb", "oturn", "ocopy", "tab", "page", "first", "wcopy", "cexp",
             "cprep", "cturn", "ccopy")
    s = {n: k.sem("sa_" + n) for n in names}
    key_in = [k.sem(f"sa_key{i}") for i in range(2)]
    val_in = [k.sem(f"sa_val{i}") for i in range(2)]
    with ExitStack() as es:
        sb = lambda n, sh, t=F32: es.enter_context(nc.sbuf_tensor("sa" + n, sh, t))
        spare = flat(k.oH[:, :, :]).bitcast(F32)
        spare2 = flat(k.oL[:, :, :]).bitcast(F32)
        keys = spare[:, 0:2 * 12 * P].rearrange("p (u j n) -> p u j n", u=2, j=12)
        kT = spare[:, 3072:3072 + 3072].rearrange("p (u n) -> p u n", u=2)
        vals = sb("vals", [P, HS, 12, P])
        Ss = spare2[:, 0:NK]
        Ws = spare2[:, NK:NK + WIN + NS]
        Cs = spare2[:, 1600:1632]
        PT = spare2[:, 1632:1632 + 14 * P].rearrange("p (j n) -> p j n", j=14)
        comb = spare2[:, 3500:3628]
        qbd, bias = sb("qbd", [P, NB, 32]), sb("bias", [P, 132])
        st = sb("st", [P, 64])
        imp, drop = sb("imp", [P, 16]), sb("drop", [P, 32])
        ctab, xs = sb("ctab", [P, 24]), sb("xs", [P, 120])
        PTc = sb("PTc", [NCB, P])
        ptab = sb("ptab", [1, NB * PAGES], I32)
        cache = d['cache_nsa_sel_kv'].rearrange("n p z g c -> p n z (g c)")
        state = d['state_nsa_win_kv'].rearrange("b (j p) z g c -> b z p j (g c)", p=P)
        block = es.enter_context(nc.Block())
        NEG_C, NEG_S, NEG_W, SUM_C, SUM_S, SUM_W, F_C, F_S, F_W, G3, TMP, CSUM = 0, 1, 2, 3, 4, 5, 6, 7, 8, 9, 12, 14
        col = lambda c, w=1: st[:, c:c + w]

        @block.sync
        def _(sp):
            sp.dma_start(ptab[:, :], d['page_table'].rearrange("(o a) b -> o (a b)", o=1)).then_inc(s["tab"], 16)
            for u in range(HS):
                sp.dma_start(bias[32 * u:32 * u + 32, :], bass.AP(tensor=k.skew.tensor, offset=P - 1,
                                                                   ap=[[384 * P, H], [383, NS], [1, 132]])).then_inc(s["bias"], 16)
            sp.wait_ge(s["tab"], 16)
            for b in range(NB):
                if b >= 2:
                    sp.wait_ge(s["kturn"], 3 * (b - 1))
                with sp.Fori(0, PAGES) as j:
                    page = sp.value_load(ptab[0:1, bass.ds(j + b * PAGES, 1)], min_val=0, max_val=cache.shape[1] - 1)
                    sp.dma_start(keys[:, b % 2, bass.ds(j, 1), :].rearrange("p o n -> p (o n)"),
                                 cache[:, bass.ds(page, 1), 0, :].rearrange("p o n -> p (o n)")).then_inc(key_in[b % 2], 16)
                sp.dma_start(keys[:, b % 2, PAGES:12, :], state[b, 0]).then_inc(key_in[b % 2], 16)

        @block.gpsimd
        def _(pool):
            pool.wait_ge(s["tab"], 16)
            for b in range(NB):
                if b >= HS:
                    pool.wait_ge(s["o"], 1)
                with pool.Fori(0, PAGES) as j:
                    page = pool.value_load(ptab[0:1, bass.ds(j + b * PAGES, 1)], min_val=0, max_val=cache.shape[1] - 1)
                    pool.dma_start(vals[:, b % HS, bass.ds(j, 1), :].rearrange("p o n -> p (o n)"),
                                   cache[:, bass.ds(page, 1), 1, :].rearrange("p o n -> p (o n)")).then_inc(val_in[b // HS], 16)
                pool.dma_start(vals[:, b % HS, PAGES:12, :], state[b, 1]).then_inc(val_in[b // HS], 16)

        BT, BS, BW, BX, BO = 0, 2, 4, 5, 7
        XC, XSN, XWN, XI, XG = 0, 32, 36, 64, 96

        @block.tensor
        def _(pe):
            pe.wait_ge(s["q"], 2)
            for hf in range(2):
                for u in range(HS):
                    b = hf * HS + u
                    pe.wait_ge(key_in[b % 2], 16 * 9 * (b // 2 + 1))
                    for q in range(3):
                        n = 3 * b + q
                        if n >= 2:
                            pe.wait_ge(s["kcopy"], n - 1)
                        for j in range(4):
                            ins = nc.tensor.transpose(k.ps[:, BT + n % 2, j * P:(j + 1) * P], keys[:, b % 2, 4 * q + j, :],
                                                      k.c('ident'))
                        ins.then_inc(s["kturn"], 1)
                    if hf and u == 0:
                        pe.wait_ge(s["sprep"], 2 * hf)
                        pe.wait_ge(s["wprep"], 1)
                        pe.wait_ge(s["cprep"], 2 * hf)
                        pe.wait_ge(s["fac"], 1)
                    r = slice(32 * u, 32 * u + 32)
                    nc.tensor.matmul(k.ps[r, BX, XC:XC + NCB], qbd[:, b, :], k.kcT[:, b, :], start=True, stop=True)
                    new = slice(SEQ + b * NS, SEQ + (b + 1) * NS)
                    nc.tensor.matmul(k.ps[r, BX, XSN:XSN + NS], qbd[:, b, :], k.kT[:, 0, new], start=True, stop=True)
                    nc.tensor.matmul(k.ps[r, BX, XWN:XWN + NS], qbd[:, b, :], k.kT[:, 1, new], start=True, stop=True)
                    for q in range(3):
                        pe.wait_ge(s["kcopy"], 3 * b + q + 1)
                        ins = nc.tensor.matmul(k.ps[r, BS + q if q < 2 else BW, :], qbd[:, b, :], kT[:, b % 2, q * 512:(q + 1) * 512],
                                               start=True, stop=True)
                    ins.then_inc(s["score"], 1)
                nc.tensor.matmul(k.ps[:, BX, XG:XG + 24], k.c('tokrow', TS)[:, hf * P:(hf + 1) * P], k.gN[0:TS, NT, :],
                                 start=True, stop=True).then_inc(s["gate"], 1)
                pe.wait_ge(s["csoft"], hf + 1)
                nc.tensor.matmul(k.ps[:, BX, XI:XI + NCB], k.c('headsum'), Cs, start=True, stop=True).then_inc(s["imp"], 1)
                nc.tensor.transpose(k.ps[0:NCB, 6, 0:P], Cs, k.c('ident')).then_inc(s["cturn"], 1)
                pe.wait_ge(s["ccopy"], hf + 1)
                if hf:
                    pe.wait_ge(s["comb"], 1)
                for u in range(HS):
                    b = hf * HS + u
                    nc.tensor.matmul(k.ps[32 * u:32 * u + 32, BO, 0:P], PTc[:, 32 * u:32 * u + 32], k.vcN[:, b, :],
                                     start=True, stop=True)
                pe.wait_ge(s["kcopy"], 3 * (hf * HS + HS))
                for q in range(4):
                    pe.wait_ge(s["exp"], 3 * hf + (2 if q < 2 else 3))
                    n = 4 * hf + q
                    if n >= 2:
                        pe.wait_ge(s["pcopy"], n - 1)
                    if q < 3:
                        for j in range(4):
                            src = Ss[:, (4 * q + j) * P:(4 * q + j + 1) * P] if q < 2 else Ws[:, j * P:(j + 1) * P]
                            ins = nc.tensor.transpose(k.ps[:, BT + q % 2, j * P:(j + 1) * P], src, k.c('ident'))
                    else:
                        nc.tensor.transpose(k.ps[0:NS, BT + 1, 0:P], Ss[:, PAST:NK], k.c('ident'))
                        ins = nc.tensor.transpose(k.ps[0:NS, BT + 1, P:2 * P], Ws[:, WIN:WIN + NS], k.c('ident'))
                    ins.then_inc(s["pturn"], 1)
                pe.wait_ge(val_in[hf], 16 * 9 * HS)
                pe.wait_ge(s["pcopy"], 4 * hf + 4)
                for u in range(HS):
                    b, r = hf * HS + u, slice(32 * u, 32 * u + 32)
                    for z, tiles in ((0, range(0, 8)), (1, range(8, 12))):
                        out = k.ps[r, BO, (z + 1) * P:(z + 2) * P]
                        for j in tiles:
                            nc.tensor.matmul(out, PT[:, j, r], vals[:, u, j, :], start=(j == tiles[0]), stop=False)
                        ins = nc.tensor.matmul(out, PT[0:NS, 12 + z, r], k.vS[:, b, z, :], start=False, stop=True)
                ins.then_inc(s["o"], 1)
                pe.wait_ge(s["comb"], hf + 1)
                nc.tensor.transpose(k.ps[:, 6, P:2 * P], comb, k.c('ident')).then_inc(s["oturn"], 1)

        @block.scalar
        def _(act):
            for hf in range(2):
                for b in range(hf * HS, hf * HS + HS):
                    for q in range(3):
                        act.wait_ge(s["kturn"], 3 * b + q + 1)
                        if b >= 2:
                            act.wait_ge(s["score"], b - 1)
                        nc.scalar.copy(kT[:, b % 2, q * 512:(q + 1) * 512], k.ps[:, BT + (3 * b + q) % 2, :]).then_inc(s["kcopy"], 1)
                act.wait_ge(s["cprep"], 2 * hf + 2)
                nc.scalar.activation(Cs, xs[:, XC:XC + NCB], ACT.Exp, bias=col(NEG_C), accum_out=col(SUM_C)).then_inc(s["exp"], 1)
                act.wait_ge(s["smax"], hf + 1)
                nc.scalar.activation(Ss, Ss, ACT.Exp, bias=col(NEG_S), accum_out=col(SUM_S)).then_inc(s["exp"], 1)
                act.wait_ge(s["wmax"], hf + 1)
                nc.scalar.activation(Ws, Ws, ACT.Exp, bias=col(NEG_W), accum_out=col(SUM_W)).then_inc(s["exp"], 1)
                for q in range(4):
                    act.wait_ge(s["pturn"], 4 * hf + q + 1)
                    if q < 3:
                        ins = nc.scalar.copy(PT[:, 4 * q:4 * q + 4, :].rearrange("p j n -> p (j n)"), k.ps[:, BT + q % 2, :])
                    else:
                        ins = nc.scalar.copy(PT[0:NS, 12:14, :].rearrange("p j n -> p (j n)"), k.ps[0:NS, BT + 1, 0:2 * P])
                    ins.then_inc(s["pcopy"], 1)

        @block.vector
        def _(dve):
            tt, ts, stt, red = nc.vector.tensor_tensor, nc.vector.tensor_scalar, nc.vector.scalar_tensor_tensor, nc.vector.tensor_reduce
            nc.vector.memset(qbd[:, :, :], 0.0).then_inc(s["first"], 1)
            dve.wait_ge(s["first"], 1)
            for g in range(G):
                r = slice(g * DH, (g + 1) * DH)
                for hh in range(HPG):
                    ins = nc.vector.tensor_copy(qbd[r, :, (g * HPG + hh) * NS:(g * HPG + hh + 1) * NS],
                                                k.qT[r, hh, SEQ:].rearrange("p (b t) -> p b t", b=NB))
                ins.then_inc(s["q"], 1)
            dve.wait_ge(s["bias"], 64)
            step = [0]

            def done(ins):
                step[0] += 1
                ins.then_inc(s["page"], 1)
                dve.wait_ge(s["page"], step[0])

            for hf in range(2):
                dve.wait_ge(s["score"], HS * (hf + 1))
                dve.wait_ge(s["gate"], hf + 1)
                nc.vector.tensor_copy(xs[:, XG:XG + 24], k.ps[:, BX, XG:XG + 24])
                done(nc.vector.tensor_copy(xs[:, 0:40], k.ps[:, BX, 0:40]))
                c4 = xs[:, XC + NCB - 4:XC + NCB]
                tt(c4, c4, bias[:, CB - 1:P:CB], ALU.add).then_inc(s["cprep"], 1)
                dve.wait_ge(s["cprep"], 2 * hf + 1)
                red(col(NEG_C), xs[:, XC:XC + NCB], AX, ALU.max, negate=True).then_inc(s["cprep"], 1)
                if hf:
                    dve.wait_ge(s["pcopy"], 4)
                done(nc.vector.tensor_copy(Ws[:, 0:WIN], k.ps[:, BW, :]))
                done(tt(Ws[:, 0:NS], Ws[:, 0:NS], k.c('winmask_s'), ALU.add))
                done(tt(Ws[:, WIN - P:WIN], Ws[:, WIN - P:WIN], bias[:, 0:P], ALU.add))
                done(tt(Ws[:, WIN:WIN + NS], xs[:, XWN:XWN + NS], bias[:, P:P + NS], ALU.add))
                ins = red(col(NEG_W), Ws, AX, ALU.max, negate=True)
                ins.then_inc(s["wmax"], 1)
                dve.sem_inc(s["wprep"], 1)
                dve.wait_ge(s["exp"], 3 * hf + 1)
                done(nc.vector.reciprocal(col(CSUM), col(SUM_C)))
                ts(Cs, Cs, col(CSUM), None, ALU.mult).then_inc(s["csoft"], 1)
                dve.wait_ge(s["imp"], hf + 1)
                done(red(imp[:, :], k.ps[:, BX, XI:XI + NCB].rearrange("p (b c) -> p b c", c=2), AX, ALU.add))
                done(red(col(TMP), imp[:, 1:15], AX, ALU.min))
                done(stt(drop[:, 1:15], imp[:, 1:15], col(TMP), k.c('blk')[:, 1:15], ALU.is_equal, ALU.mult))
                done(red(col(TMP), drop[:, 1:15], AX, ALU.max))
                done(ts(drop[:, 16:32], k.c('blk'), col(TMP), -BIG, ALU.is_equal, ALU.mult))
                done(tt(Ss[:, 0:PAST].rearrange("p (b n) -> p b n", n=SB), k.ps[:, BS:BS + 2, :].rearrange("p u (b n) -> p (u b) n", n=SB),
                        drop[:, 16:32].unsqueeze(2).broadcast_to([P, 16, SB]), ALU.add))
                done(tt(Ss[:, PAST - P:PAST], Ss[:, PAST - P:PAST], bias[:, 0:P], ALU.add))
                done(tt(Ss[:, PAST:NK], xs[:, XSN:XSN + NS], bias[:, P:P + NS], ALU.add))
                dve.sem_inc(s["sprep"], 2)
                red(col(NEG_S), Ss, AX, ALU.max, negate=True).then_inc(s["smax"], 1)
                dve.wait_ge(s["cturn"], hf + 1)
                nc.vector.tensor_copy(PTc[:, :], k.ps[0:NCB, 6, 0:P]).then_inc(s["ccopy"], 1)
                done(tt(ctab[:, :], xs[:, XG:XG + 24], k.c('headhot'), ALU.mult))
                done(red(col(G3, 3), ctab[:, :].rearrange("p (z h) -> p z h", z=3), AX, ALU.add))
                dve.wait_ge(s["exp"], 3 * hf + 3)
                done(nc.vector.reciprocal(col(TMP, 2), col(SUM_S, 2)))
                tt(col(F_S, 2), col(G3 + 1, 2), col(TMP, 2), ALU.mult).then_inc(s["fac"], 1)
                dve.wait_ge(s["fac"], hf + 1)
                dve.wait_ge(s["o"], hf + 1)
                done(ts(comb, k.ps[:, BO, 0:P], col(G3), None, ALU.mult))
                done(stt(comb, k.ps[:, BO, P:2 * P], col(F_S), comb, ALU.mult, ALU.add))
                stt(comb, k.ps[:, BO, 2 * P:3 * P], col(F_W), comb, ALU.mult, ALU.add).then_inc(s["comb"], 1)
                dve.wait_ge(s["oturn"], hf + 1)
                for h in range(H):
                    g, m, odd = h // HPG, h // 2, h % 2
                    nc.vector.tensor_copy(k.oTs[odd * DH:(odd + 1) * DH, m, hf * 16:hf * 16 + 16].rearrange("p (u t) -> p u t", u=HS),
                                          k.ps[g * DH:(g + 1) * DH, 6, P:2 * P].rearrange("p (u r) -> p u r", u=HS)[:, :, h * NS:(h + 1) * NS])


def prompt_attention(k):
    nc, d = k.nc, k.d
    C, S, W = range(3)
    jobs = []
    for i in range(NT):
        for g in range(G):
            for kind in (C, S, W):
                first = {C: 0, S: 0, W: max(0, i - WIN // P)}[kind]
                jobs.append((i, g, kind, [0] if kind == C else list(range(first, i + 1))))
    NJ = len(jobs)
    groups, count = [], [0, 0]
    for i, g, kind, tiles in jobs:
        mine = []
        for a in range(0, len(tiles), 4):
            bank = (count[0] + count[1]) % 2
            mine.append((bank, count[bank], count[0] + count[1], tiles[a:a + 4], a))
            count[bank] += 1
        groups.append(mine)
    NG = count[0] + count[1]
    STEPS = 3 * NJ + NJ // 3
    spare = flat(k.oL[:, :, :]).bitcast(F32)
    prob = spare[:, 0:2 * SEQ].rearrange("p (u n) -> p u n", u=2)
    probT = spare[:, 2 * SEQ:4 * SEQ].rearrange("p (u t n) -> p u t n", u=2, t=NT)
    with nc.sbuf_tensor("qslot", [P, 2, P], F32) as qslot, nc.sbuf_tensor("pastat", [P, 4, 8], F32) as stat, \
            nc.sbuf_tensor("oacc", [P, NT, R], F32) as oacc:
        q_copied, scored, maxed, exped = k.sem("pa_q"), k.sem("pa_scored"), k.sem("pa_maxed"), k.sem("pa_exped")
        turned, out_done, combined, step = k.sem("pa_turned"), k.sem("pa_o"), k.sem("pa_comb"), k.sem("pa_step")
        out = [k.sem("pa_out_v"), k.sem("pa_out_s")]
        C_SCORED, C_EXPED, C_TURNED, C_OUT, C_O, C_COMB = 12, 2, 2, 1, 2, 2
        NEG, SUM, FAC, CSUM = range(4)

        def width(j):
            i, g, kind, tiles = jobs[j]
            return 4 * (i + 1) if kind == C else P * len(tiles)

        def scores(j):
            b = 2 * (j % 2)
            w = width(j)
            return k.ps[:, b:b + 2, :].rearrange("p b n -> p (b n)")[:, 0:w]

        def turned_rows(j):
            return width(j) if jobs[j][2] == C else P

        with nc.Block() as block:

            @block.gpsimd
            def _(pool):
                with pool.Fori(0, HPG) as hh:
                    for i in range(NT):
                        pool.wait_ge(scored, hh * NJ + (6 * i + 6))
                        nc.gpsimd.tensor_copy(qslot[:, i % 2, :],
                                              k.qT[:, bass.ds(hh, 1), i * P:(i + 1) * P].rearrange("p o n -> p (o n)")).then_inc(q_copied, 1)

            @block.tensor
            def _(pe):
                pe.sem_inc(scored, C_SCORED)
                pe.sem_inc(turned, C_TURNED)
                pe.sem_inc(out_done, C_O)

                def score(hh, j):
                    i, g, kind, tiles = jobs[j]
                    r = slice(g * DH, (g + 1) * DH)
                    if j % 6 == 0:
                        pe.wait_ge(q_copied, hh * NT + i + 1)
                    pe.wait_ge(exped, hh * NJ + (j - 1 + C_EXPED))
                    w = width(j)
                    for a in range(0, w, 512):
                        n = min(512, w - a)
                        keys = k.kcT[r, 8, 0:w] if kind == C else k.kT[r, kind - 1, tiles[0] * P + a:tiles[0] * P + a + n]
                        ins = nc.tensor.matmul(scores(j)[:, a:a + n], qslot[r, i % 2, :], keys, start=True, stop=True)
                    ins.then_inc(scored, 1)

                def turn(hh, j):
                    pe.wait_ge(exped, hh * NJ + (j + 1 + C_EXPED))
                    n = turned_rows(j)
                    for bank, nth, _, tiles, a in groups[j]:
                        pe.wait_ge(out[bank], hh * count[bank] + (nth - 1 + 1 + C_OUT))
                        for u in range(len(tiles)):
                            ins = nc.tensor.transpose(k.ps[0:n, 4 + bank, u * P:(u + 1) * P],
                                                      prob[:, j % 2, (a + u) * P:(a + u) * P + n], k.c('ident'))
                        ins.then_inc(turned, 1)

                def values(hh, j):
                    i, g, kind, tiles = jobs[j]
                    for bank, nth, _, _, _ in groups[j]:
                        pe.wait_ge(out[bank], hh * count[bank] + (nth + 1 + C_OUT))
                    pe.wait_ge(combined, hh * NJ + (j - 1 + C_COMB))
                    n = turned_rows(j)
                    for u, t in enumerate(tiles):
                        v = k.vcN[0:n, 8, g * DH:(g + 1) * DH] if kind == C else k.vN[:, t, kind - 1, g * DH:(g + 1) * DH]
                        ins = nc.tensor.matmul(k.ps[:, 6 + j % 2, 0:DH], probT[0:n, j % 2, u, :], v,
                                               start=(u == 0), stop=(u == len(tiles) - 1))
                    ins.then_inc(out_done, 1)

                with pe.Fori(0, HPG) as hh:
                    for j in range(NJ + 3):
                        if j < NJ:
                            score(hh, j)
                        if 2 <= j < NJ + 2:
                            turn(hh, j - 2)
                        if j >= 3:
                            values(hh, j - 3)

            def turned_out(eng, copy, hh, j, which):
                n = turned_rows(j)
                for bank, nth, order, tiles, a in groups[j]:
                    if bank == which:
                        eng.wait_ge(turned, hh * NG + (order + 1 + C_TURNED))
                        eng.wait_ge(out_done, hh * NJ + (j - 1 + C_O))
                        w = len(tiles) * P
                        copy(probT[0:n, j % 2, a:a + len(tiles), :].rearrange("p u n -> p (u n)"),
                             k.ps[0:n, 4 + bank, 0:w]).then_inc(out[bank], 1)

            @block.scalar
            def _(act):
                act.sem_inc(exped, C_EXPED)
                act.sem_inc(out[1], C_OUT)
                with act.Fori(0, HPG) as hh:
                    for j in range(NJ + 2):
                        if j < NJ:
                            act.wait_ge(maxed, hh * NJ + (j + 1))
                            before = groups[j - 2][-1][2] + 1 if j >= 2 else (groups[j - 2][-1][2] + 1 - NG)
                            act.wait_ge(turned, hh * NG + (before + C_TURNED))
                            nc.scalar.activation(prob[:, j % 2, 0:width(j)], scores(j), ACT.Exp, bias=stat[:, NEG, j % 8:j % 8 + 1],
                                                 accum_out=stat[:, SUM, j % 8:j % 8 + 1]).then_inc(exped, 1)
                        if j >= 2:
                            turned_out(act, nc.scalar.copy, hh, j - 2, 1)

            @block.vector
            def _(dve):
                dve.sem_inc(combined, C_COMB)
                dve.sem_inc(out[0], C_OUT)
                done = [0]

                def settle(hh, ins):
                    done[0] += 1
                    ins.then_inc(step, 1)
                    dve.wait_ge(step, hh * STEPS + done[0])

                def maximum(hh, j):
                    i, g, kind, tiles = jobs[j]
                    dve.wait_ge(scored, hh * NJ + (j + 1 + C_SCORED))
                    sc, w = scores(j), width(j)
                    near = min(2, i + 1)
                    bias = k.toep[:, bass.ds(hh + g * HPG, 1), (2 - near) * P:2 * P].rearrange("p o n -> p (o n)")
                    if kind == C:
                        part = sc[:, w - 4 * near:w]
                        ins = nc.vector.tensor_tensor(part, part, bias[:, CB - 1::CB], ALU.add)
                    else:
                        if kind == W and len(tiles) == WIN // P + 1:
                            nc.vector.tensor_tensor(sc[:, 0:P], sc[:, 0:P], k.c('winmask'), ALU.add)
                        part = sc[:, w - near * P:w]
                        ins = nc.vector.tensor_tensor(part, part, bias, ALU.add)
                    settle(hh, ins)
                    neg = stat[:, NEG, j % 8:j % 8 + 1]
                    ins = nc.vector.tensor_reduce(neg, sc, AX, ALU.max, negate=True)
                    if kind == C:
                        settle(hh, ins)
                        ins = nc.vector.tensor_scalar(neg, neg, 1e20, None, ALU.min)
                    ins.then_inc(maxed, 1)

                def combine(hh, j):
                    i, g, kind, tiles = jobs[j]
                    dve.wait_ge(exped, hh * NJ + (j + 1 + C_EXPED))
                    one = slice(j % 8, j % 8 + 1)
                    total = stat[:, SUM, one]
                    if kind == C:
                        settle(hh, nc.vector.tensor_scalar(stat[:, CSUM, one], total, 1e-30, None, ALU.max))
                        total = stat[:, CSUM, one]
                    rcp = stat[:, FAC, one]
                    settle(hh, nc.vector.reciprocal(rcp, total))
                    gate = k.gN[:, i, bass.ds(hh + (kind * H + g * HPG), 1)]
                    if kind != C:
                        settle(hh, nc.vector.tensor_tensor(rcp, gate, rcp, ALU.mult))
                    dve.wait_ge(out_done, hh * NJ + (j + 1 + C_O))
                    o = k.ps[:, 6 + j % 2, 0:DH]
                    acc = oacc[:, i, bass.ds((hh + g * HPG) * DH, DH)]
                    if kind == C:
                        ins = nc.vector.tensor_scalar(acc, o, rcp, gate, ALU.mult, ALU.mult)
                    else:
                        dve.wait_ge(combined, hh * NJ + (j + C_COMB))
                        ins = nc.vector.scalar_tensor_tensor(acc, o, rcp, acc, ALU.mult, ALU.add)
                    ins.then_inc(combined, 1)

                with dve.Fori(0, HPG) as hh:
                    for j in range(NJ + 3):
                        if j < NJ:
                            maximum(hh, j)
                        if 2 <= j < NJ + 2:
                            turned_out(dve, nc.vector.tensor_copy, hh, j - 2, 0)
                        if j >= 3:
                            combine(hh, j - 3)
                    assert done[0] == STEPS

        t_turned, t_hi, t_lo = k.sem("pt_turned"), k.sem("pt_hi"), k.sem("pt_lo")
        with nc.Block() as block:

            @block.tensor
            def _(pe):
                for t in range(NT):
                    if t >= 4:
                        pe.wait_ge(t_lo, t - 3)
                    for m in range(4):
                        ins = nc.tensor.transpose(k.ps[:, t % 4, m * P:(m + 1) * P], oacc[:, t, m * P:(m + 1) * P], k.c('ident'))
                    ins.then_inc(t_turned, 1)

            def tile(buf, t):
                return buf[:, 0:4, t * P:(t + 1) * P]

            def bank(t):
                return k.ps[:, t % 4, :].rearrange("p (m n) -> p m n", m=4)

            @block.scalar
            def _(act):
                for t in range(NT):
                    act.wait_ge(t_turned, t + 1)
                    nc.scalar.copy(tile(k.oH, t), bank(t)).then_inc(t_hi, 1)
                nc.scalar.copy(k.oH[:, 0:4, SEQ:], k.oTs[:, :, :]).then_inc(t_hi, 1)

            @block.vector
            def _(dve):
                for t in range(NT):
                    dve.wait_ge(t_hi, t + 1)
                    nc.vector.tensor_tensor(tile(k.oL, t), bank(t), tile(k.oH, t), ALU.subtract).then_inc(t_lo, 1)
                dve.wait_ge(t_hi, NT + 1)
                nc.vector.tensor_tensor(k.oL[:, 0:4, SEQ:], k.oTs[:, :, :], k.oH[:, 0:4, SEQ:], ALU.subtract)


def lru(k):
    nc, d = k.nc, k.d
    MT = R // P
    CWD = 4
    n = 2 * MT
    dn = Dense(k, "lrp", n)
    s = {x: k.sem("lr_" + x) for x in ("in", "cleared", "gw", "sturn", "conv", "gate", "gsig", "expo",
                                       "tanh", "quot", "root", "beta", "scan", "prod", "hi", "lam", "lexp", "step", "pack",
                                       "pturn", "pout", "stored", "taps")}
    with ExitStack() as es:
        sb = lambda nm, sh, t=F32: es.enter_context(nc.sbuf_tensor("lr" + nm, sh, t))
        xin, xs = sb("xin", [P, MT, 3 + SEQ]), sb("xs", [P, MT, NB, 3 + NS])
        gg, xc = sb("gg", [P, MT, T]), sb("xc", [P, MT, T])
        rg, ig = sb("rg", [P, MT, T]), sb("ig", [P, MT, T])
        gw = sb("gw", [P, 2, MT, P])
        srow, h0, lam = sb("srow", [32, R]), sb("h0", [P, MT, NB]), sb("lam", [P, 6, MT])
        a5, b5, h5 = sb("a5", [P, NB, NS + 1]), sb("b5", [P, NB, NS + 1]), sb("h5", [P, MT, NB, NS + 1])
        pack, prow = sb("pack", [P, MT, 36]), sb("prow", [36, R])
        with nc.Block() as block:

            @block.sync
            def _(sp):
                sp.dma_start(srow[0:24, :], d['state_lru_conv'].rearrange("b j c -> (b j) c")).then_inc(s["in"], 16)
                sp.dma_start(srow[24:32, :], d['state_lru_h']).then_inc(s["in"], 16)
                for i in range(n):
                    dn.load(sp, i, i % 4, w_tile(d['w_in'], COL['lg' if i % 2 else 'lx'] + i // 2 * P), first=i < 4)
                sp.wait_ge(s["cleared"], 1)
                for z in range(2):
                    for u in range(2):
                        r = slice(u * 64, (u + 1) * 64)
                        sp.dma_start(gw[r, z, :, r], d['lru_gate_w'][z].rearrange("(m u) c e -> u c m e", u=2)[u]).then_inc(s["gw"], 16)
                sp.wait_ge(s["gw"], 64)

            @block.gpsimd
            def _(pool):
                nc.gpsimd.memset(gw[:, :, :, :], 0.0).then_inc(s["cleared"], 1)
                nc.gpsimd.memset(xin[:, :, 0:3], 0.0)

            @block.scalar
            def _(act):
                dn.start_evac(act)
                dn.split_hi(act, 0, 0, 0)
                for i in range(n):
                    if i + 1 < n:
                        dn.split_hi(act, i + 1, (i + 1) % 4, (i + 1) // 4)
                    dn.wait_tile(act, i)
                    m = i // 2
                    if i % 2:
                        nc.scalar.activation(cols3(gg[:, m, :]), dense_out(k.ps, 1), ACT.Gelu_apprx_tanh,
                                             bias=k.vec[:, VB_LG + m:VB_LG + m + 1], scale=1 / WS).then_inc(dn.evacuated, 1)
                    else:
                        b = k.vec[:, VB_LX + m:VB_LX + m + 1]
                        ins = nc.scalar.activation(cols3(rg[:, m, :]), dense_out(k.ps, 0), ACT.Identity, bias=b, scale=1 / WS)
                        ins.then_inc(dn.evacuated, 1)

            @block.vector
            def _(dve):
                for i in range(n):
                    dn.split_lo(dve, i, i % 4)
                    if i % 2:
                        m = i // 2
                        dve.wait_ge(dn.evacuated, 2 * m + 1 + 2)
                        nc.vector.tensor_copy(xin[:, m, 3:], rg[:, m, 0:SEQ])
                        nc.vector.tensor_copy(xs[:, m, :, 3:], rg[:, m, SEQ:].rearrange("p (b t) -> p b t", b=NB))
                dve.wait_ge(s["sturn"], 1)
                states = k.ps[:, 7, 0:P].rearrange("p (m r) -> p m r", m=MT)
                nc.vector.tensor_copy(h0[:, :, :], states[:, :, 24:32])
                for m in range(MT):
                    nc.vector.tensor_copy(xs[:, m, :, 0:3], states[:, m, 0:24].rearrange("p (b j) -> p b j", b=NB))

            @block.tensor
            def _(pe):
                pe.wait_ge(s["in"], 32)
                for m in range(MT):
                    ins = nc.tensor.transpose(k.ps[:, 7, m * 32:(m + 1) * 32], srow[:, m * P:(m + 1) * P], k.c('ident')[0:32, 0:32])
                ins.then_inc(s["sturn"], 1)
                dn.multiply_all(pe, k.hH, k.hL)

        vec = lambda c: k.vec[:, c:c + 1]
        with nc.Block() as block:

            @block.vector
            def _(dve):
                tt, ts, stt = nc.vector.tensor_tensor, nc.vector.tensor_scalar, nc.vector.scalar_tensor_tensor
                step = [0]

                def settle(ins):
                    step[0] += 1
                    ins.then_inc(s["step"], 1)
                    dve.wait_ge(s["step"], step[0])

                LV = k.vec[:, V_LAM:V_LAM + MT]
                settle(ts(lam[:, 0, :], LV, -1.0, None, ALU.mult))
                settle(tt(lam[:, 0, :], LV, lam[:, 0, :], ALU.max))
                ts(lam[:, 1, :], LV, -1.0, 0.0, ALU.mult, ALU.max).then_inc(s["lam"], 1)
                dve.wait_ge(s["lexp"], 1)
                z, w, w2, poly = lam[:, 2, :], lam[:, 3, :], lam[:, 4, :], lam[:, 5, :]
                settle(ts(w, z, 2.0, None, ALU.add))
                settle(nc.vector.reciprocal(w, w))
                settle(tt(w, w, z, ALU.mult))
                settle(tt(w2, w, w, ALU.mult))
                settle(ts(poly, w2, 1 / 17, 1 / 15, ALU.mult, ALU.add))
                for q in (13, 11, 9, 7, 5, 3, 1):
                    settle(tt(poly, poly, w2, ALU.mult))
                    settle(ts(poly, poly, 1 / q, None, ALU.add))
                settle(tt(poly, poly, w, ALU.mult))
                settle(stt(poly, poly, 2.0, lam[:, 1, :], ALU.mult, ALU.add))
                settle(ts(k.vec[:, V_LRC:V_LRC + MT], poly, -8.0, None, ALU.mult))
                ts(lam[:, 0, :], poly, 8.0, None, ALU.mult).then_inc(s["lam"], 1)

                for m in range(MT):
                    xcs = xc[:, m, SEQ:].rearrange("p (b t) -> p b t", b=NB)
                    ts(xc[:, m, 0:SEQ], xin[:, m, 0:SEQ], vec(V_CW + m), vec(V_CB + m), ALU.mult, ALU.add).then_inc(s["taps"], 1)
                    ts(xcs, xs[:, m, :, 0:NS], vec(V_CW + m), vec(V_CB + m), ALU.mult, ALU.add).then_inc(s["taps"], 1)
                    for j in range(1, CWD):
                        dve.wait_ge(s["taps"], 8 * m + 2 * j)
                        ins = stt(xc[:, m, 0:SEQ], xin[:, m, j:j + SEQ], vec(V_CW + 4 * j + m), xc[:, m, 0:SEQ], ALU.mult, ALU.add)
                        ins.then_inc(s["taps"], 1)
                        ins = stt(xcs, xs[:, m, :, j:j + NS], vec(V_CW + 4 * j + m), xcs, ALU.mult, ALU.add)
                        ins.then_inc(s["taps"], 1)
                    dve.wait_ge(s["taps"], 8 * m + 8)
                    nc.vector.tensor_copy(pack[:, m, 0:3], xin[:, m, SEQ:SEQ + 3])
                    ins = nc.vector.tensor_copy(pack[:, m, 3:27].rearrange("p (b j) -> p b j", b=NB), xs[:, m, :, NS:NS + 3])
                    ins.then_inc(s["conv"], 1)
                for m in range(MT):
                    dve.wait_ge(s["gsig"], 2 * m + 2)
                    ins = tt(ig[:, m, :], ig[:, m, :], xc[:, m, :], ALU.mult).then_inc(s["beta"], 1)
                for m in range(MT):
                    dve.wait_ge(s["tanh"], m + 1)
                    one_u = xin[:, m, 0:SEQ]
                    one_us = h5[:, m, :, 0:NS]
                    us = rg[:, m, SEQ:].rearrange("p (b t) -> p b t", b=NB)
                    settle(ts(one_u, rg[:, m, 0:SEQ], 1.0, None, ALU.add))
                    settle(ts(one_us, us, 1.0, None, ALU.add))
                    settle(nc.vector.reciprocal(one_u, one_u))
                    settle(nc.vector.reciprocal(one_us, one_us))
                    tt(rg[:, m, 0:SEQ], rg[:, m, 0:SEQ], one_u, ALU.mult)
                    tt(us, us, one_us, ALU.mult).then_inc(s["quot"], 1)
                settle(nc.vector.memset(a5[:, :, 0:1], 0.0))
                for m in range(MT):
                    dve.wait_ge(s["root"], m + 1)
                    settle(tt(ig[:, m, :], ig[:, m, :], rg[:, m, :], ALU.mult))
                    nc.vector.tensor_copy(b5[:, :, 0:1], h0[:, m, :].unsqueeze(2))
                    nc.vector.tensor_copy(b5[:, :, 1:], ig[:, m, SEQ:].rearrange("p (b t) -> p b t", b=NB))
                    settle(nc.vector.tensor_copy(a5[:, :, 1:], xc[:, m, SEQ:].rearrange("p (b t) -> p b t", b=NB)))
                    nc.vector.tensor_tensor_scan(rg[:, m, 0:SEQ], xc[:, m, 0:SEQ], ig[:, m, 0:SEQ], 0.0, ALU.mult, ALU.add)
                    settle(nc.vector.tensor_tensor_scan(h5[:, m, :, :].rearrange("p b t -> p (b t)"), a5[:, :, :].rearrange("p b t -> p (b t)"),
                                                        b5[:, :, :].rearrange("p b t -> p (b t)"), 0.0, ALU.mult, ALU.add))
                    nc.vector.tensor_copy(pack[:, m, 27:28], rg[:, m, SEQ - 1:SEQ])
                    nc.vector.tensor_copy(pack[:, m, 28:36], h5[:, m, :, NS]).then_inc(s["pack"], 1)
                    tt(gg[:, m, 0:SEQ], gg[:, m, 0:SEQ], rg[:, m, 0:SEQ], ALU.mult)
                    gs = gg[:, m, SEQ:].rearrange("p (b t) -> p b t", b=NB)
                    tt(gs, gs, h5[:, m, :, 1:], ALU.mult).then_inc(s["prod"], 1)
                dve.wait_ge(s["pturn"], 1)
                nc.vector.tensor_copy(prow[:, :], k.ps[0:36, 7, :]).then_inc(s["pout"], 1)

            @block.tensor
            def _(pe):
                for m in range(MT):
                    pe.wait_ge(s["conv"], m + 1)
                    for z in range(2):
                        if m >= 1:
                            pe.wait_ge(s["gsig"], 2 * m + z - 1)
                        for c in range(3):
                            ins = nc.tensor.matmul(k.ps[:, 3 * z + c, 0:CH], gw[:, z, m, :], xc[:, m, c * CH:(c + 1) * CH],
                                                   start=True, stop=True)
                        ins.then_inc(s["gate"], 1)
                pe.wait_ge(s["pack"], MT)
                for m in range(MT):
                    ins = nc.tensor.transpose(k.ps[0:36, 7, m * P:(m + 1) * P], pack[:, m, :], k.c('ident'))
                ins.then_inc(s["pturn"], 1)

            @block.scalar
            def _(act):
                act.wait_ge(s["lam"], 1)
                nc.scalar.activation(lam[:, 2, :], lam[:, 0, :], ACT.Exp, scale=-1.0).then_inc(s["lexp"], 1)
                for m in range(MT):
                    for z in range(2):
                        act.wait_ge(s["gate"], 2 * m + z + 1)
                        nc.scalar.activation(cols3((rg, ig)[z][:, m, :]), dense_out(k.ps, z), ACT.Sigmoid,
                                             bias=vec(V_LGB + 4 * z + m)).then_inc(s["gsig"], 1)
                act.wait_ge(s["lam"], 2)
                for m in range(MT):
                    act.wait_ge(s["beta"], m + 1)
                    act.wait_ge(s["gsig"], 2 * m + 1)
                    nc.scalar.activation(xc[:, m, :], rg[:, m, :], ACT.Exp, scale=vec(V_LRC + m)).then_inc(s["expo"], 1)
                    nc.scalar.activation(rg[:, m, :], rg[:, m, :], ACT.Tanh, scale=lam[:, 0, m:m + 1]).then_inc(s["tanh"], 1)
                for m in range(MT):
                    act.wait_ge(s["quot"], m + 1)
                    nc.scalar.activation(rg[:, m, :], rg[:, m, :], ACT.Sqrt, scale=2.0).then_inc(s["root"], 1)
                for m in range(MT):
                    act.wait_ge(s["prod"], m + 1)
                    nc.scalar.copy(k.oH[:, 4 + m, :], gg[:, m, :]).then_inc(s["hi"], 1)

            @block.gpsimd
            def _(pool):
                for m in range(MT):
                    pool.wait_ge(s["hi"], m + 1)
                    nc.gpsimd.tensor_tensor(k.oL[:, 4 + m, :], gg[:, m, :], k.oH[:, 4 + m, :], ALU.subtract)

            @block.sync
            def _(sp):
                sp.wait_ge(s["pout"], 1)
                for rows, out in ((prow[0:3, :], d['out_conv_p'][0, 0]), (prow[3:27, :], d['out_conv_s'][0].rearrange("b j c -> (b j) c")),
                                  (prow[27:28, :], d['out_h_p'][0]), (prow[28:36, :], d['out_h_s'][0])):
                    sp.dma_start(out, rows).then_inc(s["stored"], 16)
                sp.wait_ge(s["stored"], 64)


def gla(k):
    nc, d = k.nc, k.d
    n = 13
    cols = [COL['gq'] + i * P for i in range(8)] + [COL['ga']] + [COL['gg'] + i * P for i in range(4)]
    dn = Dense(k, "glp", n)
    NC = SEQ // GC
    s = {x: k.sem("gl_" + x) for x in ("aw", "x", "abs", "exp", "ln", "g", "cum", "gate", "alpha", "init", "step", "e1", "em", "ed", "dec",
                                       "qi", "ki", "kd", "tr", "vout", "kout", "att", "attm", "ds", "state", "o", "sq", "ms",
                                       "root", "on", "ot", "res", "hi", "lo", "s0", "mask", "qm", "kdm", "stored", "q2")}
    with ExitStack() as es:
        sb = lambda nm, sh, t=F32: es.enter_context(nc.sbuf_tensor("gl" + nm, sh, t))
        kk, vT, sg = sb("k", [P, 2, T]), sb("v", [P, 4, T]), sb("sg", [P, 4, T])
        q2 = sb("q", [P, 2, 2, T])
        q = q2[:, 1]
        aT, aw, reset = sb("aT", [16, T]), sb("aw", [16, 256]), sb("reset", [P, T])
        ki, kd = sb("ki", [P, 2, T]), sb("kd", [P, 2, T])
        gx = k.oH[:, 8:12, :].rearrange("p a b -> p (a b)").bitcast(F32).rearrange("p (m t) -> p m t", m=2)
        bc = k.oL[:, 8:12, :].rearrange("p a b -> p (a b)").bitcast(F32).rearrange("p (m t) -> p m t", m=2)
        dec, dec_s = sb("dec", [P, 2, NC]), sb("decs", [P, 2 * NB])
        with nc.Block() as block:

            @block.sync
            def _(sp):
                sp.dma_start(aw[:, :], d['gla_alpha_w']).then_inc(s["aw"], 16)
                for i in range(n):
                    dn.load(sp, i, i % 4, w_tile(d['w_in'], cols[i]), first=i < 4)
                sp.wait_ge(s["aw"], 16)

            @block.scalar
            def _(act):
                dn.start_evac(act)
                dn.split_hi(act, 0, 0, 0)
                for i in range(n):
                    if i + 1 < n:
                        dn.split_hi(act, i + 1, (i + 1) % 4, (i + 1) // 4)
                    dn.wait_tile(act, i)
                    ps = dense_out(k.ps, i % 2)
                    if i < 8:
                        out = (q[:, 0], q[:, 1], kk[:, 0], kk[:, 1], vT[:, 0], vT[:, 1], vT[:, 2], vT[:, 3])[i]
                        ins = nc.scalar.activation(cols3(out), ps, ACT.Identity, bias=k.vec[:, VB_GQ + i:VB_GQ + i + 1], scale=1 / WS)
                    elif i == 8:
                        ins = nc.scalar.activation(cols3(aT[:, :]), ps[0:16], ACT.Identity, bias=k.vec[0:16, VB_GA:VB_GA + 1], scale=1 / WS)
                    else:
                        h = i - 9
                        ins = nc.scalar.activation(cols3(sg[:, h, :]), ps, ACT.Silu, bias=k.vec[:, VB_GG + h:VB_GG + h + 1], scale=1 / WS)
                    ins.then_inc(dn.evacuated, 1)

            @block.vector
            def _(dve):
                nc.vector.memset(reset[:, :], 1.0).then_inc(s["init"], 1)
                dve.wait_ge(s["init"], 1)
                nc.vector.memset(reset[:, 0:SEQ:GC], 0.0)
                nc.vector.memset(reset[:, SEQ:T:NS], 0.0)
                for i in range(n):
                    dn.split_lo(dve, i, i % 4)

            @block.gpsimd
            def _(pool):
                for h in range(GH):
                    pool.wait_ge(dn.evacuated, 2 + 10 + h)
                    nc.gpsimd.tensor_scalar(sg[:, h, :], sg[:, h, :], k.vec[:, V_GNG + h:V_GNG + h + 1], None, ALU.mult)

            @block.tensor
            def _(pe):
                dn.multiply_all(pe, k.hH, k.hL)

        def chunks(ap):
            return ((ap[:, 0:SEQ].rearrange("p (c t) -> p c t", t=GC), ap[:, GC - 1:SEQ:GC]),
                    (ap[:, SEQ:].rearrange("p (c t) -> p c t", t=NS), ap[:, SEQ + NS - 1::NS]))

        with nc.Block() as block:

            @block.tensor
            def _(pe):
                for m in range(2):
                    for c in range(3):
                        ins = nc.tensor.matmul(k.ps[:, 3 * m + c, 0:CH], aw[:, m * P:(m + 1) * P], aT[:, c * CH:(c + 1) * CH],
                                               start=True, stop=True)
                    ins.then_inc(s["alpha"], 1)

            @block.scalar
            def _(act):
                for m in range(2):
                    act.wait_ge(s["alpha"], m + 1)
                    nc.scalar.activation(cols3(gx[:, m, :]), dense_out(k.ps, m), ACT.Identity, bias=k.vec[:, V_GAB + m:V_GAB + m + 1]).then_inc(s["x"], 1)
                for m in range(2):
                    act.wait_ge(s["abs"], m + 1)
                    nc.scalar.activation(ki[:, m, :], ki[:, m, :], ACT.Exp, scale=-1.0).then_inc(s["exp"], 1)
                    act.wait_ge(s["exp"], m + 1)
                    nc.scalar.activation(ki[:, m, :], ki[:, m, :], ACT.Ln, bias=1.0).then_inc(s["ln"], 1)
                for m in range(2):
                    act.wait_ge(s["cum"], 2 * m + 2)
                    nc.scalar.activation(gx[:, m, :], bc[:, m, :], ACT.Exp, scale=1 / 16).then_inc(s["e1"], 1)
                    nc.scalar.activation(ki[:, m, :], bc[:, m, :], ACT.Exp, scale=-1 / 16).then_inc(s["em"], 1)
                    nc.scalar.activation(kd[:, m, :], kd[:, m, :], ACT.Exp, scale=1 / 16).then_inc(s["ed"], 1)
                    nc.scalar.activation(dec[:, m, :], bc[:, m, GC - 1:SEQ:GC], ACT.Exp, scale=1 / 16)
                    nc.scalar.activation(dec_s[:, m::2], bc[:, m, SEQ + NS - 1::NS], ACT.Exp, scale=1 / 16)

            @block.vector
            def _(dve):
                tt, stt = nc.vector.tensor_tensor, nc.vector.scalar_tensor_tensor
                for m in range(2):
                    dve.wait_ge(s["x"], m + 1)
                    stt(ki[:, m, :], gx[:, m, :], -1.0, gx[:, m, :], ALU.mult, ALU.max).then_inc(s["abs"], 1)
                for m in range(2):
                    dve.wait_ge(s["ln"], m + 1)
                    stt(gx[:, m, :], gx[:, m, :], 0.0, ki[:, m, :], ALU.min, ALU.subtract).then_inc(s["g"], 1)
                    dve.wait_ge(s["g"], m + 1)
                    nc.vector.tensor_tensor_scan(bc[:, m, :], reset[:, :], gx[:, m, :], 0.0, ALU.mult, ALU.add).then_inc(s["cum"], 1)
                    dve.wait_ge(s["cum"], 2 * m + 1)
                    for (whole, last), (out, _) in zip(chunks(bc[:, m, :]), chunks(kd[:, m, :])):
                        ins = stt(out, whole, -1.0, last.unsqueeze(2).broadcast_to(whole.shape), ALU.mult, ALU.add)
                    ins.then_inc(s["cum"], 1)
                for m in range(2):
                    dve.wait_ge(s["e1"], m + 1)
                    for u in range(2):
                        r = slice(u * GK, (u + 1) * GK)
                        ins = stt(q2[r, u, m, :], q[r, m, :], GK ** -0.5, gx[r, m, :], ALU.mult, ALU.mult)
                    ins.then_inc(s["q2"], 1)
                    dve.wait_ge(s["em"], m + 1)
                    tt(ki[:, m, :], kk[:, m, :], ki[:, m, :], ALU.mult)
                    dve.wait_ge(s["ed"], m + 1)
                    tt(kd[:, m, :], kk[:, m, :], kd[:, m, :], ALU.mult)
                dve.wait_ge(s["q2"], 2)
                for u in range(2):
                    nc.vector.memset(q2[(1 - u) * GK:(2 - u) * GK, u], 0.0)

        rows = [P] * NT + [TS]
        vN, kN = sb("vN", [P, 2, 512]), sb("kN", [P, 2, 256])
        stat = sb("stat", [P, 2, 4])
        slots = k.w32[:, :, :, :].rearrange("p a b c -> p (a b c)")
        S = slots[:, 0:1024].rearrange("p (s m v) -> p s m v", s=4, m=2)
        sq, on = slots[:, 3072:3584], slots[:, 3584:4096]
        att, res = (w[:, :, :, :].rearrange("p a b c -> p (a b c)").bitcast(F32).rearrange("p (s n) -> p s n", s=2)
                    for w in (k.wH, k.wL))
        spare = kk[:, :, :].rearrange("p m t -> p (m t)")
        S0 = spare[:, 0:2048].rearrange("p (b m v) -> p b m v", b=NB, m=2)
        reset_f = reset[:, :]
        qm = reset_f[:, 0:1024].rearrange("p (u m b t) -> p u m b t", u=2, m=2, b=NB)
        kdm = slots[0:TS, 1024:3072].rearrange("p (b n) -> p b n", b=NB)
        BV, BK, BA, BD, BO, BT = 0, 1, 2, (3, 5), 4, 6
        with nc.Block() as block:

            @block.sync
            def _(sp):
                for m in range(2):
                    sp.dma_start(S0[:, :, m, :], d['state_gla'].rearrange("b (m u) k v -> m (u k) b v", m=2)[m]).then_inc(s["s0"], 16)
                sp.wait_ge(s["state"], 1 + NC)
                sp.dma_start(d['out_gla_p'][0, 0].rearrange("(m u) k v -> (u k) m v", m=2), S[:, NC % 4]).then_inc(s["stored"], 16)
                sp.wait_ge(s["state"], 1 + NC + 2)
                for m in range(2):
                    sp.dma_start(d['out_gla_s'][0].rearrange("b (m u) k v -> m (u k) b v", m=2)[m], S0[:, :, m, :]).then_inc(s["stored"], 16)
                sp.wait_ge(s["stored"], 48)

            def hp(h):
                return slice(h % 2 * GK, h % 2 * GK + GK)

            def turn_out(pe, t):
                w = rows[t]
                pe.wait_ge(s["on"], t + 1)
                if t:
                    pe.wait_ge(s["res"], t)
                for h in range(GH):
                    ins = nc.tensor.transpose(k.ps[:, BT, h * P:h * P + w], on[0:w, h * P:(h + 1) * P], k.c('ident')[0:w, 0:w])
                ins.then_inc(s["ot"], 1)

            def heads(ap, w=P):
                return ap.rearrange("p (h n) -> p h n", h=GH)[:, :, 0:w]

            def after(act, t):
                w = rows[t]
                act.wait_ge(s["o"], t + 1)
                if t:
                    act.wait_ge(s["ms"], 2 * t)
                nc.scalar.activation(sq[0:w, :], k.ps[0:w, BO, :], ACT.Square).then_inc(s["sq"], 1)
                act.wait_ge(s["ms"], 2 * t + 2)
                nc.scalar.activation(stat[0:w, t % 2, :], stat[0:w, t % 2, :], ACT.Sqrt).then_inc(s["root"], 1)
                act.wait_ge(s["res"], t + 1)
                c = slice(t * P, t * P + w)
                nc.scalar.copy(k.oH[:, 8:12, c], heads(res[:, t % 2, :], w)).then_inc(s["hi"], 1)

            def finish(dve, t):
                w, c = rows[t], slice(t * P, t * P + rows[t])
                st = stat[0:w, t % 2, :]
                dve.wait_ge(s["sq"], t + 1)
                nc.vector.tensor_reduce(st, heads(sq[0:w, :]), AX, ALU.add).then_inc(s["ms"], 1)
                dve.wait_ge(s["ms"], 2 * t + 1)
                nc.vector.tensor_scalar(st, st, 1.0 / GV, EPS, ALU.mult, ALU.add).then_inc(s["ms"], 1)
                dve.wait_ge(s["root"], t + 1)
                nc.vector.reciprocal(st, st).then_inc(s["step"], 1)
                dve.wait_ge(s["step"], t + 1)
                nc.vector.tensor_tensor(heads(on[0:w, :]), heads(k.ps[0:w, BO, :]), st.unsqueeze(2).broadcast_to([w, GH, GV]),
                                        ALU.mult).then_inc(s["on"], 1)
                dve.wait_ge(s["ot"], t + 1)
                if t >= 2:
                    dve.wait_ge(s["lo"], t - 1)
                nc.vector.tensor_tensor(heads(res[:, t % 2, :], w), heads(k.ps[:, BT, :], w), sg[:, :, c], ALU.mult).then_inc(s["res"], 1)

            @block.tensor
            def _(pe):
                def turn(t):
                    w, c = rows[t], slice(t * P, t * P + rows[t])
                    if t >= 1:
                        pe.wait_ge(s["vout"], t)
                        pe.wait_ge(s["kout"], t)
                    for h in range(GH):
                        nc.tensor.transpose(k.ps[0:w, BV, h * P:(h + 1) * P], vT[:, h, c], k.c('ident'))
                    for m in range(2):
                        ins = nc.tensor.transpose(k.ps[0:w, BK, m * P:(m + 1) * P], kd[:, m, c], k.c('ident'))
                    ins.then_inc(s["tr"], 1)

                turn(0)
                for t in range(NT + 1):
                    w, c = rows[t], slice(t * P, t * P + rows[t])
                    if t:
                        pe.wait_ge(s["attm"], t)
                    for h in range(GH):
                        ins = nc.tensor.matmul(k.ps[0:w, BA, h * P:h * P + w], ki[:, h // 2, c], q2[:, h % 2, h // 2, c], start=True, stop=True)
                    ins.then_inc(s["att"], 1)
                    if t < NT:
                        turn(t + 1)
                    pe.wait_ge(s["vout"], t + 1)
                    pe.wait_ge(s["kout"], t + 1)
                    if t < NT:
                        if t:
                            pe.wait_ge(s["state"], 1 + 2 * t)
                        for ch in range(2):
                            r = slice(ch * GC, (ch + 1) * GC)
                            for h in range(GH):
                                ins = nc.tensor.matmul(k.ps[hp(h), BD[ch], h // 2 * GV:(h // 2 + 1) * GV],
                                                       kN[r, t % 2, h * GK:(h + 1) * GK], vN[r, t % 2, h * GV:(h + 1) * GV], start=True, stop=True)
                        ins.then_inc(s["ds"], 1)
                    pe.wait_ge(s["attm"], t + 1)
                    if t:
                        pe.wait_ge(s["on"], t)
                    ob = BO
                    for h in range(GH):
                        nc.tensor.matmul(k.ps[0:w, ob, h * GV:(h + 1) * GV], att[0:w, t % 2, h * P:h * P + w], vN[0:w, t % 2, h * GV:(h + 1) * GV],
                                         start=True, stop=False)
                        if t < NT:
                            for ch in range(2):
                                n_ch = 2 * t + ch
                                pe.wait_ge(s["state"], 1 + n_ch)
                                cc = slice(t * P + ch * GC, t * P + (ch + 1) * GC)
                                ins = nc.tensor.matmul(k.ps[ch * GC:(ch + 1) * GC, ob, h * GV:(h + 1) * GV], q2[:, h % 2, h // 2, cc],
                                                       S[:, n_ch % 4, h // 2, :], start=False, stop=True)
                        else:
                            pe.wait_ge(s["s0"], 32)
                            pe.wait_ge(s["qm"], 4)
                            for b in range(NB):
                                ins = nc.tensor.matmul(k.ps[0:w, ob, h * GV:(h + 1) * GV], qm[:, h % 2, h // 2, b, :], S0[:, b, h // 2, :],
                                                       start=False, stop=(b == NB - 1))
                    ins.then_inc(s["o"], 1)
                    if t:
                        turn_out(pe, t - 1)
                pe.wait_ge(s["kdm"], 1)
                pe.wait_ge(s["attm"], NT + 1)
                pe.wait_ge(s["state"], 1 + NC)
                for b in range(NB):
                    for h in range(GH):
                        o = b % 2 * 256 + h // 2 * GV
                        ins = nc.tensor.matmul(k.ps[hp(h), b // 2, o:o + GV], kdm[:, b, h * GK:(h + 1) * GK], vN[0:TS, NT % 2, h * GV:(h + 1) * GV],
                                               start=True, stop=True)
                ins.then_inc(s["ds"], 1)
                turn_out(pe, NT)

            @block.scalar
            def _(act):
                for t in range(NT + 1):
                    w = rows[t]
                    act.wait_ge(s["tr"], t + 1)
                    if t >= 2:
                        act.wait_ge(s["o"], t - 1)
                    nc.scalar.copy(vN[0:w, t % 2, :], k.ps[0:w, BV, :]).then_inc(s["vout"], 1)
                    nc.scalar.copy(kN[0:w, t % 2, :], k.ps[0:w, BK, 0:256]).then_inc(s["kout"], 1)
                    if t:
                        after(act, t - 1)
                after(act, NT)

            @block.gpsimd
            def _(pool):
                for t in range(NT + 1):
                    w, c = rows[t], slice(t * P, t * P + rows[t])
                    pool.wait_ge(s["hi"], t + 1)
                    nc.gpsimd.tensor_tensor(k.oL[:, 8:12, c], heads(res[:, t % 2, :], w), k.oH[:, 8:12, c], ALU.subtract).then_inc(s["lo"], 1)

            @block.vector
            def _(dve):
                tt, ts, stt = nc.vector.tensor_tensor, nc.vector.tensor_scalar, nc.vector.scalar_tensor_tensor
                nc.vector.memset(S[:, 0], 0.0).then_inc(s["state"], 1)
                for m in range(2):
                    for u in range(2):
                        tt(qm[:, u, m], k.c('seqcols').rearrange("p (b t) -> p b t", b=NB),
                           q2[:, u, m, SEQ:].unsqueeze(1).broadcast_to([P, NB, TS]), ALU.mult).then_inc(s["qm"], 1)
                for t in range(NT + 1):
                    w = rows[t]
                    dve.wait_ge(s["att"], t + 1)
                    if t >= 2:
                        dve.wait_ge(s["o"], t - 1)
                    mask = k.c('gmask') if t < NT else k.c('gmask_s', TS)
                    tt(heads(att[0:w, t % 2, :], w), heads(k.ps[0:w, BA, :], w),
                       mask.unsqueeze(1).broadcast_to([w, GH, w]), ALU.mult).then_inc(s["attm"], 1)
                    if t < NT:
                        dve.wait_ge(s["ds"], t + 1)
                        for ch in range(2):
                            n_ch = 2 * t + ch
                            dve.wait_ge(s["state"], 1 + n_ch)
                            if n_ch >= 3:
                                dve.wait_ge(s["o"], (n_ch - 3) // 2 + 1)
                            for m in range(2):
                                ins = stt(S[:, (n_ch + 1) % 4, m, :], S[:, n_ch % 4, m, :], dec[:, m, n_ch:n_ch + 1],
                                          k.ps[:, BD[ch], m * GV:(m + 1) * GV], ALU.mult, ALU.add)
                            ins.then_inc(s["state"], 1)
                    else:
                        dve.wait_ge(s["kout"], NT + 1)
                        tt(kdm[:, :, :], kN[0:TS, NT % 2, :].unsqueeze(1).broadcast_to([TS, NB, 256]),
                           k.c('seqrows', TS).unsqueeze(2).broadcast_to([TS, NB, 256]), ALU.mult).then_inc(s["kdm"], 1)
                    if t:
                        finish(dve, t - 1)
                dve.wait_ge(s["ds"], NT + 1)
                dve.wait_ge(s["s0"], 32)
                flat_s0 = S0.rearrange("p b m v -> p (b m) v")
                dve.wait_ge(s["o"], NT + 1)
                tt(flat_s0, flat_s0, dec_s[:, :].unsqueeze(2).broadcast_to([P, 2 * NB, GV]), ALU.mult).then_inc(s["state"], 1)
                dve.wait_ge(s["state"], 1 + NC + 1)
                tt(S0.rearrange("p b m v -> p (b m v)"), S0.rearrange("p b m v -> p (b m v)"),
                   k.ps[:, 0:4, :].rearrange("p a n -> p (a n)"), ALU.add).then_inc(s["state"], 1)
                finish(dve, NT)


def merge(k):
    nc, d = k.nc, k.d
    loaded = [k.sem(f"mg_w{i}") for i in range(3)]
    split_hi, split_lo = k.sem("mg_hi"), k.sem("mg_lo")
    gate_mult, used, gate_out, branch_out = k.sem("mg_gmult"), k.sem("mg_used"), k.sem("mg_gout"), k.sem("mg_bout")
    added, sum_hi, sum_lo = k.sem("mg_added"), k.sem("mg_sumhi"), k.sem("mg_sumlo")
    NU = 3 * KD
    with nc.sbuf_tensor("mgw", [P, 3, 12, P], F32) as w32, nc.sbuf_tensor("mgwH", [P, 2, 12, P], F16) as wH, \
            nc.sbuf_tensor("mgwL", [P, 2, 12, P], F16) as wL, nc.sbuf_tensor("mgsg", [P, 2, T], F32) as sg, \
            nc.sbuf_tensor("mgacc", [P, 2, T], F32) as acc, nc.sbuf_tensor("mgtmp", [P, T], F32) as tmp, \
            nc.Block() as block:

        def units(eng, body, lookahead):
            if lookahead:
                with eng.Fori(0, NU // 6 - 1) as it:
                    for u in range(6):
                        body(it * 6 + u, u, it * 2 + u // 3)
                for u in range(6):
                    body(NU - 6 + u, u, KD - 2 + u // 3)
            else:
                with eng.Fori(0, NU // 6) as it:
                    for u in range(6):
                        body(it * 6 + u, u, it * 2 + u // 3)

        @block.sync
        def _(sp):
            def load(u, dt):
                z, slot = u % 3, u % 3
                sp.dma_start(w32[:, slot, 0:8, :], w_tile(d['w_in'], COL['merge'] + z * D + dt * P)).then_inc(loaded[slot], 16)
                sp.dma_start(w32[:, slot, 8:12, :], d['w_branch'][z][:, bass.ds(dt * P, P)].rearrange("(kt p) n -> p kt n", p=P)).then_inc(loaded[slot], 16)

            for u in range(3):
                load(u, 0)
            with sp.Fori(1, KD) as dt:
                for u in range(3):
                    sp.wait_ge(split_lo, dt * 3 + (u - 2))
                    load(u, dt)

        @block.tensor
        def _(pe):
            pe.sem_inc(used, 2)

            def unit(i, u, dt):
                s, z = u % 2, u % 3
                pe.wait_ge(split_lo, i + 1)
                pe.wait_ge(gate_out, i + 1)
                for kt in range(KD):
                    for w, x in ((wH, k.hH), (wH, k.hL), (wL, k.hH)):
                        for c in range(3):
                            ins = nc.tensor.matmul(k.ps[:, c, 0:CH], w[:, s, kt, :], x[:, kt, c * CH:(c + 1) * CH],
                                                   start=(kt == 0 and w is wH and x is k.hH), stop=(kt == KD - 1 and w is wL))
                ins.then_inc(gate_mult, 1)
                pe.wait_ge(branch_out, i + 2)
                for kt in range(4):
                    for w, x in ((wH, k.oH), (wH, k.oL), (wL, k.oH)):
                        for c in range(3):
                            ins = nc.tensor.matmul(k.ps[:, 3 + c, 0:CH], w[:, s, 8 + kt, :], x[:, 4 * z + kt, c * CH:(c + 1) * CH],
                                                   start=(kt == 0 and w is wH and x is k.oH), stop=(kt == 3 and w is wL))
                ins.then_inc(used, 1)

            units(pe, unit, False)

        @block.scalar
        def _(act):
            act.sem_inc(gate_out, 1)

            def split(i, u):
                act.wait_ge(used, i + 1)
                nc.scalar.activation(wH[:, u % 2, :, :], w32[:, u % 3, :, :], ACT.Copy, scale=WS).then_inc(split_hi, 1)

            def unit(i, u, dt):
                if not isinstance(i, int) or i + 1 < NU:
                    nxt = (u + 1) % 6
                    act.wait_ge(loaded[nxt % 3], (dt + (1 if nxt % 3 == 0 else 0)) * 32 + 32)
                    split(i + 1, nxt)
                act.wait_ge(gate_mult, i + 1)
                act.wait_ge(branch_out, i + 1)
                b = VB_MG + u % 3 * KD + dt
                nc.scalar.activation(cols3(sg[:, u % 2, :]), dense_out(k.ps, 0), ACT.Sigmoid, bias=k.vec[:, bass.ds(b, 1)],
                                     scale=1 / WS).then_inc(gate_out, 1)
                if u % 3 == 2:
                    act.wait_ge(added, dt * 2 + 3)
                    nc.scalar.copy(k.mH[:, bass.ds(dt, 1), :], acc[:, u // 3, :].unsqueeze(1)).then_inc(sum_hi, 1)

            act.wait_ge(loaded[0], 32)
            split(0, 0)
            units(act, unit, True)

        @block.vector
        def _(dve):
            dve.sem_inc(branch_out, 2)
            dve.sem_inc(added, 1)

            def split(i, u):
                dve.wait_ge(split_hi, i + 1)
                nc.vector.scalar_tensor_tensor(wL[:, u % 2, :, :], w32[:, u % 3, :, :], WS, wH[:, u % 2, :, :],
                                               ALU.mult, ALU.subtract).then_inc(split_lo, 1)

            def unit(i, u, dt):
                if not isinstance(i, int) or i + 1 < NU:
                    split(i + 1, (u + 1) % 6)
                z, a = u % 3, u // 3
                if z == 0:
                    dve.wait_ge(sum_lo, dt + 1)
                else:
                    dve.wait_ge(added, dt * 2 + z)
                dve.wait_ge(gate_out, i + 2)
                dve.wait_ge(used, i + 3)
                out = acc[:, a, :] if z == 0 else tmp[:, :]
                nc.vector.scalar_tensor_tensor(cols3(out), ps_branch, 1 / WS, cols3(sg[:, u % 2, :]), ALU.mult, ALU.mult).then_inc(branch_out, 1)
                if z:
                    dve.wait_ge(branch_out, i + 3)
                    nc.vector.tensor_tensor(acc[:, a, :], acc[:, a, :], tmp[:, :], ALU.add).then_inc(added, 1)

            ps_branch = dense_out(k.ps, 1)
            split(0, 0)
            units(dve, unit, True)

        @block.gpsimd
        def _(pool):
            pool.sem_inc(sum_lo, 2)
            with pool.Fori(0, KD // 2) as it:
                for a in range(2):
                    dt = it * 2 + a
                    pool.wait_ge(sum_hi, dt + 1)
                    o = bass.ds(dt, 1)
                    nc.gpsimd.tensor_tensor(k.mL[:, o, :], acc[:, a, :].unsqueeze(1), k.mH[:, o, :], ALU.subtract).then_inc(sum_lo, 1)


def w_out(k):
    nc, d, xT = k.nc, k.d, k.xT
    dn, x_back = Dense(k, "wo", KD), k.sem("wo_x")
    with nc.Block() as block:

        @block.sync
        def _(sp):
            for i in range(KD):
                dn.load(sp, i, i % 4, w_tile(d['w_out'], i * P), first=i < 4)
                if i == 3:
                    sp.dma_start(flat(xT[:, :, :]), k.xTd).then_inc(x_back, 16)

        @block.scalar
        def _(act):
            for i in range(KD):
                dn.split_hi(act, i, i % 4, i // 4)

        @block.vector
        def _(dve):
            dn.start_evac(dve)
            dn.split_lo(dve, 0, 0)
            dve.wait_ge(x_back, 16)
            for i in range(KD):
                if i + 1 < KD:
                    dn.split_lo(dve, i + 1, (i + 1) % 4)
                dn.wait_tile(dve, i)
                nc.vector.scalar_tensor_tensor(cols3(xT[:, i, :]), dense_out(k.ps, i % 2), 1 / WS, cols3(xT[:, i, :]),
                                               ALU.mult, ALU.add).then_inc(dn.evacuated, 1)

        @block.tensor
        def _(pe):
            dn.multiply_all(pe, k.mH, k.mL)


def mlp(k):
    nc, d, xT, aH, aL = k.nc, k.d, k.xT, k.mH, k.mL
    NG = FF // D
    dn = Dense(k, "mp", 2 * KD * NG)
    hi_made, squared, lo_made = k.sem("mp_ahi"), k.sem("mp_sq"), k.sem("mp_alo")
    with nc.sbuf_tensor("mprelu", [P, 2, T], F32) as relu, nc.sbuf_tensor("mpsq", [P, T], F32) as sq, nc.Block() as block:

        def groups(eng, body):
            with eng.Fori(0, NG - 1) as g:
                for t in range(2 * KD):
                    body(g, t, g * 16 + t)
            for t in range(2 * KD):
                body(NG - 1, t, (NG - 1) * 16 + t)

        def last(i):
            return isinstance(i, int) and i + 1 == dn.n

        @block.sync
        def _(sp):
            def load(g, t, i):
                src = w_tile(d['mlp_w1'], g * D + t * P) if t < KD else \
                    d['mlp_w2'][bass.ds(g * D, D), (t - KD) * P:(t - KD + 1) * P].rearrange("(kt p) n -> p kt n", p=P)
                dn.load(sp, i, t % 4, src, first=isinstance(i, int) and i < 4)

            for t in range(2 * KD):
                load(0, t, t)
            with sp.Fori(1, NG) as g:
                for t in range(2 * KD):
                    load(g, t, g * 16 + t)

        @block.tensor
        def _(pe):
            dn.start_pe(pe)
            with pe.Fori(0, NG) as g:
                with pe.Fori(0, KD // 2) as j:
                    for u in range(2):
                        dn.multiply(pe, g * 16 + j * 2 + u, u, k.hH, k.hL)
                dn.multiply(pe, g * 16 + KD, 0, aH, aL, ready=lambda pe, kt: pe.wait_ge(lo_made, g * 8 + (kt + 3)))
                dn.multiply(pe, g * 16 + KD + 1, 1, aH, aL)
                with pe.Fori(1, KD // 2) as j:
                    for u in range(2):
                        dn.multiply(pe, g * 16 + j * 2 + (KD + u), u, aH, aL)

        @block.scalar
        def _(act):
            def tile(g, t, i):
                if not last(i):
                    nxt = (t + 1) % 16
                    dn.split_hi(act, i + 1, nxt % 4, g * 4 + (t + 1) // 4)
                if t < KD:
                    act.wait_ge(dn.evacuated, i + 3)
                    nc.scalar.activation(aH[:, t, :], relu[:, t % 2, :], ACT.Square).then_inc(hi_made, 1)

            dn.split_hi(act, 0, 0, 0)
            groups(act, tile)

        @block.vector
        def _(dve):
            def tile(g, t, i):
                if not last(i):
                    dn.split_lo(dve, i + 1, (t + 1) % 4)
                dn.wait_tile(dve, i)
                ps = dense_out(k.ps, t % 2)
                if t < KD:
                    dve.wait_ge(lo_made, g * 8 + (t + 1))
                    ins = nc.vector.tensor_scalar(cols3(relu[:, t % 2, :]), ps, 1 / WS, 0.0, ALU.mult, ALU.max)
                else:
                    dve.wait_ge(dn.evacuated, i + 2)
                    ins = nc.vector.scalar_tensor_tensor(cols3(xT[:, t - KD, :]), ps, 1 / WS, cols3(xT[:, t - KD, :]), ALU.mult, ALU.add)
                ins.then_inc(dn.evacuated, 1)

            dn.start_evac(dve)
            dn.split_lo(dve, 0, 0)
            groups(dve, tile)

        @block.gpsimd
        def _(pool):
            pool.sem_inc(lo_made, 2)
            with pool.Fori(0, NG) as g:
                for t in range(KD):
                    n = g * 8 + t
                    pool.wait_ge(dn.evacuated, g * 16 + (t + 3))
                    pool.wait_ge(lo_made, n + 2)
                    nc.gpsimd.tensor_tensor(sq[:, :], relu[:, t % 2, :], relu[:, t % 2, :], ALU.mult).then_inc(squared, 1)
                    pool.wait_ge(squared, n + 1)
                    pool.wait_ge(hi_made, n + 1)
                    nc.gpsimd.tensor_tensor(aL[:, t, :], sq[:, :], aH[:, t, :], ALU.subtract).then_inc(lo_made, 1)


def store_y(k):
    nc, d, xT = k.nc, k.d, k.xT
    turned, out0, out1 = k.sem("y_turned"), k.sem("y_out0"), k.sem("y_out1")
    stored = [k.sem(f"y_stored{i}") for i in range(2)]
    yp = d['out_y_prompt'].rearrange("b (n p) c -> (b n) p c", p=P)
    ys = d['out_y_sample'].rearrange("b t c -> (b t) c")
    with nc.sbuf_tensor("yn", [P, 2, D], F32) as yn, nc.Block() as block:

        @block.tensor
        def _(pe):
            for t in range(NT + 1):
                w = P if t < NT else TS
                if t >= 4:
                    pe.wait_ge(out0, t - 3)
                    pe.wait_ge(out1, t - 3)
                for kt in range(KD):
                    ins = nc.tensor.transpose(k.ps[0:w, 2 * (t % 4) + kt // 4, kt % 4 * P:(kt % 4 + 1) * P], xT[:, kt, t * P:t * P + w],
                                              k.c('ident'))
                    if kt == 3:
                        ins.then_inc(turned, 1)
                ins.then_inc(turned, 1)

        def halves(eng, copy, hf, out):
            for t in range(NT + 1):
                w = P if t < NT else TS
                eng.wait_ge(turned, 2 * t + 1 + hf)
                if t >= 2:
                    eng.wait_ge(stored[t % 2], 16 * (t // 2))
                copy(yn[0:w, t % 2, hf * 512:(hf + 1) * 512], k.ps[0:w, 2 * (t % 4) + hf, :]).then_inc(out, 1)

        @block.scalar
        def _(act):
            halves(act, nc.scalar.copy, 0, out0)

        @block.vector
        def _(dve):
            halves(dve, nc.vector.tensor_copy, 1, out1)

        @block.sync
        def _(sp):
            for t in range(NT + 1):
                sp.wait_ge(out0, t + 1)
                sp.wait_ge(out1, t + 1)
                if t < NT:
                    sp.dma_start(yp[t], yn[:, t % 2, :]).then_inc(stored[t % 2], 16)
                else:
                    sp.dma_start(ys, yn[0:TS, t % 2, :]).then_inc(stored[t % 2], 16)
            sp.wait_ge(stored[0], 16 * 5)
            sp.wait_ge(stored[1], 16 * 4)


def build(nc, d):
    k = Prog(nc, d)
    with ExitStack() as ctx:
        sb = lambda n, s, t=F32: ctx.enter_context(nc.sbuf_tensor(n, s, t))
        k.cst = sb("cst", [P, CW])
        k.c = lambda n, rows=P: k.cst[0:rows, CN[n][0]:CN[n][0] + CN[n][1]]
        k.vec = sb("vec", [P, 256])
        k.hH, k.hL = sb("hH", [P, KD, T], F16), sb("hL", [P, KD, T], F16)
        k.oH, k.oL = sb("oH", [P, 12, T], F16), sb("oL", [P, 12, T], F16)
        k.w32 = sb("w32", [P, 4, KD, P])
        k.wH, k.wL = sb("wH", [P, 2, KD, P], F16), sb("wL", [P, 2, KD, P], F16)
        k.ps = ctx.enter_context(nc.psum_tensor("ps", [P, 8, 512], F32))
        k.xTd = nc.dram_tensor("xTd", (P, KD * T), F32, kind="Internal").ap()
        k.skew = nc.dram_tensor("skew", (H, P, 384), F32, kind="Internal").ap()
        load_constants(k)
        k.end_stage()
        with nc.sbuf_tensor("xT", [P, KD, T], F32) as xT:
            k.xT = xT
            load_x(k)
            k.end_stage()
            norm(k, "n1", VG1)
            k.end_stage()
        with ExitStack() as nsa:
            sb2 = lambda n, s, t=F32: nsa.enter_context(nc.sbuf_tensor(n, s, t))
            k.kcT = sb2("kcT", [P, 9, NCB])
            k.vcN = sb2("vcN", [NCB, 9, P])
            k.cmpT = sb2("cmpT", [P, 2, T])
            compress(k)
            k.end_stage()
            k.qT = sb2("qT", [P, HPG, T])
            k.kT = sb2("kT", [P, 2, T])
            k.vN = sb2("vN", [P, NT, 2, P])
            k.vS = sb2("vS", [NS, NB, 2, P])
            k.gN = sb2("gN", [P, NT + 1, 24])
            k.toep = sb2("toep", [P, H, 256])
            k.oTs = sb2("oTs", [P, 4, TS])
            project_nsa(k)
            k.end_stage()
            sample_attention(k)
            k.end_stage()
            prompt_attention(k)
            k.end_stage()
        lru(k)
        k.end_stage()
        gla(k)
        k.end_stage()
        with ExitStack() as tail:
            k.mH = tail.enter_context(nc.sbuf_tensor("mH", [P, KD, T], F16))
            k.mL = tail.enter_context(nc.sbuf_tensor("mL", [P, KD, T], F16))
            merge(k)
            k.end_stage()
            k.xT = tail.enter_context(nc.sbuf_tensor("xT2", [P, KD, T], F32))
            w_out(k)
            k.end_stage()
            norm(k, "n2", VG2)
            k.end_stage()
            mlp(k)
            k.end_stage()
            norm(k, "n3", VG3, last=True)
            k.end_stage()
            store_y(k)


OUTS = [('y_prompt', (1, SEQ, D)), ('y_sample', (NB, NS, D)),
        ('cmp_p', (1, 1, SEQ, 2, G, DH)), ('cmp_s', (1, NB, NS, 2, G, DH)),
        ('sel_p', (1, 1, SEQ, 2, G, DH)), ('sel_s', (1, NB, NS, 2, G, DH)),
        ('win_p', (1, 1, WIN, 2, G, DH)), ('win_s', (1, NB, WIN, 2, G, DH)),
        ('conv_p', (1, 1, 3, R)), ('conv_s', (1, NB, 3, R)), ('h_p', (1, 1, R)), ('h_s', (1, NB, R)),
        ('gla_p', (1, 1, GH, GK, GV)), ('gla_s', (1, NB, GH, GK, GV))]
SQUEEZED = ('w_in', 'b_in', 'w_branch', 'w_out', 'mlp_w1', 'mlp_w2', 'cache_nsa_cmp_kv', 'cache_nsa_sel_kv',
            'state_nsa_win_kv', 'state_lru_conv', 'state_lru_h', 'state_gla', 'nsa_cmp_pe', 'nsa_cmp_w1',
            'nsa_cmp_w2', 'lru_gate_w', 'gla_alpha_w')


def kernel(**inputs):
    import concourse.bacc as bacc
    from concourse.bass_utils import run_bass_kernel_spmd

    nc = bacc.Bacc("TRN2", target_bir_lowering=False, num_devices=1)
    arrays, d = {}, {}
    for name, a in list(inputs.items()) + [('consts', shape_constants())]:
        a = np.ascontiguousarray(a)
        arrays[f"in_{name}"] = a
        ap = nc.dram_tensor(f"in_{name}", a.shape, mybir.dt.from_np(a.dtype), kind="ExternalInput").ap()
        d[name] = ap[0] if name in SQUEEZED else ap
    for name, shape in OUTS:
        d['out_' + name] = nc.dram_tensor(f"out_{name}", shape, F32, kind="ExternalOutput").ap()
    build(nc, d)
    r = run_bass_kernel_spmd(nc, [arrays], core_ids=[0])
    return tuple(r.results[0][f"out_{n}"] for n, _ in OUTS)
```

```python
from contextlib import ExitStack

import numpy as np

import concourse.bass as bass
from concourse import mybir

F32 = mybir.dt.float32
F16 = mybir.dt.float16
I32 = mybir.dt.int32
ACT = mybir.ActivationFunctionType
ALU = mybir.AluOpType
AX = mybir.AxisListType.X

P = 128
D = 1024
KD = D // P
SEQ = 1024
NB = 8
NS = 4
TS = NB * NS
T = SEQ + TS
NT = SEQ // P
CH = T // 3
PAST = 1024
PAGES = PAST // P
H, G, HPG, DH = 8, 2, 4, 64
WIN = 512
CB = 32
NCB = SEQ // CB
SB = 64
NSB = PAST // SB
R = 512
GH, GK, GV = 4, 64, 128
GC = 64
FF = 4096
EPS = 1e-6
WS = 64.0
BIG = 1e30
COL = {}
_o = 0
for _n, _w in (('q', 512), ('cmp', 256), ('sel', 256), ('win', 256), ('ngate', 24), ('lx', 512),
               ('lg', 512), ('gq', 256), ('gk', 256), ('gv', 512), ('ga', 16), ('gg', 512),
               ('merge', 3072)):
    COL[_n] = _o
    _o += _w

CN = {}
_o = 0
for _n, _w in (('ident', 128), ('ones', 128), ('winmask', 128), ('gmask', 128), ('gmask_s', 32),
               ('headsum', 128), ('tokrow', 256), ('headhot', 24), ('seqcols', 256), ('seqrows', 8),
               ('winmask_s', 4), ('blk', 16), ('bucket', 384)):
    CN[_n] = (_o, _w)
    _o += _w
CW = _o


def shape_constants():
    c = np.zeros((P, CW), np.float32)

    def put(name, a):
        o, w = CN[name]
        c[:a.shape[0], o:o + w] = a

    i, j = np.arange(P)[:, None], np.arange(P)[None, :]
    put('ident', (i == j).astype(np.float32))
    put('ones', np.ones((P, P), np.float32))
    put('winmask', np.where(j <= i, -BIG, 0.0))
    put('gmask', ((i <= j) & (i // GC == j // GC)).astype(np.float32))
    s, t = np.arange(TS)[:, None], np.arange(TS)[None, :]
    put('gmask_s', ((s <= t) & (s // NS == t // NS)).astype(np.float32))
    seq, head, tok = np.arange(P) // 32, np.arange(P) % 32 // NS, np.arange(P) % NS
    grp = head // HPG
    put('headsum', ((seq[:, None] == seq) & (grp[:, None] == grp) & (tok[:, None] == tok)).astype(np.float32))
    put('tokrow', np.concatenate([(np.arange(TS)[:, None] == (4 * hf + seq) * NS + tok).astype(np.float32)
                                  for hf in range(2)], 1))
    put('headhot', (np.arange(24)[None] % 8 == head[:, None]).astype(np.float32))
    put('seqcols', np.broadcast_to((np.arange(NB)[:, None] == np.arange(TS)[None] // NS).reshape(1, -1), (P, 256)))
    put('seqrows', (np.arange(TS)[:, None] // NS == np.arange(NB)[None]).astype(np.float32))
    put('winmask_s', np.where(np.arange(NS)[None] <= tok[:, None], -BIG, 0.0))
    put('blk', np.broadcast_to(np.arange(16.0)[None], (P, 16)))
    b = np.zeros((33, 384), np.float32)
    for col in range(384):
        d = 255 - col
        if d < 0:
            b[32, col] = 1
            continue
        n = d if d < 16 else min(31, 16 + int(np.log(max(d, 1) / 16) / np.log(8) * 16 + 1e-9))
        b[n, col] += 1
        b[31, col] -= 1
    put('bucket', b)
    return c


class Prog:

    def __init__(self, nc, d):
        self.nc, self.d = nc, d
        self.stage, self.pool = [], list(nc.free_semaphores)

    def sem(self, name):
        self.stage.append(self.nc.alloc_semaphore(name, self.pool.pop(0)))
        return self.stage[-1]

    def end_stage(self):
        self.nc.clear_and_free_semaphores(self.stage)
        self.pool += [s.num for s in self.stage]
        self.stage = []


def flat(ap):
    return ap.rearrange("p a b -> p (a b)")



VB_Q, VB_CMP, VB_SEL, VB_WIN, VB_NG, VB_LX, VB_LG = 0, 4, 6, 8, 10, 11, 15
VB_GQ, VB_GK, VB_GV, VB_GA, VB_GG, VB_MG = 19, 21, 23, 27, 28, 32
VG1, VG2, VG3 = 56, 64, 72
V_LGB, V_LAM, V_CW, V_CB, V_GAB, V_GNG = 80, 88, 92, 108, 112, 114
NV = 118
V_BQ8, V_LRC = 120, 124


def load(k):
    nc, d = k.nc, k.d
    loaded, table_loaded, ident_in = k.sem("c_loaded"), k.sem("c_table"), k.sem("c_ident")
    vec_turned, bias_made, cols_ready = k.sem("c_turned"), k.sem("c_bias"), k.sem("c_cols")
    spread, rows_made, rows_out, table_set = k.sem("c_spread"), k.sem("c_rows"), k.sem("c_rowsout"), k.sem("c_tset")
    xl = [k.sem(f"x_loaded{i}") for i in range(3)]
    turned, copied, saved, summed = k.sem("x_turned"), k.sem("x_copied"), k.sem("x_saved"), k.sem("x_summed")
    xp = d['x_prompt'].rearrange("b (n p) c -> (b n) p c", p=P)
    xs = d['x_sample'].rearrange("b t c -> (b t) c")
    with nc.sbuf_tensor("vrows", [P, P], F32) as vrows, nc.sbuf_tensor("tbl", [33, H], F32) as tbl, \
            nc.sbuf_tensor("tblb", [33, H, P], F32) as tblb, nc.sbuf_tensor("brow", [P, H, 384], F32) as brow, \
            nc.sbuf_tensor("xn", [P, 3, D], F32) as xn, nc.sbuf_tensor("xsq", [P, D], F32) as xsq, nc.Block() as block:

        def half(u):
            t, hf = u // 2, u % 2
            return t, hf, P if t < NT else TS

        @block.sync
        def _(sp):
            sp.dma_start(k.cst[:, :], d['consts']).then_inc(ident_in, 16)
            for t in range(NT + 1):
                if t >= 3:
                    sp.wait_ge(turned, 2 * (t - 2))
                    sp.wait_ge(summed, t - 2)
                if t < NT:
                    sp.dma_start(xn[:, t % 3, :], xp[t]).then_inc(xl[t % 3], 16)
                else:
                    sp.dma_start(xn[0:TS, t % 3, :], xs).then_inc(xl[t % 3], 16)
            for h in range(H):
                sp.wait_ge(rows_made, h + 1)
                sp.dma_start(k.skew[h], brow[:, h, :]).then_inc(rows_out, 16)
            sp.wait_ge(copied, 2 * (NT + 1))
            sp.dma_start(k.xTd, flat(k.xT[:, :, :])).then_inc(saved, 16)
            sp.wait_ge(rows_out, 16 * H)
            sp.wait_ge(saved, 16)

        @block.gpsimd
        def _(pool):
            b = d['b_in']
            rows = [(0, b, 0, 10), (10, b, COL['ngate'], 1), (11, b, COL['lx'], 8), (19, b, COL['gq'], 8),
                    (27, b, COL['ga'], 1), (28, b, COL['gg'], 28), (56, d['norm_mix_g'], 0, 8),
                    (64, d['norm_mlp_g'], 0, 8), (72, d['norm_final_g'], 0, 8), (80, d['lru_gate_b'], 0, 8),
                    (88, d['lru_lambda'], 0, 4), (92, d['lru_conv_w'], 0, 16), (108, d['lru_conv_b'], 0, 4),
                    (112, d['gla_alpha_b'], 0, 2), (114, d['gla_norm_g'], 0, 4)]
            pool.wait_ge(table_set, 1)
            pool.dma_start(tbl[0:32, :], d['rel_bias']).then_inc(table_loaded, 16)
            for r, src, off, n in rows:
                pool.dma_start(vrows[r:r + n, :], bass.AP(tensor=src.tensor, offset=off, ap=[[P, n], [1, P]])).then_inc(loaded, 16)

        @block.tensor
        def _(pe):
            pe.wait_ge(ident_in, 16)
            for u in range(2 * (NT + 1)):
                t, hf, n = half(u)
                if hf == 0:
                    pe.wait_ge(xl[t % 3], 16 * (t // 3 + 1))
                if u >= 4:
                    pe.wait_ge(copied, u - 3)
                for j in range(4):
                    ins = nc.tensor.transpose(k.ps[:, u % 4, j * P:j * P + n], xn[0:n, t % 3, (4 * hf + j) * P:(4 * hf + j + 1) * P],
                                              k.c('ident')[0:n, 0:n])
                ins.then_inc(turned, 1)
                if 4 <= u < 4 + H:
                    h = u - 4
                    pe.wait_ge(spread, 1)
                    if h >= 2:
                        pe.wait_ge(rows_made, h - 1)
                    nc.tensor.matmul(k.ps[:, 4 + h % 2, 0:384], tblb[:, h, :], k.c('bucket', 33),
                                     start=True, stop=True).then_inc(bias_made, 1)
            pe.wait_ge(loaded, 16 * 15)
            nc.tensor.transpose(k.ps[:, 6, 0:NV], vrows[0:NV, :], k.c('ident')[0:NV, 0:NV]).then_inc(vec_turned, 1)

        @block.scalar
        def _(act):
            for u in range(2 * (NT + 1)):
                t, hf, n = half(u)
                if hf == 0:
                    act.wait_ge(xl[t % 3], 16 * (t // 3 + 1))
                    if t:
                        act.wait_ge(summed, t)
                    nc.scalar.activation(xsq[0:n, :], xn[0:n, t % 3, :], ACT.Square, accum_out=k.sums[0:n, t:t + 1]).then_inc(summed, 1)
                act.wait_ge(turned, u + 1)
                nc.scalar.copy(k.xT[:, 4 * hf:4 * hf + 4, t * P:t * P + n],
                               k.ps[:, u % 4, :].rearrange("p (j n) -> p j n", j=4)[:, :, 0:n]).then_inc(copied, 1)

        @block.vector
        def _(dve):
            nc.vector.memset(tbl[32:33, :], -BIG).then_inc(table_set, 1)
            dve.wait_ge(table_set, 1)
            dve.wait_ge(table_loaded, 16)
            nc.vector.tensor_copy(tblb[:, :, :], tbl[:, :].unsqueeze(2).broadcast_to([33, H, P])).then_inc(spread, 1)
            for h in range(H):
                dve.wait_ge(bias_made, h + 1)
                nc.vector.tensor_copy(brow[:, h, :], k.ps[:, 4 + h % 2, 0:384]).then_inc(rows_made, 1)
            dve.wait_ge(vec_turned, 1)
            nc.vector.tensor_copy(k.vec[:, 0:NV], k.ps[:, 6, 0:NV]).then_inc(cols_ready, 1)
            dve.wait_ge(cols_ready, 1)
            nc.vector.tensor_scalar(k.vec[:, V_BQ8:V_BQ8 + 4], k.vec[:, VB_Q:VB_Q + 4], DH ** -0.5, None, ALU.mult)


def dense_out(ps, b, w=CH):
    return ps[:, 3 * b:3 * b + 3, 0:w]


def cols3(ap):
    return ap.rearrange("p (c n) -> p c n", c=3)


def norm(k, name, gcol, sums_by_token=False):
    nc, xT = k.nc, k.xT
    turned, ms_ready, root_ready, step = k.sem(name + "_turned"), k.sem(name + "_ms"), k.sem(name + "_root"), k.sem(name + "_step")
    diag_ready, spread = k.sem(name + "_diag"), k.sem(name + "_spread")
    scaled, hi_ready, lo_pool, lo_dve = k.sem(name + "_scaled"), k.sem(name + "_hi"), k.sem(name + "_lop"), k.sem(name + "_lod")
    NC = NT + 1
    by_dve = (1, 3, 5)
    with nc.sbuf_tensor(name + "dg", [P, NC, P], F32) as diag, nc.sbuf_tensor(name + "tmp", [P, 4, T], F32) as tmp, \
            nc.sbuf_tensor(name + "st", [P, 4, 16], F32) as st, nc.Block() as block:
        ms, root, y, t2 = (st[:, i, 0:NC] for i in range(4))
        sums = k.sums[:, :] if sums_by_token else k.ps[:, 7, 0:NC]

        @block.tensor
        def _(pe):
            if not sums_by_token:
                for t in range(NC):
                    w = P if t < NT else TS
                    ins = nc.tensor.matmul(k.ps[0:w, 7, t:t + 1], k.ssq[:, t * P:t * P + w], k.c('ones')[:, 0:1], start=True, stop=True)
                ins.then_inc(turned, 1)
            pe.wait_ge(diag_ready, 1)
            for c in range(3):
                ins = nc.tensor.matmul(k.ps[:, c, 0:CH], k.c('ones'), diag[:, :, :].rearrange("p t n -> p (t n)")[:, c * CH:(c + 1) * CH],
                                       start=True, stop=True)
            ins.then_inc(spread, 1)

        @block.scalar
        def _(act):
            act.wait_ge(ms_ready, 3)
            nc.scalar.activation(root, ms, ACT.Sqrt).then_inc(root_ready, 1)
            for kt in range(KD):
                act.wait_ge(scaled, kt + 1)
                nc.scalar.copy(k.hH[:, kt, :], tmp[:, kt % 4, :]).then_inc(hi_ready, 1)

        @block.vector
        def _(dve):
            tt, ts = nc.vector.tensor_tensor, nc.vector.tensor_scalar
            nc.vector.memset(ms, 1.0).then_inc(ms_ready, 1)
            dve.wait_ge(ms_ready, 1)
            if not sums_by_token:
                dve.wait_ge(turned, 1)
            ts(ms[:, 0:NT], sums[:, 0:NT], 1.0 / D, EPS, ALU.mult, ALU.add).then_inc(ms_ready, 1)
            ts(ms[0:TS, NT:NC], sums[0:TS, NT:NC], 1.0 / D, EPS, ALU.mult, ALU.add).then_inc(ms_ready, 1)
            dve.wait_ge(root_ready, 1)
            made = [0]

            def settle(ins):
                made[0] += 1
                ins.then_inc(step, 1)
                dve.wait_ge(step, made[0])

            settle(nc.vector.reciprocal(y, root))
            settle(tt(t2, y, y, ALU.mult))
            settle(tt(t2, t2, ms, ALU.mult))
            settle(ts(t2, t2, -0.5, 1.5, ALU.mult, ALU.add))
            settle(tt(y, y, t2, ALU.mult))
            tt(diag[:, :, :], k.c('ident').unsqueeze(1).broadcast_to([P, NC, P]), y.unsqueeze(2).broadcast_to([P, NC, P]),
               ALU.mult).then_inc(diag_ready, 1)
            dve.wait_ge(spread, 1)

            def low(kt):
                dve.wait_ge(hi_ready, kt + 1)
                tt(k.hL[:, kt, :], tmp[:, kt % 4, :], k.hH[:, kt, :], ALU.subtract).then_inc(lo_dve, 1)

            for kt in range(KD):
                if kt >= 4:
                    old = kt - 4
                    if old in by_dve:
                        dve.wait_ge(lo_dve, by_dve.index(old) + 1)
                    else:
                        dve.wait_ge(lo_pool, old // 2 + 1)
                nc.vector.scalar_tensor_tensor(cols3(tmp[:, kt % 4, :]), cols3(xT[:, kt, :]), k.vec[:, gcol + kt:gcol + kt + 1],
                                               dense_out(k.ps, 0), ALU.mult, ALU.mult).then_inc(scaled, 1)
                if kt - 1 in by_dve:
                    low(kt - 1)

        @block.gpsimd
        def _(pool):
            for kt in range(KD):
                if kt not in by_dve:
                    pool.wait_ge(hi_ready, kt + 1)
                    nc.gpsimd.tensor_tensor(k.hL[:, kt, :], tmp[:, kt % 4, :], k.hH[:, kt, :], ALU.subtract).then_inc(lo_pool, 1)


class Dense:

    def __init__(self, k, name, n):
        self.k, self.n = k, n
        self.loaded = [k.sem(f"{name}_w{i}") for i in range(4)]
        self.hi, self.lo = k.sem(name + "_hi"), k.sem(name + "_lo")
        self.multiplied, self.evacuated = k.sem(name + "_mult"), k.sem(name + "_evac")

    def load(self, sp, i, slot, src, first=False):
        if not first:
            sp.wait_ge(self.lo, i - 3)
        sp.dma_start(self.k.w32[:, slot, :, :], src).then_inc(self.loaded[slot], 16)

    def start_pe(self, pe):
        pe.sem_inc(self.multiplied, 2)

    def start_evac(self, eng):
        eng.sem_inc(self.evacuated, 2)

    def split_hi(self, act, i, slot, turn):
        act.wait_ge(self.loaded[slot], turn * 16 + 16)
        act.wait_ge(self.multiplied, i + 1)
        self.k.nc.scalar.activation(self.k.wH[:, slot % 2, :, :], self.k.w32[:, slot, :, :], ACT.Copy,
                                    scale=WS).then_inc(self.hi, 1)

    def split_lo(self, dve, i, slot):
        dve.wait_ge(self.hi, i + 1)
        self.k.nc.vector.scalar_tensor_tensor(self.k.wL[:, slot % 2, :, :], self.k.w32[:, slot, :, :], WS,
                                              self.k.wH[:, slot % 2, :, :], ALU.mult, ALU.subtract).then_inc(self.lo, 1)

    def multiply(self, pe, i, parity, inH, inL, ready=None):
        k, nc = self.k, self.k.nc
        pe.wait_ge(self.lo, i + 1)
        pe.wait_ge(self.evacuated, i + 1)
        wH, wL = k.wH[:, parity], k.wL[:, parity]
        for kt in range(KD):
            if ready is not None:
                ready(pe, kt)
            for w, x in ((wH, inH), (wH, inL), (wL, inH)):
                for c in range(3):
                    ins = nc.tensor.matmul(k.ps[:, 3 * parity + c, 0:CH], w[:, kt, :], x[:, kt, c * CH:(c + 1) * CH],
                                           start=(kt == 0 and x is inH and w is wH), stop=(kt == KD - 1 and w is wL))
        ins.then_inc(self.multiplied, 1)

    def multiply_all(self, pe, inH, inL):
        self.start_pe(pe)
        if self.n >= 4:
            with pe.Fori(0, self.n // 2) as j:
                self.multiply(pe, j * 2, 0, inH, inL)
                self.multiply(pe, j * 2 + 1, 1, inH, inL)
        else:
            self.multiply(pe, 0, 0, inH, inL)
            self.multiply(pe, 1, 1, inH, inL)
        if self.n % 2:
            self.multiply(pe, self.n - 1, 0, inH, inL)

    def wait_tile(self, eng, i):
        eng.wait_ge(self.multiplied, i + 3)


def w_tile(w, col, k0=0):
    return w[k0:k0 + D, bass.ds(col, P)].rearrange("(kt p) n -> p kt n", p=P)


def compress(k):
    nc, d = k.nc, k.d
    cmpT = k.cmpT
    dn = Dense(k, "cp", 2)
    WAVES, WB = 2, 4 * NCB
    PR = CB // 2
    TILES = 4 * PAGES // 2
    NBLK = (NB + 1) * NCB
    table_in, w_in, page_turned = k.sem("cb_table"), k.sem("cb_win"), k.sem("cb_turned")
    page_in = [k.sem(f"cb_page{s}") for s in range(8)]
    tile_out = [k.sem("cb_outs"), k.sem("cb_outv")]
    hid_done, hid_out, prompt_copied = k.sem("cb_hid"), k.sem("cb_hidout"), k.sem("cb_prompt")
    pe_turned, pe_copied, gelu_done, out_done, copied = (k.sem("cb_peturn"), k.sem("cb_pecopy"), k.sem("cb_gelu"),
                                                         k.sem("cb_out"), k.sem("cb_copied"))
    with nc.sbuf_tensor("w1p", [P, 2, PR, DH], F32) as w1, nc.sbuf_tensor("w2p", [DH, 2, DH], F32) as w2, \
            nc.sbuf_tensor("x2", [P, 2, G, WB * PR], F32) as x2, nc.sbuf_tensor("pen", [PR, 2, 2, DH], F32) as pen, \
            nc.sbuf_tensor("ptab", [1, NB * PAGES], I32) as ptab, nc.Block() as block:
        cache = d['cache_nsa_cmp_kv'].rearrange("n (q t) z g c -> q n (t z g c)", t=2)
        spare, spare2 = (flat(o[:, :, :]).bitcast(F32) for o in (k.oH, k.oL))
        pages = spare[:, 0:4096].rearrange("p (s n) -> p s n", s=8)
        xp = spare[:, 4096:4096 + 2 * (G * SEQ // 2 + PR)].rearrange("p (z n) -> p z n", z=2)
        hraw = spare2[0:DH, 0:2 * G * NBLK].rearrange("p (z g n) -> p z g n", z=2, g=G)
        hid = spare2[0:DH, 1200:1200 + 2 * G * NBLK].rearrange("p (z g n) -> p z g n", z=2, g=G)
        pos = spare2[0:DH, 2400:2402]

        @block.sync
        def _(sp):
            sp.dma_start(ptab[:, :], d['page_table'].rearrange("(o a) b -> o (a b)", o=1)).then_inc(table_in, 16)
            for i in range(2):
                dn.load(sp, i, i, w_tile(d['w_in'], COL['cmp'] + i * P), first=True)
            sp.wait_ge(table_in, 16)
            with sp.Fori(0, NB // 2) as it:
                for s in range(8):
                    sp.wait_ge(page_turned, it * 8 + (s + 1))
                    for a in range(2):
                        page = sp.value_load(ptab[0:1, bass.ds(it * 16 + (2 * s + a), 1)], min_val=0, max_val=cache.shape[1] - 1)
                        sp.dma_start(pages[a * DH:(a + 1) * DH, s, :], cache[:, bass.ds(page, 1), :].rearrange("p o c -> p (o c)")).then_inc(page_in[s], 16)

        @block.gpsimd
        def _(pool):
            for z in range(2):
                pool.dma_start(pen[:, z, :, :], d['nsa_cmp_pe'].rearrange("(r t) z c -> z r t c", t=2)[z]).then_inc(w_in, 16)
                pool.dma_start(w1[:, z, :, :], d['nsa_cmp_w1'][z].rearrange("(r q) e -> q r e", q=P)).then_inc(w_in, 16)
                pool.dma_start(w2[:, z, :], d['nsa_cmp_w2'][z]).then_inc(w_in, 16)

        @block.tensor
        def _(pe):
            pe.sem_inc(page_turned, 8)
            pe.sem_inc(hid_done, 2)
            dn.multiply_all(pe, k.hH, k.hL)
            pe.wait_ge(dn.evacuated, 4)
            with pe.Fori(0, WAVES) as wv:
                for n in range(TILES):
                    s = n % 8
                    pe.wait_ge(page_in[s], wv * 64 + (n // 8 * 32 + 32))
                    m = n // 2
                    pe.wait_ge(tile_out[m % 2], wv * 16 + (m // 2 * 4 + 4))
                    for tz in range(4):
                        ins = nc.tensor.transpose(k.ps[:, n % 4, tz * P:(tz + 1) * P], pages[:, s, tz * P:(tz + 1) * P], k.c('ident'))
                    ins.then_inc(page_turned, 1)
                pe.wait_ge(w_in, 96)
                pe.wait_ge(tile_out[0], wv * 16 + 20)
                pe.wait_ge(tile_out[1], wv * 16 + 20)
                pe.wait_ge(hid_out, wv * 2 + 2)
                for z in range(2):
                    for r in range(PR):
                        ins = nc.tensor.matmul(k.ps[0:DH, 4 + z, 0:G * WB], w1[:, z, r, :], x2[:, z, :, r::PR],
                                               start=(r == 0), stop=(r == PR - 1))
                    ins.then_inc(hid_done, 1)
            for z in range(2):
                ins = nc.tensor.transpose(k.ps[:, 6, z * PR:(z + 1) * PR], pen[:, z, :, :].rearrange("r t c -> r (t c)"), k.c('ident')[0:PR, 0:PR])
            ins.then_inc(pe_turned, 1)
            pe.wait_ge(pe_copied, 1)
            pe.wait_ge(prompt_copied, 4)
            pe.wait_ge(hid_out, 2 * WAVES + 2)
            for z in range(2):
                for r in range(PR):
                    ins = nc.tensor.matmul(k.ps[0:DH, 4 + z, 0:G * NCB + 1], w1[:, z, r, :], xp[:, z, r::PR],
                                           start=(r == 0), stop=(r == PR - 1))
                ins.then_inc(hid_done, 1)
            pe.wait_ge(gelu_done, 2)
            for g in range(G):
                ins = nc.tensor.matmul(k.ps[g * DH:(g + 1) * DH, 0, 0:NBLK], w2[:, 0, :], hid[:, 0, g, :], start=True, stop=True)
            ins.then_inc(out_done, 1)
            for s in range(NB + 1):
                for g in range(G):
                    o = s % 4 * P + g * DH
                    ins = nc.tensor.matmul(k.ps[0:NCB, 1 + s // 4, o:o + DH], hid[:, 1, g, s * NCB:(s + 1) * NCB], w2[:, 1, :],
                                           start=True, stop=True)
            ins.then_inc(out_done, 1)

        def tiles_out(eng, copy, wv, parity):
            eng.wait_ge(hid_done, wv * 2 + 2)
            for m in range(parity, TILES // 2, 2):
                eng.wait_ge(page_turned, wv * TILES + (2 * m + 2 + 8))
                for g in range(G):
                    for t in range(2):
                        src = k.ps[g * DH:(g + 1) * DH, 2 * parity:2 * parity + 2, t * 2 * P:(t + 1) * 2 * P]
                        copy(x2[t * DH:(t + 1) * DH, :, g, m * 2 * P:(m + 1) * 2 * P].rearrange("p z (b n) -> p z b n", b=2),
                             src.rearrange("p b (z n) -> p z b n", z=2)).then_inc(tile_out[parity], 1)

        @block.scalar
        def _(act):
            dn.start_evac(act)
            act.sem_inc(hid_out, 2)
            act.sem_inc(tile_out[0], 4)
            for i in range(2):
                dn.split_hi(act, i, i, 0)
            for i in range(2):
                dn.wait_tile(act, i)
                nc.scalar.activation(cols3(cmpT[:, i, :]), dense_out(k.ps, i), ACT.Identity,
                                     bias=k.vec[:, VB_CMP + i:VB_CMP + i + 1], scale=1 / WS).then_inc(dn.evacuated, 1)
            with act.Fori(0, WAVES) as wv:
                tiles_out(act, nc.scalar.copy, wv, 0)
                for z in range(2):
                    act.wait_ge(hid_done, wv * 2 + (z + 3))
                    nc.scalar.copy(hraw[:, z, :, bass.ds(wv * WB, WB)], k.ps[0:DH, 4 + z, 0:G * WB].rearrange("p (g n) -> p g n", g=G)).then_inc(hid_out, 1)
            for z in range(2):
                act.wait_ge(hid_done, 2 + 2 * WAVES + z + 1)
                nc.scalar.copy(hraw[:, z, :, NB * NCB:], k.ps[0:DH, 4 + z, 0:G * NCB].rearrange("p (g n) -> p g n", g=G)).then_inc(copied, 1)
                nc.scalar.copy(pos[:, z:z + 1], k.ps[0:DH, 4 + z, G * NCB:G * NCB + 1]).then_inc(copied, 1)
            act.wait_ge(copied, 4)
            act.wait_ge(hid_out, 2 + 2 * WAVES)
            for z in range(2):
                nc.scalar.activation(hid[:, z], hraw[:, z], ACT.Gelu_apprx_tanh, bias=pos[:, z:z + 1]).then_inc(gelu_done, 1)
            act.wait_ge(out_done, 1)
            nc.scalar.copy(k.kcT[:, :, :].rearrange("p s n -> p (s n)"), k.ps[:, 0, 0:NBLK])

        @block.vector
        def _(dve):
            dve.sem_inc(tile_out[1], 4)
            for i in range(2):
                dn.split_lo(dve, i, i)
            dve.wait_ge(dn.evacuated, 4)
            for g in range(G):
                for t in range(2):
                    nc.vector.tensor_copy(xp[t * DH:(t + 1) * DH, :, g * SEQ // 2:(g + 1) * SEQ // 2],
                                          cmpT[g * DH:(g + 1) * DH, :, t:SEQ:2]).then_inc(prompt_copied, 1)
            with dve.Fori(0, WAVES) as wv:
                tiles_out(dve, nc.vector.tensor_copy, wv, 1)
            dve.wait_ge(pe_turned, 1)
            nc.vector.tensor_copy(xp[:, :, SEQ:], k.ps[:, 6, 0:2 * PR].rearrange("p (z l) -> p z l", z=2)).then_inc(pe_copied, 1)
            dve.wait_ge(out_done, 2)
            nc.vector.tensor_copy(k.vcN[:, 0:8, :], k.ps[0:NCB, 1:3, :].rearrange("p b (s n) -> p (b s) n", n=P))
            nc.vector.tensor_copy(k.vcN[:, 8, :], k.ps[0:NCB, 3, 0:P])


def project_nsa(k):
    nc, d = k.nc, k.d
    cols = [COL['q'] + m * P for m in range(4)] + [COL['sel'], COL['sel'] + P, COL['win'], COL['win'] + P, COL['ngate']]
    n = len(cols)
    dn = Dense(k, "pn", n)
    with nc.sbuf_tensor("vT", [P, 2, T], F32) as vT, nc.sbuf_tensor("gT", [24, T], F32) as gT, \
            nc.sbuf_tensor("nat", [P, 3, 768], F32) as nat:
        with nc.Block() as block:

            @block.sync
            def _(sp):
                for i in range(n):
                    dn.load(sp, i, i % 4, w_tile(d['w_in'], cols[i]), first=i < 4)

            @block.scalar
            def _(act):
                dn.start_evac(act)
                dn.split_hi(act, 0, 0, 0)
                for i in range(n):
                    if i + 1 < n:
                        dn.split_hi(act, i + 1, (i + 1) % 4, (i + 1) // 4)
                    dn.wait_tile(act, i)
                    ps = dense_out(k.ps, i % 2)
                    if i < 4:
                        for u in range(2):
                            g, hh = i // 2, (2 * i + u) % HPG
                            r = slice(u * DH, (u + 1) * DH)
                            ins = nc.scalar.activation(cols3(k.qT[g * DH:(g + 1) * DH, hh, :]), ps[r], ACT.Identity,
                                                       bias=k.vec[r, V_BQ8 + i:V_BQ8 + i + 1], scale=DH ** -0.5 / WS)
                    elif i < 8:
                        out = (k.kT[:, 0, :], vT[:, 0, :], k.kT[:, 1, :], vT[:, 1, :])[i - 4]
                        b = VB_SEL + i - 4
                        ins = nc.scalar.activation(cols3(out), ps, ACT.Identity, bias=k.vec[:, b:b + 1], scale=1 / WS)
                    else:
                        ins = nc.scalar.activation(cols3(gT[:, :]), ps[0:24], ACT.Sigmoid, bias=k.vec[0:24, VB_NG:VB_NG + 1],
                                                   scale=1 / WS)
                    ins.then_inc(dn.evacuated, 1)

            @block.vector
            def _(dve):
                for i in range(n):
                    dn.split_lo(dve, i, i % 4)

            @block.tensor
            def _(pe):
                dn.multiply_all(pe, k.hH, k.hL)

        turned, first_out, second_out, vals_kept = k.sem("na_turned"), k.sem("na_out1"), k.sem("na_out2"), k.sem("na_kept")
        stored = [k.sem(f"na_stored{i}") for i in range(3)]
        other, new_turned = k.sem("na_other"), k.sem("na_new")
        with nc.Block() as block:
            rows = [P] * NT + [TS]
            outs = [(d['out_cmp_p'], d['out_cmp_s']), (d['out_sel_p'], d['out_sel_s']), (d['out_win_p'], d['out_win_s'])]

            def stores(t):
                if t == NT:
                    return [(outs[j][1][0], j) for j in range(3)]
                return [(outs[j][0][0, 0], j) for j in range(3) if j < 2 or t >= (SEQ - WIN) // P]

            @block.tensor
            def _(pe):
                for t in range(NT + 1):
                    m = rows[t]
                    if t >= 4:
                        pe.wait_ge(first_out, t - 3)
                        pe.wait_ge(second_out, t - 3)
                    for j, src in enumerate((k.cmpT[:, 0], k.cmpT[:, 1], k.kT[:, 0], vT[:, 0], k.kT[:, 1], vT[:, 1])):
                        nc.tensor.transpose(k.ps[0:m, 2 * (t % 4) + j // 4, (j % 4) * P:(j % 4 + 1) * P],
                                            src[:, t * P:t * P + m], k.c('ident'))
                    nc.tensor.transpose(k.ps[0:m, 2 * (t % 4) + 1, 256:280], gT[:, t * P:t * P + m],
                                        k.c('ident')[0:24, 0:24]).then_inc(turned, 1)
                pe.wait_ge(first_out, 8)
                pe.wait_ge(second_out, 8)
                for b in range(NB):
                    for z in range(2):
                        c = (2 * b + z) * P
                        ins = nc.tensor.transpose(k.ps[0:NS, 2 + c // 512, c % 512:c % 512 + P],
                                                  vT[:, z, SEQ + b * NS:SEQ + (b + 1) * NS], k.c('ident'))
                ins.then_inc(new_turned, 1)

            @block.scalar
            def _(act):
                for t in range(NT + 1):
                    act.wait_ge(turned, t + 1)
                    if t >= 3:
                        act.wait_ge(stored[t % 3], 16 * sum(len(stores(u)) for u in range(t % 3, t, 3)))
                        act.wait_ge(vals_kept, t - 2)
                    nc.scalar.copy(nat[0:rows[t], t % 3, 0:512], k.ps[0:rows[t], 2 * (t % 4), :]).then_inc(first_out, 1)

            @block.vector
            def _(dve):
                for t in range(NT + 1):
                    dve.wait_ge(turned, t + 1)
                    if t >= 3:
                        dve.wait_ge(stored[t % 3], 16 * sum(len(stores(u)) for u in range(t % 3, t, 3)))
                        dve.wait_ge(vals_kept, t - 2)
                    m, b = rows[t], 2 * (t % 4) + 1
                    nc.vector.tensor_copy(nat[0:m, t % 3, 512:768], k.ps[0:m, b, 0:256])
                    nc.vector.tensor_copy(k.gN[0:m, t, :], k.ps[0:m, b, 256:280]).then_inc(second_out, 1)
                dve.wait_ge(new_turned, 1)
                nc.vector.tensor_copy(k.vS[:, :, :, :].rearrange("t b z n -> t (b z n)"),
                                      k.ps[0:NS, 2:6, :].rearrange("t b n -> t (b n)"))

            @block.sync
            def _(sp):
                sp.dma_start(k.toep[:, :, :], bass.AP(tensor=k.skew.tensor, offset=P - 1,
                                                      ap=[[383, P], [384 * P, H], [1, 256]])).then_inc(other, 16)
                win_state = d['state_nsa_win_kv'].rearrange("b s z g c -> b (s z g c)")
                win_out = d['out_win_s'][0].rearrange("b s z g c -> b (s z g c)")
                sp.dma_start(win_out[:, 0:(WIN - NS) * 256], win_state[:, NS * 256:]).then_inc(other, 16)
                for t in range(NT + 1):
                    sp.wait_ge(first_out, t + 1)
                    sp.wait_ge(second_out, t + 1)
                    for out, j in stores(t):
                        src = nat[0:rows[t], t % 3, j * 256:(j + 1) * 256]
                        if t < NT:
                            r = t * P - (SEQ - WIN if j == 2 else 0)
                            sp.dma_start(out.rearrange("s z g c -> s (z g c)")[r:r + P], src).then_inc(stored[t % 3], 16)
                        elif j < 2:
                            sp.dma_start(out.rearrange("b s z g c -> (b s) (z g c)"), src).then_inc(stored[t % 3], 16)
                        else:
                            new = out.rearrange("b s z g c -> b s (z g c)")
                            for b in range(NB):
                                sp.dma_start(new[b, WIN - NS:WIN], nat[b * NS:(b + 1) * NS, t % 3, 512:768]).then_inc(other, 16)
                for r in range(3):
                    n_st = sum(len(stores(u)) - (u == NT) for u in range(r, NT + 1, 3))
                    sp.wait_ge(stored[r], 16 * n_st)
                sp.wait_ge(other, 16 * (2 + NB))

            @block.gpsimd
            def _(pool):
                for t in range(NT):
                    pool.wait_ge(first_out, t + 1)
                    pool.wait_ge(second_out, t + 1)
                    nc.gpsimd.tensor_copy(k.vN[:, t, 0, :], nat[:, t % 3, 384:512])
                    nc.gpsimd.tensor_copy(k.vN[:, t, 1, :], nat[:, t % 3, 640:768]).then_inc(vals_kept, 1)


def sample_attention(k):
    nc, d = k.nc, k.d
    HS = 4
    WT = WIN // P
    NK = PAST + NS
    names = ("q", "bias", "kturn", "kcopy", "score", "gate", "csoft", "imp", "drop", "sprep", "smax", "wprep", "wmax",
             "exp", "pturn", "pcopy", "o", "fac", "comb", "oturn", "ocopy", "tab", "page", "first", "wcopy", "cexp",
             "cprep", "cturn", "ccopy", "khigh")
    s = {n: k.sem("sa_" + n) for n in names}
    key_in = [k.sem(f"sa_key{i}") for i in range(2)]
    val_in = [k.sem(f"sa_val{i}") for i in range(2)]
    val_sync = [k.sem(f"sa_vals{i}") for i in range(2)]
    with ExitStack() as es:
        sb = lambda n, sh, t=F32: es.enter_context(nc.sbuf_tensor("sa" + n, sh, t))
        spare = flat(k.oH[:, :, :]).bitcast(F32)
        spare2 = flat(k.oL[:, :, :]).bitcast(F32)
        keys = spare[:, 0:2 * 12 * P].rearrange("p (u j n) -> p u j n", u=2, j=12)
        kT = spare[:, 3072:3072 + 3072].rearrange("p (u n) -> p u n", u=2)
        vals = sb("vals", [P, HS, 12, P])
        Ss = spare2[:, 0:NK]
        Ws = spare2[:, NK:NK + WIN + NS]
        Cs = spare2[:, 1600:1632]
        PT = spare2[:, 1632:1632 + 14 * P].rearrange("p (j n) -> p j n", j=14)
        comb = spare2[:, 3500:3628]
        qbd, bias = sb("qbd", [P, NB, 32]), sb("bias", [P, 132])
        st = sb("st", [P, 64])
        imp, drop = sb("imp", [P, 16]), sb("drop", [P, 32])
        ctab, xs = sb("ctab", [P, 24]), sb("xs", [P, 120])
        PTc = sb("PTc", [NCB, P])
        ptab = sb("ptab", [1, NB * PAGES], I32)
        cache = d['cache_nsa_sel_kv'].rearrange("n p z g c -> p n z (g c)")
        state = d['state_nsa_win_kv'].rearrange("b (j p) z g c -> b z p j (g c)", p=P)
        block = es.enter_context(nc.Block())
        NEG_C, NEG_S, NEG_W, SUM_C, SUM_S, SUM_W, F_C, F_S, F_W, G3, TMP, CSUM = 0, 1, 2, 3, 4, 5, 6, 7, 8, 9, 12, 14
        col = lambda c, w=1: st[:, c:c + w]

        KA, VA = 5, 2

        def key_pages(eng, b, a0, a1):
            with eng.Fori(a0, a1) as j:
                page = eng.value_load(ptab[0:1, bass.ds(j + b * PAGES, 1)], min_val=0, max_val=cache.shape[1] - 1)
                eng.dma_start(keys[:, b % 2, bass.ds(j, 1), :].rearrange("p o n -> p (o n)"),
                              cache[:, bass.ds(page, 1), 0, :].rearrange("p o n -> p (o n)")).then_inc(key_in[b % 2], 16)

        def val_pages(eng, b, a0, a1, arrived):
            with eng.Fori(a0, a1) as j:
                page = eng.value_load(ptab[0:1, bass.ds(j + b * PAGES, 1)], min_val=0, max_val=cache.shape[1] - 1)
                eng.dma_start(vals[:, b % HS, bass.ds(j, 1), :].rearrange("p o n -> p (o n)"),
                              cache[:, bass.ds(page, 1), 1, :].rearrange("p o n -> p (o n)")).then_inc(arrived[b // HS], 16)

        @block.sync
        def _(sp):
            sp.dma_start(ptab[:, :], d['page_table'].rearrange("(o a) b -> o (a b)", o=1)).then_inc(s["tab"], 16)
            for u in range(HS):
                sp.dma_start(bias[32 * u:32 * u + 32, :], bass.AP(tensor=k.skew.tensor, offset=P - 1,
                                                                   ap=[[384 * P, H], [383, NS], [1, 132]])).then_inc(s["bias"], 16)
            sp.wait_ge(s["tab"], 16)
            for b in range(NB):
                if b >= 2:
                    sp.wait_ge(s["kturn"], 3 * (b - 1))
                key_pages(sp, b, 0, KA)
                if b < HS:
                    val_pages(sp, b, 0, VA, val_sync)
            sp.wait_ge(s["o"], 1)
            for b in range(HS, NB):
                val_pages(sp, b, 0, VA, val_sync)

        @block.gpsimd
        def _(pool):
            pool.wait_ge(s["tab"], 16)
            for b in range(NB):
                if b >= HS:
                    pool.wait_ge(s["o"], 1)
                val_pages(pool, b, VA, PAGES, val_in)
                pool.dma_start(vals[:, b % HS, PAGES:12, :], state[b, 1]).then_inc(val_in[b // HS], 16)

        BT, BS, BW, BX, BO = 0, 2, 4, 5, 7
        XC, XSN, XWN, XI, XG = 0, 32, 36, 64, 96

        @block.tensor
        def _(pe):
            pe.wait_ge(s["q"], 2)
            for hf in range(2):
                for u in range(HS):
                    b = hf * HS + u
                    pe.wait_ge(key_in[b % 2], 16 * 9 * (b // 2 + 1))
                    for q in range(3):
                        n = 3 * b + q
                        if n >= 2:
                            pe.wait_ge(s["kcopy"], n - 1)
                        for j in range(4):
                            ins = nc.tensor.transpose(k.ps[:, BT + n % 2, j * P:(j + 1) * P], keys[:, b % 2, 4 * q + j, :],
                                                      k.c('ident'))
                        ins.then_inc(s["kturn"], 1)
                    if hf and u == 0:
                        pe.wait_ge(s["sprep"], 2 * hf)
                        pe.wait_ge(s["wprep"], 1)
                        pe.wait_ge(s["cprep"], 2 * hf)
                        pe.wait_ge(s["fac"], 1)
                    r = slice(32 * u, 32 * u + 32)
                    nc.tensor.matmul(k.ps[r, BX, XC:XC + NCB], qbd[:, b, :], k.kcT[:, b, :], start=True, stop=True)
                    new = slice(SEQ + b * NS, SEQ + (b + 1) * NS)
                    nc.tensor.matmul(k.ps[r, BX, XSN:XSN + NS], qbd[:, b, :], k.kT[:, 0, new], start=True, stop=True)
                    nc.tensor.matmul(k.ps[r, BX, XWN:XWN + NS], qbd[:, b, :], k.kT[:, 1, new], start=True, stop=True)
                    for q in range(3):
                        pe.wait_ge(s["kcopy"], 3 * b + q + 1)
                        ins = nc.tensor.matmul(k.ps[r, BS + q if q < 2 else BW, :], qbd[:, b, :], kT[:, b % 2, q * 512:(q + 1) * 512],
                                               start=True, stop=True)
                    ins.then_inc(s["score"], 1)
                nc.tensor.matmul(k.ps[:, BX, XG:XG + 24], k.c('tokrow', TS)[:, hf * P:(hf + 1) * P], k.gN[0:TS, NT, :],
                                 start=True, stop=True).then_inc(s["gate"], 1)
                pe.wait_ge(s["csoft"], hf + 1)
                nc.tensor.matmul(k.ps[:, BX, XI:XI + NCB], k.c('headsum'), Cs, start=True, stop=True).then_inc(s["imp"], 1)
                nc.tensor.transpose(k.ps[0:NCB, 6, 0:P], Cs, k.c('ident')).then_inc(s["cturn"], 1)
                pe.wait_ge(s["ccopy"], hf + 1)
                if hf:
                    pe.wait_ge(s["comb"], 1)
                for u in range(HS):
                    b = hf * HS + u
                    nc.tensor.matmul(k.ps[32 * u:32 * u + 32, BO, 0:P], PTc[:, 32 * u:32 * u + 32], k.vcN[:, b, :],
                                     start=True, stop=True)
                pe.wait_ge(s["kcopy"], 3 * (hf * HS + HS))
                for q in range(4):
                    pe.wait_ge(s["exp"], 3 * hf + (2 if q < 2 else 3))
                    n = 4 * hf + q
                    if n >= 2:
                        pe.wait_ge(s["pcopy"], n - 1)
                    if q < 3:
                        for j in range(4):
                            src = Ss[:, (4 * q + j) * P:(4 * q + j + 1) * P] if q < 2 else Ws[:, j * P:(j + 1) * P]
                            ins = nc.tensor.transpose(k.ps[:, BT + q % 2, j * P:(j + 1) * P], src, k.c('ident'))
                    else:
                        nc.tensor.transpose(k.ps[0:NS, BT + 1, 0:P], Ss[:, PAST:NK], k.c('ident'))
                        ins = nc.tensor.transpose(k.ps[0:NS, BT + 1, P:2 * P], Ws[:, WIN:WIN + NS], k.c('ident'))
                    ins.then_inc(s["pturn"], 1)
                pe.wait_ge(val_in[hf], 16 * (9 - VA) * HS)
                pe.wait_ge(val_sync[hf], 16 * VA * HS)
                pe.wait_ge(s["pcopy"], 4 * hf + 4)
                for u in range(HS):
                    b, r = hf * HS + u, slice(32 * u, 32 * u + 32)
                    for z, tiles in ((0, range(0, 8)), (1, range(8, 12))):
                        out = k.ps[r, BO, (z + 1) * P:(z + 2) * P]
                        for j in tiles:
                            nc.tensor.matmul(out, PT[:, j, r], vals[:, u, j, :], start=(j == tiles[0]), stop=False)
                        ins = nc.tensor.matmul(out, PT[0:NS, 12 + z, r], k.vS[:, b, z, :], start=False, stop=True)
                ins.then_inc(s["o"], 1)
                pe.wait_ge(s["comb"], hf + 1)
                nc.tensor.transpose(k.ps[:, 6, P:2 * P], comb, k.c('ident')).then_inc(s["oturn"], 1)

        @block.scalar
        def _(act):
            def other_keys(b):
                act.dma_start(keys[:, b % 2, PAGES:12, :], state[b, 0]).then_inc(key_in[b % 2], 16)
                key_pages(act, b, KA, PAGES)

            act.wait_ge(s["tab"], 16)
            other_keys(0)
            other_keys(1)
            for hf in range(2):
                for b in range(hf * HS, hf * HS + HS):
                    for q in range(3):
                        act.wait_ge(s["kturn"], 3 * b + q + 1)
                        if b >= 2:
                            act.wait_ge(s["score"], b - 1)
                        nc.scalar.copy(kT[:, b % 2, q * 512:(q + 1) * 512], k.ps[:, BT + (3 * b + q) % 2, :]).then_inc(s["kcopy"], 1)
                    if b + 2 < NB:
                        other_keys(b + 2)
                act.wait_ge(s["cprep"], 2 * hf + 2)
                nc.scalar.activation(Cs, xs[:, XC:XC + NCB], ACT.Exp, bias=col(NEG_C), accum_out=col(SUM_C)).then_inc(s["exp"], 1)
                act.wait_ge(s["smax"], hf + 1)
                nc.scalar.activation(Ss, Ss, ACT.Exp, bias=col(NEG_S), accum_out=col(SUM_S)).then_inc(s["exp"], 1)
                act.wait_ge(s["wmax"], hf + 1)
                nc.scalar.activation(Ws, Ws, ACT.Exp, bias=col(NEG_W), accum_out=col(SUM_W)).then_inc(s["exp"], 1)
                for q in range(4):
                    act.wait_ge(s["pturn"], 4 * hf + q + 1)
                    if q < 3:
                        ins = nc.scalar.copy(PT[:, 4 * q:4 * q + 4, :].rearrange("p j n -> p (j n)"), k.ps[:, BT + q % 2, :])
                    else:
                        ins = nc.scalar.copy(PT[0:NS, 12:14, :].rearrange("p j n -> p (j n)"), k.ps[0:NS, BT + 1, 0:2 * P])
                    ins.then_inc(s["pcopy"], 1)

        @block.vector
        def _(dve):
            tt, ts, stt, red = nc.vector.tensor_tensor, nc.vector.tensor_scalar, nc.vector.scalar_tensor_tensor, nc.vector.tensor_reduce
            nc.vector.memset(qbd[:, :, :], 0.0).then_inc(s["first"], 1)
            dve.wait_ge(s["first"], 1)
            for g in range(G):
                r = slice(g * DH, (g + 1) * DH)
                for hh in range(HPG):
                    ins = nc.vector.tensor_copy(qbd[r, :, (g * HPG + hh) * NS:(g * HPG + hh + 1) * NS],
                                                k.qT[r, hh, SEQ:].rearrange("p (b t) -> p b t", b=NB))
                ins.then_inc(s["q"], 1)
            half = [slice(g * DH, (g + 1) * DH) for g in range(G)]
            for g in range(G):
                for u in range(G):
                    nc.vector.tensor_copy(k.kH[half[u], g], k.kT[half[g], :, 0:SEQ]).then_inc(s["khigh"], 1)
                    nc.vector.tensor_copy(k.kcH[half[u], g, :], k.kcT[half[g], 8, :]).then_inc(s["khigh"], 1)
            dve.wait_ge(s["khigh"], 8)
            for g in range(G):
                for u in range(G):
                    tt(k.kL[half[u], g], k.kT[half[g], :, 0:SEQ], k.kH[half[g], g], ALU.subtract)
                    tt(k.kcL[half[u], g, :], k.kcT[half[g], 8, :], k.kcH[half[g], g, :], ALU.subtract)
            dve.wait_ge(s["bias"], 64)
            step = [0]

            def done(ins):
                step[0] += 1
                ins.then_inc(s["page"], 1)
                dve.wait_ge(s["page"], step[0])

            for hf in range(2):
                dve.wait_ge(s["score"], HS * (hf + 1))
                dve.wait_ge(s["gate"], hf + 1)
                nc.vector.tensor_copy(xs[:, XG:XG + 24], k.ps[:, BX, XG:XG + 24])
                done(nc.vector.tensor_copy(xs[:, 0:40], k.ps[:, BX, 0:40]))
                c4 = xs[:, XC + NCB - 4:XC + NCB]
                tt(c4, c4, bias[:, CB - 1:P:CB], ALU.add).then_inc(s["cprep"], 1)
                dve.wait_ge(s["cprep"], 2 * hf + 1)
                red(col(NEG_C), xs[:, XC:XC + NCB], AX, ALU.max, negate=True).then_inc(s["cprep"], 1)
                if hf:
                    dve.wait_ge(s["pcopy"], 4)
                done(nc.vector.tensor_copy(Ws[:, 0:WIN], k.ps[:, BW, :]))
                done(tt(Ws[:, 0:NS], Ws[:, 0:NS], k.c('winmask_s'), ALU.add))
                done(tt(Ws[:, WIN - P:WIN], Ws[:, WIN - P:WIN], bias[:, 0:P], ALU.add))
                done(tt(Ws[:, WIN:WIN + NS], xs[:, XWN:XWN + NS], bias[:, P:P + NS], ALU.add))
                ins = red(col(NEG_W), Ws, AX, ALU.max, negate=True)
                ins.then_inc(s["wmax"], 1)
                dve.sem_inc(s["wprep"], 1)
                dve.wait_ge(s["exp"], 3 * hf + 1)
                done(nc.vector.reciprocal(col(CSUM), col(SUM_C)))
                ts(Cs, Cs, col(CSUM), None, ALU.mult).then_inc(s["csoft"], 1)
                dve.wait_ge(s["imp"], hf + 1)
                done(red(imp[:, :], k.ps[:, BX, XI:XI + NCB].rearrange("p (b c) -> p b c", c=2), AX, ALU.add))
                done(red(col(TMP), imp[:, 1:15], AX, ALU.min))
                done(stt(drop[:, 1:15], imp[:, 1:15], col(TMP), k.c('blk')[:, 1:15], ALU.is_equal, ALU.mult))
                done(red(col(TMP), drop[:, 1:15], AX, ALU.max))
                done(ts(drop[:, 16:32], k.c('blk'), col(TMP), -BIG, ALU.is_equal, ALU.mult))
                done(tt(Ss[:, 0:PAST].rearrange("p (b n) -> p b n", n=SB), k.ps[:, BS:BS + 2, :].rearrange("p u (b n) -> p (u b) n", n=SB),
                        drop[:, 16:32].unsqueeze(2).broadcast_to([P, 16, SB]), ALU.add))
                done(tt(Ss[:, PAST - P:PAST], Ss[:, PAST - P:PAST], bias[:, 0:P], ALU.add))
                done(tt(Ss[:, PAST:NK], xs[:, XSN:XSN + NS], bias[:, P:P + NS], ALU.add))
                dve.sem_inc(s["sprep"], 2)
                red(col(NEG_S), Ss, AX, ALU.max, negate=True).then_inc(s["smax"], 1)
                dve.wait_ge(s["cturn"], hf + 1)
                nc.vector.tensor_copy(PTc[:, :], k.ps[0:NCB, 6, 0:P]).then_inc(s["ccopy"], 1)
                done(tt(ctab[:, :], xs[:, XG:XG + 24], k.c('headhot'), ALU.mult))
                done(red(col(G3, 3), ctab[:, :].rearrange("p (z h) -> p z h", z=3), AX, ALU.add))
                dve.wait_ge(s["exp"], 3 * hf + 3)
                done(nc.vector.reciprocal(col(TMP, 2), col(SUM_S, 2)))
                tt(col(F_S, 2), col(G3 + 1, 2), col(TMP, 2), ALU.mult).then_inc(s["fac"], 1)
                dve.wait_ge(s["fac"], hf + 1)
                dve.wait_ge(s["o"], hf + 1)
                done(ts(comb, k.ps[:, BO, 0:P], col(G3), None, ALU.mult))
                done(stt(comb, k.ps[:, BO, P:2 * P], col(F_S), comb, ALU.mult, ALU.add))
                stt(comb, k.ps[:, BO, 2 * P:3 * P], col(F_W), comb, ALU.mult, ALU.add).then_inc(s["comb"], 1)
                dve.wait_ge(s["oturn"], hf + 1)
                for h in range(H):
                    g, m, odd = h // HPG, h // 2, h % 2
                    nc.vector.tensor_copy(k.oTs[odd * DH:(odd + 1) * DH, m, hf * 16:hf * 16 + 16].rearrange("p (u t) -> p u t", u=HS),
                                          k.ps[g * DH:(g + 1) * DH, 6, P:2 * P].rearrange("p (u r) -> p u r", u=HS)[:, :, h * NS:(h + 1) * NS])


def prompt_attention(k):
    nc, d = k.nc, k.d
    C, S, W = range(3)
    jobs = []
    for i in range(NT):
        for g in range(G):
            for kind in (C, S, W):
                first = {C: 0, S: 0, W: max(0, i - WIN // P)}[kind]
                jobs.append((i, g, kind, [0] if kind == C else list(range(first, i + 1))))
    NJ = len(jobs)
    groups, count = [], [0, 0]
    for i, g, kind, tiles in jobs:
        mine = []
        for a in range(0, len(tiles), 4):
            bank = (count[0] + count[1]) % 2
            mine.append((bank, count[bank], count[0] + count[1], tiles[a:a + 4], a))
            count[bank] += 1
        groups.append(mine)
    NG = count[0] + count[1]
    STEPS = 2 * NJ + NJ // 3
    spare = flat(k.oL[:, :, :]).bitcast(F32)
    prob = spare[:, 0:3 * SEQ].rearrange("p (u n) -> p u n", u=3)
    probT = spare[:, 3 * SEQ:6 * SEQ].rearrange("p (u t n) -> p u t n", u=3, t=NT)
    kH, kL, kcH, kcL = k.kH, k.kL, k.kcH, k.kcL
    qP = flat(k.oH[:, :, :])[:, 0:H * SEQ].rearrange("p (h t) -> p h t", h=H)
    with nc.sbuf_tensor("pastat", [P, 3, 12], F32) as stat, \
            nc.sbuf_tensor("oacc", [P, NT, R], F32) as oacc:
        scored, maxed, exped = k.sem("pa_scored"), k.sem("pa_maxed"), k.sem("pa_exped")
        turned, out_done, combined, step = k.sem("pa_turned"), k.sem("pa_o"), k.sem("pa_comb"), k.sem("pa_step")
        out = [k.sem("pa_out0"), k.sem("pa_out1")]
        C_SCORED, C_EXPED, C_TURNED, C_OUT, C_O, C_COMB = 2, 2, 5, 1, 3, 2
        NEG, SUM, FAC = range(3)

        def width(j):
            i, g, kind, tiles = jobs[j]
            return 4 * (i + 1) if kind == C else P * len(tiles)

        def scores(j):
            b = 2 * (j % 2)
            w = width(j)
            return k.ps[:, b:b + 2, :].rearrange("p b n -> p (b n)")[:, 0:w]

        def turned_rows(j):
            return width(j) if jobs[j][2] == C else P

        qh_made = [k.sem(f"pp_qh{g}") for g in range(G)]
        with nc.Block() as block:
            half = [slice(g * DH, (g + 1) * DH) for g in range(G)]

            def low(eng, g):
                heads = slice(g * HPG, (g + 1) * HPG)
                eng.tensor_tensor(qP[half[1 - g], heads, :], k.qT[half[g], :, 0:SEQ], qP[half[g], heads, :], ALU.subtract)

            @block.scalar
            def _(act):
                nc.scalar.copy(qP[half[0], 0:HPG, :], k.qT[half[0], :, 0:SEQ]).then_inc(qh_made[0], 1)

            @block.gpsimd
            def _(pool):
                pool.wait_ge(qh_made[0], 1)
                low(nc.gpsimd, 0)

            @block.vector
            def _(dve):
                nc.vector.tensor_copy(qP[half[1], HPG:H, :], k.qT[half[1], :, 0:SEQ]).then_inc(qh_made[1], 1)
                dve.wait_ge(qh_made[1], 1)
                low(nc.vector, 1)

        with nc.Block() as block:

            @block.tensor
            def _(pe):
                pe.sem_inc(scored, C_SCORED)
                pe.sem_inc(turned, C_TURNED)
                pe.sem_inc(out_done, C_O)

                def score(hh, j):
                    i, g, kind, tiles = jobs[j]
                    pe.wait_ge(exped, hh * NJ + (j - 1 + C_EXPED))
                    w = width(j)
                    for a in range(0, w, 512):
                        n = min(512, w - a)
                        q = qP[:, bass.ds(hh + g * HPG, 1), i * P:(i + 1) * P].rearrange("p o n -> p (o n)")
                        for part, (whole, blocks) in enumerate(((kH, kcH), (kL, kcL))):
                            keys = blocks[:, g, 0:w] if kind == C else whole[:, g, kind - 1, tiles[0] * P + a:tiles[0] * P + a + n]
                            ins = nc.tensor.matmul(scores(j)[:, a:a + n], q, keys, start=(part == 0), stop=(part == 1))
                    ins.then_inc(scored, 1)

                def turn(hh, j):
                    pe.wait_ge(exped, hh * NJ + (j + 1 + C_EXPED))
                    n = turned_rows(j)
                    for bank, nth, _, tiles, a in groups[j]:
                        pe.wait_ge(out[bank], hh * count[bank] + (nth - 1 + 1 + C_OUT))
                        for u in range(len(tiles)):
                            ins = nc.tensor.transpose(k.ps[0:n, 4 + bank, u * P:(u + 1) * P],
                                                      prob[:, j % 3, (a + u) * P:(a + u) * P + n], k.c('ident'))
                        ins.then_inc(turned, 1)

                def values(hh, j):
                    i, g, kind, tiles = jobs[j]
                    for bank, nth, _, _, _ in groups[j]:
                        pe.wait_ge(out[bank], hh * count[bank] + (nth + 1 + C_OUT))
                    pe.wait_ge(combined, hh * NJ + (j - 1 + C_COMB))
                    n = turned_rows(j)
                    for u, t in enumerate(tiles):
                        v = k.vcN[0:n, 8, g * DH:(g + 1) * DH] if kind == C else k.vN[:, t, kind - 1, g * DH:(g + 1) * DH]
                        ins = nc.tensor.matmul(k.ps[:, 6 + j % 2, 0:DH], probT[0:n, j % 3, u, :], v,
                                               start=(u == 0), stop=(u == len(tiles) - 1))
                    ins.then_inc(out_done, 1)

                with pe.Fori(0, HPG) as hh:
                    for j in range(NJ + 4):
                        if j < NJ:
                            score(hh, j)
                        if 2 <= j < NJ + 2:
                            turn(hh, j - 2)
                        if j >= 4:
                            values(hh, j - 4)

            def turned_out(eng, copy, hh, j):
                n = turned_rows(j)
                for bank, nth, order, tiles, a in groups[j]:
                    eng.wait_ge(turned, hh * NG + (order + 1 + C_TURNED))
                    eng.wait_ge(out_done, hh * NJ + (j - 2 + C_O))
                    w = len(tiles) * P
                    copy(probT[0:n, j % 3, a:a + len(tiles), :].rearrange("p u n -> p (u n)"),
                         k.ps[0:n, 4 + bank, 0:w]).then_inc(out[bank], 1)

            @block.scalar
            def _(act):
                act.sem_inc(exped, C_EXPED)
                act.sem_inc(out[0], C_OUT)
                act.sem_inc(out[1], C_OUT)
                with act.Fori(0, HPG) as hh:
                    for j in range(NJ + 2):
                        if j >= 2:
                            turned_out(act, nc.scalar.copy, hh, j - 2)
                        if j < NJ:
                            act.wait_ge(maxed, hh * NJ + (j + 1))
                            before = groups[j - 3][-1][2] + 1 - (0 if j >= 3 else NG)
                            act.wait_ge(turned, hh * NG + (before + C_TURNED))
                            nc.scalar.activation(prob[:, j % 3, 0:width(j)], scores(j), ACT.Exp, bias=stat[:, NEG, j % 12:j % 12 + 1],
                                                 accum_out=stat[:, SUM, j % 12:j % 12 + 1]).then_inc(exped, 1)

            @block.vector
            def _(dve):
                dve.sem_inc(combined, C_COMB)
                done = [0]

                def settle(hh, ins):
                    done[0] += 1
                    ins.then_inc(step, 1)
                    dve.wait_ge(step, hh * STEPS + done[0])

                def maximum(hh, j):
                    i, g, kind, tiles = jobs[j]
                    dve.wait_ge(scored, hh * NJ + (j + 1 + C_SCORED))
                    sc, w = scores(j), width(j)
                    near = min(2, i + 1)
                    bias = k.toep[:, bass.ds(hh + g * HPG, 1), (2 - near) * P:2 * P].rearrange("p o n -> p (o n)")
                    if kind == C:
                        part = sc[:, w - 4 * near:w]
                        ins = nc.vector.tensor_tensor(part, part, bias[:, CB - 1::CB], ALU.add)
                    else:
                        if kind == W and len(tiles) == WIN // P + 1:
                            nc.vector.tensor_tensor(sc[:, 0:P], sc[:, 0:P], k.c('winmask'), ALU.add)
                        part = sc[:, w - near * P:w]
                        ins = nc.vector.tensor_tensor(part, part, bias, ALU.add)
                    settle(hh, ins)
                    neg = stat[:, NEG, j % 12:j % 12 + 1]
                    ins = nc.vector.tensor_reduce(neg, sc, AX, ALU.max, negate=True)
                    if kind == C:
                        settle(hh, ins)
                        ins = nc.vector.tensor_scalar(neg, neg, 1e20, None, ALU.min)
                    ins.then_inc(maxed, 1)

                def factors(hh, j):
                    i, g = jobs[j][0], jobs[j][1]
                    dve.wait_ge(exped, hh * NJ + (j + 1 + C_EXPED))
                    three = slice((j - 2) % 12, (j - 2) % 12 + 3)
                    fac = stat[:, FAC, three]
                    settle(hh, nc.vector.tensor_scalar(fac, stat[:, SUM, three], 1e-30, None, ALU.max))
                    settle(hh, nc.vector.reciprocal(fac, fac))
                    gate = k.gN[:, i, :].rearrange("p (z h) -> p z h", z=3)[:, :, bass.ds(hh + g * HPG, 1)].rearrange("p z o -> p (z o)")
                    settle(hh, nc.vector.tensor_tensor(fac, gate, fac, ALU.mult))

                def combine(hh, j):
                    i, g, kind, tiles = jobs[j]
                    dve.wait_ge(out_done, hh * NJ + (j + 1 + C_O))
                    o = k.ps[:, 6 + j % 2, 0:DH]
                    fac = stat[:, FAC, j % 12:j % 12 + 1]
                    acc = oacc[:, i, bass.ds((hh + g * HPG) * DH, DH)]
                    if kind == C:
                        ins = nc.vector.tensor_scalar(acc, o, fac, None, ALU.mult)
                    else:
                        dve.wait_ge(combined, hh * NJ + (j + C_COMB))
                        ins = nc.vector.scalar_tensor_tensor(acc, o, fac, acc, ALU.mult, ALU.add)
                    ins.then_inc(combined, 1)

                with dve.Fori(0, HPG) as hh:
                    for j in range(NJ + 5):
                        if j < NJ:
                            maximum(hh, j)
                        if j % 3 == 1 and 1 < j < NJ + 2:
                            factors(hh, j - 2)
                        if j >= 5:
                            combine(hh, j - 5)
                    assert done[0] == STEPS

        t_turned, t_hi, t_lo = k.sem("pt_turned"), k.sem("pt_hi"), k.sem("pt_lo")
        with nc.Block() as block:

            @block.tensor
            def _(pe):
                for t in range(NT):
                    if t >= 4:
                        pe.wait_ge(t_lo, t - 3)
                    for m in range(4):
                        ins = nc.tensor.transpose(k.ps[:, t % 4, m * P:(m + 1) * P], oacc[:, t, m * P:(m + 1) * P], k.c('ident'))
                    ins.then_inc(t_turned, 1)

            def tile(buf, t):
                return buf[:, 0:4, t * P:(t + 1) * P]

            def bank(t):
                return k.ps[:, t % 4, :].rearrange("p (m n) -> p m n", m=4)

            @block.scalar
            def _(act):
                for t in range(NT):
                    act.wait_ge(t_turned, t + 1)
                    nc.scalar.copy(tile(k.oH, t), bank(t)).then_inc(t_hi, 1)
                nc.scalar.copy(k.oH[:, 0:4, SEQ:], k.oTs[:, :, :]).then_inc(t_hi, 1)

            @block.vector
            def _(dve):
                for t in range(NT):
                    dve.wait_ge(t_hi, t + 1)
                    nc.vector.tensor_tensor(tile(k.oL, t), bank(t), tile(k.oH, t), ALU.subtract).then_inc(t_lo, 1)
                dve.wait_ge(t_hi, NT + 1)
                nc.vector.tensor_tensor(k.oL[:, 0:4, SEQ:], k.oTs[:, :, :], k.oH[:, 0:4, SEQ:], ALU.subtract)


def lru(k):
    nc, d = k.nc, k.d
    MT = R // P
    CWD = 4
    n = 2 * MT
    dn = Dense(k, "lrp", n)
    s = {x: k.sem("lr_" + x) for x in ("in", "cleared", "gw", "sturn", "conv", "gate", "gsig", "expo",
                                       "tanh", "quot", "root", "beta", "scan", "prod", "hi", "lam", "lexp", "step", "pack",
                                       "pturn", "pout", "stored", "taps")}
    with ExitStack() as es:
        sb = lambda nm, sh, t=F32: es.enter_context(nc.sbuf_tensor("lr" + nm, sh, t))
        xin, xs = sb("xin", [P, MT, 3 + SEQ]), sb("xs", [P, MT, NB, 3 + NS])
        gg, xc = sb("gg", [P, MT, T]), sb("xc", [P, MT, T])
        rg, ig = sb("rg", [P, MT, T]), sb("ig", [P, MT, T])
        gw = sb("gw", [P, 2, MT, P])
        srow, h0, lam = sb("srow", [32, R]), sb("h0", [P, MT, NB]), sb("lam", [P, 6, MT])
        a5, b5, h5 = sb("a5", [P, NB, NS + 1]), sb("b5", [P, NB, NS + 1]), sb("h5", [P, MT, NB, NS + 1])
        pack, prow = sb("pack", [P, MT, 36]), sb("prow", [36, R])
        with nc.Block() as block:

            @block.sync
            def _(sp):
                sp.dma_start(srow[0:24, :], d['state_lru_conv'].rearrange("b j c -> (b j) c")).then_inc(s["in"], 16)
                sp.dma_start(srow[24:32, :], d['state_lru_h']).then_inc(s["in"], 16)
                for i in range(n):
                    dn.load(sp, i, i % 4, w_tile(d['w_in'], COL['lg' if i % 2 else 'lx'] + i // 2 * P), first=i < 4)
                sp.wait_ge(s["cleared"], 1)
                for z in range(2):
                    for u in range(2):
                        r = slice(u * 64, (u + 1) * 64)
                        sp.dma_start(gw[r, z, :, r], d['lru_gate_w'][z].rearrange("(m u) c e -> u c m e", u=2)[u]).then_inc(s["gw"], 16)
                sp.wait_ge(s["gw"], 64)

            @block.gpsimd
            def _(pool):
                nc.gpsimd.memset(gw[:, :, :, :], 0.0).then_inc(s["cleared"], 1)
                nc.gpsimd.memset(xin[:, :, 0:3], 0.0)

            @block.scalar
            def _(act):
                dn.start_evac(act)
                dn.split_hi(act, 0, 0, 0)
                for i in range(n):
                    if i + 1 < n:
                        dn.split_hi(act, i + 1, (i + 1) % 4, (i + 1) // 4)
                    dn.wait_tile(act, i)
                    m = i // 2
                    if i % 2:
                        nc.scalar.activation(cols3(gg[:, m, :]), dense_out(k.ps, 1), ACT.Gelu_apprx_tanh,
                                             bias=k.vec[:, VB_LG + m:VB_LG + m + 1], scale=1 / WS).then_inc(dn.evacuated, 1)
                    else:
                        b = k.vec[:, VB_LX + m:VB_LX + m + 1]
                        ins = nc.scalar.activation(cols3(rg[:, m, :]), dense_out(k.ps, 0), ACT.Identity, bias=b, scale=1 / WS)
                        ins.then_inc(dn.evacuated, 1)

            @block.vector
            def _(dve):
                for i in range(n):
                    dn.split_lo(dve, i, i % 4)
                    if i % 2:
                        m = i // 2
                        dve.wait_ge(dn.evacuated, 2 * m + 1 + 2)
                        nc.vector.tensor_copy(xin[:, m, 3:], rg[:, m, 0:SEQ])
                        nc.vector.tensor_copy(xs[:, m, :, 3:], rg[:, m, SEQ:].rearrange("p (b t) -> p b t", b=NB))
                dve.wait_ge(s["sturn"], 1)
                states = k.ps[:, 7, 0:P].rearrange("p (m r) -> p m r", m=MT)
                nc.vector.tensor_copy(h0[:, :, :], states[:, :, 24:32])
                for m in range(MT):
                    nc.vector.tensor_copy(xs[:, m, :, 0:3], states[:, m, 0:24].rearrange("p (b j) -> p b j", b=NB))

            @block.tensor
            def _(pe):
                pe.wait_ge(s["in"], 32)
                for m in range(MT):
                    ins = nc.tensor.transpose(k.ps[:, 7, m * 32:(m + 1) * 32], srow[:, m * P:(m + 1) * P], k.c('ident')[0:32, 0:32])
                ins.then_inc(s["sturn"], 1)
                dn.multiply_all(pe, k.hH, k.hL)

        vec = lambda c: k.vec[:, c:c + 1]
        with nc.Block() as block:

            @block.vector
            def _(dve):
                tt, ts, stt = nc.vector.tensor_tensor, nc.vector.tensor_scalar, nc.vector.scalar_tensor_tensor
                step = [0]

                def settle(ins):
                    step[0] += 1
                    ins.then_inc(s["step"], 1)
                    dve.wait_ge(s["step"], step[0])

                LV = k.vec[:, V_LAM:V_LAM + MT]
                settle(ts(lam[:, 0, :], LV, -1.0, None, ALU.mult))
                settle(tt(lam[:, 0, :], LV, lam[:, 0, :], ALU.max))
                ts(lam[:, 1, :], LV, -1.0, 0.0, ALU.mult, ALU.max).then_inc(s["lam"], 1)
                dve.wait_ge(s["lexp"], 1)
                z, w, w2, poly = lam[:, 2, :], lam[:, 3, :], lam[:, 4, :], lam[:, 5, :]
                settle(ts(w, z, 2.0, None, ALU.add))
                settle(nc.vector.reciprocal(w, w))
                settle(tt(w, w, z, ALU.mult))
                settle(tt(w2, w, w, ALU.mult))
                settle(ts(poly, w2, 1 / 17, 1 / 15, ALU.mult, ALU.add))
                for q in (13, 11, 9, 7, 5, 3, 1):
                    settle(tt(poly, poly, w2, ALU.mult))
                    settle(ts(poly, poly, 1 / q, None, ALU.add))
                settle(tt(poly, poly, w, ALU.mult))
                settle(stt(poly, poly, 2.0, lam[:, 1, :], ALU.mult, ALU.add))
                settle(ts(k.vec[:, V_LRC:V_LRC + MT], poly, -8.0, None, ALU.mult))
                ts(lam[:, 0, :], poly, 8.0, None, ALU.mult).then_inc(s["lam"], 1)

                for m in range(MT):
                    xcs = xc[:, m, SEQ:].rearrange("p (b t) -> p b t", b=NB)
                    ts(xc[:, m, 0:SEQ], xin[:, m, 0:SEQ], vec(V_CW + m), vec(V_CB + m), ALU.mult, ALU.add).then_inc(s["taps"], 1)
                    ts(xcs, xs[:, m, :, 0:NS], vec(V_CW + m), vec(V_CB + m), ALU.mult, ALU.add).then_inc(s["taps"], 1)
                    for j in range(1, CWD):
                        dve.wait_ge(s["taps"], 8 * m + 2 * j)
                        ins = stt(xc[:, m, 0:SEQ], xin[:, m, j:j + SEQ], vec(V_CW + 4 * j + m), xc[:, m, 0:SEQ], ALU.mult, ALU.add)
                        ins.then_inc(s["taps"], 1)
                        ins = stt(xcs, xs[:, m, :, j:j + NS], vec(V_CW + 4 * j + m), xcs, ALU.mult, ALU.add)
                        ins.then_inc(s["taps"], 1)
                    dve.wait_ge(s["taps"], 8 * m + 8)
                    nc.vector.tensor_copy(pack[:, m, 0:3], xin[:, m, SEQ:SEQ + 3])
                    ins = nc.vector.tensor_copy(pack[:, m, 3:27].rearrange("p (b j) -> p b j", b=NB), xs[:, m, :, NS:NS + 3])
                    ins.then_inc(s["conv"], 1)
                for m in range(MT):
                    dve.wait_ge(s["gsig"], 2 * m + 2)
                    ins = tt(ig[:, m, :], ig[:, m, :], xc[:, m, :], ALU.mult).then_inc(s["beta"], 1)
                for m in range(MT):
                    dve.wait_ge(s["expo"], m + 1)
                    dve.wait_ge(s["tanh"], m + 1)
                    sq, sqs = xin[:, m, 0:SEQ], h5[:, m, :, 0:NS]
                    a_s, us = (v[:, m, SEQ:].rearrange("p (b t) -> p b t", b=NB) for v in (xc, rg))
                    tt(sq, xc[:, m, 0:SEQ], xc[:, m, 0:SEQ], ALU.mult)
                    settle(tt(sqs, a_s, a_s, ALU.mult))
                    stt(rg[:, m, 0:SEQ], sq, 1.0, rg[:, m, 0:SEQ], ALU.add, ALU.mult)
                    stt(us, sqs, 1.0, us, ALU.add, ALU.mult).then_inc(s["quot"], 1)
                settle(nc.vector.memset(a5[:, :, 0:1], 0.0))
                for m in range(MT):
                    dve.wait_ge(s["root"], m + 1)
                    settle(tt(ig[:, m, :], ig[:, m, :], rg[:, m, :], ALU.mult))
                    nc.vector.tensor_copy(b5[:, :, 0:1], h0[:, m, :].unsqueeze(2))
                    nc.vector.tensor_copy(b5[:, :, 1:], ig[:, m, SEQ:].rearrange("p (b t) -> p b t", b=NB))
                    settle(nc.vector.tensor_copy(a5[:, :, 1:], xc[:, m, SEQ:].rearrange("p (b t) -> p b t", b=NB)))
                    nc.vector.tensor_tensor_scan(rg[:, m, 0:SEQ], xc[:, m, 0:SEQ], ig[:, m, 0:SEQ], 0.0, ALU.mult, ALU.add)
                    settle(nc.vector.tensor_tensor_scan(h5[:, m, :, :].rearrange("p b t -> p (b t)"), a5[:, :, :].rearrange("p b t -> p (b t)"),
                                                        b5[:, :, :].rearrange("p b t -> p (b t)"), 0.0, ALU.mult, ALU.add))
                    nc.vector.tensor_copy(pack[:, m, 27:28], rg[:, m, SEQ - 1:SEQ])
                    nc.vector.tensor_copy(pack[:, m, 28:36], h5[:, m, :, NS]).then_inc(s["pack"], 1)
                    tt(gg[:, m, 0:SEQ], gg[:, m, 0:SEQ], rg[:, m, 0:SEQ], ALU.mult)
                    gs = gg[:, m, SEQ:].rearrange("p (b t) -> p b t", b=NB)
                    tt(gs, gs, h5[:, m, :, 1:], ALU.mult).then_inc(s["prod"], 1)
                dve.wait_ge(s["pturn"], 1)
                nc.vector.tensor_copy(prow[:, :], k.ps[0:36, 7, :]).then_inc(s["pout"], 1)

            @block.tensor
            def _(pe):
                for m in range(MT):
                    pe.wait_ge(s["conv"], m + 1)
                    for z in range(2):
                        if m >= 1:
                            pe.wait_ge(s["gsig"], 2 * m + z - 1)
                        for c in range(3):
                            ins = nc.tensor.matmul(k.ps[:, 3 * z + c, 0:CH], gw[:, z, m, :], xc[:, m, c * CH:(c + 1) * CH],
                                                   start=True, stop=True)
                        ins.then_inc(s["gate"], 1)
                pe.wait_ge(s["pack"], MT)
                for m in range(MT):
                    ins = nc.tensor.transpose(k.ps[0:36, 7, m * P:(m + 1) * P], pack[:, m, :], k.c('ident'))
                ins.then_inc(s["pturn"], 1)

            @block.scalar
            def _(act):
                act.wait_ge(s["lam"], 1)
                nc.scalar.activation(lam[:, 2, :], lam[:, 0, :], ACT.Exp, scale=-1.0).then_inc(s["lexp"], 1)
                for m in range(MT):
                    for z in range(2):
                        act.wait_ge(s["gate"], 2 * m + z + 1)
                        nc.scalar.activation(cols3((rg, ig)[z][:, m, :]), dense_out(k.ps, z), ACT.Sigmoid,
                                             bias=vec(V_LGB + 4 * z + m)).then_inc(s["gsig"], 1)
                act.wait_ge(s["lam"], 2)
                for m in range(MT):
                    act.wait_ge(s["beta"], m + 1)
                    act.wait_ge(s["gsig"], 2 * m + 1)
                    nc.scalar.activation(xc[:, m, :], rg[:, m, :], ACT.Exp, scale=vec(V_LRC + m)).then_inc(s["expo"], 1)
                    nc.scalar.activation(rg[:, m, :], rg[:, m, :], ACT.Tanh, scale=lam[:, 0, m:m + 1]).then_inc(s["tanh"], 1)
                for m in range(MT):
                    act.wait_ge(s["quot"], m + 1)
                    nc.scalar.activation(rg[:, m, :], rg[:, m, :], ACT.Sqrt).then_inc(s["root"], 1)
                for m in range(MT):
                    act.wait_ge(s["prod"], m + 1)
                    nc.scalar.copy(k.oH[:, 4 + m, :], gg[:, m, :]).then_inc(s["hi"], 1)

            @block.gpsimd
            def _(pool):
                for m in range(MT):
                    pool.wait_ge(s["hi"], m + 1)
                    nc.gpsimd.tensor_tensor(k.oL[:, 4 + m, :], gg[:, m, :], k.oH[:, 4 + m, :], ALU.subtract)

            @block.sync
            def _(sp):
                sp.wait_ge(s["pout"], 1)
                for rows, out in ((prow[0:3, :], d['out_conv_p'][0, 0]), (prow[3:27, :], d['out_conv_s'][0].rearrange("b j c -> (b j) c")),
                                  (prow[27:28, :], d['out_h_p'][0]), (prow[28:36, :], d['out_h_s'][0])):
                    sp.dma_start(out, rows).then_inc(s["stored"], 16)
                sp.wait_ge(s["stored"], 64)


def gla(k):
    nc, d = k.nc, k.d
    n = 13
    cols = [COL['ga']] + [COL['gq'] + i * P for i in range(8)] + [COL['gg'] + i * P for i in range(4)]
    dn = Dense(k, "glp", n)
    NC = SEQ // GC
    s = {x: k.sem("gl_" + x) for x in ("aw", "x", "abs", "exp", "ln", "g", "cum", "gate", "alpha", "init", "step", "e1", "em", "ed", "dec",
                                       "qi", "ki", "kd", "tr", "vout", "kout", "att", "attm", "ds", "state", "o", "sq", "ms",
                                       "root", "on", "ot", "res", "hi", "lo", "s0", "mask", "qm", "kdm", "stored", "q2")}
    with ExitStack() as es:
        sb = lambda nm, sh, t=F32: es.enter_context(nc.sbuf_tensor("gl" + nm, sh, t))
        kk, vT, sg = sb("k", [P, 2, T]), sb("v", [P, 4, T]), sb("sg", [P, 4, T])
        q2 = sb("q", [P, 2, 2, T])
        q = q2[:, 1]
        aT, aw, reset = sb("aT", [16, T]), sb("aw", [16, 256]), sb("reset", [P, T])
        ki, kd = sb("ki", [P, 2, T]), sb("kd", [P, 2, T])
        gx = k.oH[:, 8:12, :].rearrange("p a b -> p (a b)").bitcast(F32).rearrange("p (m t) -> p m t", m=2)
        bc = k.oL[:, 8:12, :].rearrange("p a b -> p (a b)").bitcast(F32).rearrange("p (m t) -> p m t", m=2)
        dec, dec_s = sb("dec", [P, 2, NC]), sb("decs", [P, 2 * NB])

        def chunks(ap):
            return ((ap[:, 0:SEQ].rearrange("p (c t) -> p c t", t=GC), ap[:, GC - 1:SEQ:GC]),
                    (ap[:, SEQ:].rearrange("p (c t) -> p c t", t=NS), ap[:, SEQ + NS - 1::NS]))

        with nc.Block() as block:

            @block.sync
            def _(sp):
                sp.dma_start(aw[:, :], d['gla_alpha_w']).then_inc(s["aw"], 16)
                for i in range(n):
                    dn.load(sp, i, i % 4, w_tile(d['w_in'], cols[i]), first=i < 4)

            @block.scalar
            def _(act):
                def alphas():
                    for u in range(6):
                        m, c = u // 3, slice(u % 3 * CH, (u % 3 + 1) * CH)
                        act.wait_ge(s["alpha"], u + 1)
                        nc.scalar.activation(gx[:, m, c], k.ps[:, 6 + u % 2, 0:CH], ACT.Identity, bias=k.vec[:, V_GAB + m:V_GAB + m + 1]).then_inc(s["x"], 1)

                def exps():
                    for m in range(2):
                        act.wait_ge(s["abs"], m + 1)
                        nc.scalar.activation(ki[:, m, :], ki[:, m, :], ACT.Exp, scale=-1.0).then_inc(s["exp"], 1)

                def logs():
                    for m in range(2):
                        act.wait_ge(s["exp"], m + 1)
                        nc.scalar.activation(ki[:, m, :], ki[:, m, :], ACT.Ln, bias=1.0).then_inc(s["ln"], 1)

                def decays(m):
                    act.wait_ge(s["cum"], 2 * m + 2)
                    nc.scalar.activation(gx[:, m, :], bc[:, m, :], ACT.Exp, scale=1 / 16).then_inc(s["e1"], 1)
                    nc.scalar.activation(ki[:, m, :], bc[:, m, :], ACT.Exp, scale=-1 / 16).then_inc(s["em"], 1)
                    nc.scalar.activation(kd[:, m, :], kd[:, m, :], ACT.Exp, scale=1 / 16).then_inc(s["ed"], 1)
                    nc.scalar.activation(dec[:, m, :], bc[:, m, GC - 1:SEQ:GC], ACT.Exp, scale=1 / 16)
                    nc.scalar.activation(dec_s[:, m::2], bc[:, m, SEQ + NS - 1::NS], ACT.Exp, scale=1 / 16)

                dn.start_evac(act)
                dn.split_hi(act, 0, 0, 0)
                for i in range(n):
                    if i + 1 < n:
                        dn.split_hi(act, i + 1, (i + 1) % 4, (i + 1) // 4)
                    dn.wait_tile(act, i)
                    ps = dense_out(k.ps, i % 2)
                    if i == 0:
                        ins = nc.scalar.activation(cols3(aT[:, :]), ps[0:16], ACT.Identity, bias=k.vec[0:16, VB_GA:VB_GA + 1], scale=1 / WS)
                    elif i < 9:
                        out = (q[:, 0], q[:, 1], kk[:, 0], kk[:, 1], vT[:, 0], vT[:, 1], vT[:, 2], vT[:, 3])[i - 1]
                        ins = nc.scalar.activation(cols3(out), ps, ACT.Identity, bias=k.vec[:, VB_GQ + i - 1:VB_GQ + i], scale=1 / WS)
                    else:
                        h = i - 9
                        ins = nc.scalar.activation(cols3(sg[:, h, :]), ps, ACT.Silu, bias=k.vec[:, VB_GG + h:VB_GG + h + 1], scale=1 / WS)
                    ins.then_inc(dn.evacuated, 1)
                    if i == 1:
                        alphas()
                    elif i == 2:
                        exps()
                    elif i == 3:
                        logs()
                    elif i in (6, 7):
                        decays(i - 6)

            @block.vector
            def _(dve):
                tt, stt = nc.vector.tensor_tensor, nc.vector.scalar_tensor_tensor

                def absolutes():
                    for m in range(2):
                        dve.wait_ge(s["x"], 3 * m + 3)
                        stt(ki[:, m, :], gx[:, m, :], -1.0, gx[:, m, :], ALU.mult, ALU.max).then_inc(s["abs"], 1)

                def cumulate(m):
                    dve.wait_ge(s["ln"], m + 1)
                    stt(gx[:, m, :], gx[:, m, :], 0.0, ki[:, m, :], ALU.min, ALU.subtract).then_inc(s["g"], 1)
                    dve.wait_ge(s["g"], m + 1)
                    nc.vector.tensor_tensor_scan(bc[:, m, :], reset[:, :], gx[:, m, :], 0.0, ALU.mult, ALU.add).then_inc(s["cum"], 1)
                    dve.wait_ge(s["cum"], 2 * m + 1)
                    for (whole, last), (out, _) in zip(chunks(bc[:, m, :]), chunks(kd[:, m, :])):
                        ins = stt(out, whole, -1.0, last.unsqueeze(2).broadcast_to(whole.shape), ALU.mult, ALU.add)
                    ins.then_inc(s["cum"], 1)

                def scale(m):
                    dve.wait_ge(dn.evacuated, 5 + 2)
                    dve.wait_ge(s["e1"], m + 1)
                    for u in range(2):
                        r = slice(u * GK, (u + 1) * GK)
                        ins = stt(q2[r, u, m, :], q[r, m, :], GK ** -0.5, gx[r, m, :], ALU.mult, ALU.mult)
                    ins.then_inc(s["q2"], 1)
                    dve.wait_ge(s["em"], m + 1)
                    tt(ki[:, m, :], kk[:, m, :], ki[:, m, :], ALU.mult)
                    dve.wait_ge(s["ed"], m + 1)
                    tt(kd[:, m, :], kk[:, m, :], kd[:, m, :], ALU.mult)

                nc.vector.memset(reset[:, :], 1.0).then_inc(s["init"], 1)
                dve.wait_ge(s["init"], 1)
                nc.vector.memset(reset[:, 0:SEQ:GC], 0.0)
                nc.vector.memset(reset[:, SEQ:T:NS], 0.0).then_inc(s["init"], 1)
                dve.wait_ge(s["init"], 2)
                for i in range(n):
                    dn.split_lo(dve, i, i % 4)
                    if i == 3:
                        absolutes()
                    elif i in (5, 6):
                        cumulate(i - 5)
                    elif i in (8, 9):
                        scale(i - 8)
                    elif i == 10:
                        dve.wait_ge(s["q2"], 2)
                        for u in range(2):
                            nc.vector.memset(q2[(1 - u) * GK:(2 - u) * GK, u], 0.0)

            @block.gpsimd
            def _(pool):
                for h in range(GH):
                    pool.wait_ge(dn.evacuated, 2 + 10 + h)
                    nc.gpsimd.tensor_scalar(sg[:, h, :], sg[:, h, :], k.vec[:, V_GNG + h:V_GNG + h + 1], None, ALU.mult)

            @block.tensor
            def _(pe):
                dn.start_pe(pe)
                for i in range(2):
                    dn.multiply(pe, i, i, k.hH, k.hL)
                pe.wait_ge(s["aw"], 16)
                pe.wait_ge(dn.evacuated, 1 + 2)
                for u in range(6):
                    m, c = u // 3, slice(u % 3 * CH, (u % 3 + 1) * CH)
                    if u >= 2:
                        pe.wait_ge(s["x"], u - 1)
                    nc.tensor.matmul(k.ps[:, 6 + u % 2, 0:CH], aw[:, m * P:(m + 1) * P], aT[:, c], start=True, stop=True).then_inc(s["alpha"], 1)
                with pe.Fori(1, n // 2) as j:
                    dn.multiply(pe, j * 2, 0, k.hH, k.hL)
                    dn.multiply(pe, j * 2 + 1, 1, k.hH, k.hL)
                dn.multiply(pe, n - 1, 0, k.hH, k.hL)

        rows = [P] * NT + [TS]
        vN, kN = sb("vN", [P, 2, 512]), sb("kN", [P, 2, 256])
        stat = sb("stat", [P, 2, 4])
        slots = k.w32[:, :, :, :].rearrange("p a b c -> p (a b c)")
        S = slots[:, 0:1024].rearrange("p (s m v) -> p s m v", s=4, m=2)
        sq, on = slots[:, 3072:3584], slots[:, 3584:4096]
        att, res = (w[:, :, :, :].rearrange("p a b c -> p (a b c)").bitcast(F32).rearrange("p (s n) -> p s n", s=2)
                    for w in (k.wH, k.wL))
        spare = kk[:, :, :].rearrange("p m t -> p (m t)")
        S0 = spare[:, 0:2048].rearrange("p (b m v) -> p b m v", b=NB, m=2)
        reset_f = reset[:, :]
        qm = reset_f[:, 0:1024].rearrange("p (u m b t) -> p u m b t", u=2, m=2, b=NB)
        kdm = slots[0:TS, 1024:3072].rearrange("p (b n) -> p b n", b=NB)
        BV, BK, BA, BD, BO, BT = 0, 1, 2, (3, 5), 4, 6
        with nc.Block() as block:

            @block.sync
            def _(sp):
                for m in range(2):
                    sp.dma_start(S0[:, :, m, :], d['state_gla'].rearrange("b (m u) k v -> m (u k) b v", m=2)[m]).then_inc(s["s0"], 16)
                sp.wait_ge(s["state"], 1 + NC)
                sp.dma_start(d['out_gla_p'][0, 0].rearrange("(m u) k v -> (u k) m v", m=2), S[:, NC % 4]).then_inc(s["stored"], 16)
                sp.wait_ge(s["state"], 1 + NC + 2)
                for m in range(2):
                    sp.dma_start(d['out_gla_s'][0].rearrange("b (m u) k v -> m (u k) b v", m=2)[m], S0[:, :, m, :]).then_inc(s["stored"], 16)
                sp.wait_ge(s["stored"], 48)

            def hp(h):
                return slice(h % 2 * GK, h % 2 * GK + GK)

            def turn_out(pe, t):
                w = rows[t]
                pe.wait_ge(s["on"], t + 1)
                if t:
                    pe.wait_ge(s["res"], t)
                for h in range(GH):
                    ins = nc.tensor.transpose(k.ps[:, BT, h * P:h * P + w], on[0:w, h * P:(h + 1) * P], k.c('ident')[0:w, 0:w])
                ins.then_inc(s["ot"], 1)

            def heads(ap, w=P):
                return ap.rearrange("p (h n) -> p h n", h=GH)[:, :, 0:w]

            def after(act, t):
                w = rows[t]
                act.wait_ge(s["o"], t + 1)
                if t:
                    act.wait_ge(s["ms"], 2 * t)
                nc.scalar.activation(sq[0:w, :], k.ps[0:w, BO, :], ACT.Square).then_inc(s["sq"], 1)
                act.wait_ge(s["ms"], 2 * t + 2)
                nc.scalar.activation(stat[0:w, t % 2, :], stat[0:w, t % 2, :], ACT.Sqrt).then_inc(s["root"], 1)
                act.wait_ge(s["res"], t + 1)
                c = slice(t * P, t * P + w)
                nc.scalar.copy(k.oH[:, 8:12, c], heads(res[:, t % 2, :], w)).then_inc(s["hi"], 1)

            def finish(dve, t):
                w, c = rows[t], slice(t * P, t * P + rows[t])
                st = stat[0:w, t % 2, :]
                dve.wait_ge(s["sq"], t + 1)
                nc.vector.tensor_reduce(st, heads(sq[0:w, :]), AX, ALU.add).then_inc(s["ms"], 1)
                dve.wait_ge(s["ms"], 2 * t + 1)
                nc.vector.tensor_scalar(st, st, 1.0 / GV, EPS, ALU.mult, ALU.add).then_inc(s["ms"], 1)
                dve.wait_ge(s["root"], t + 1)
                nc.vector.reciprocal(st, st).then_inc(s["step"], 1)
                dve.wait_ge(s["step"], t + 1)
                nc.vector.tensor_tensor(heads(on[0:w, :]), heads(k.ps[0:w, BO, :]), st.unsqueeze(2).broadcast_to([w, GH, GV]),
                                        ALU.mult).then_inc(s["on"], 1)
                dve.wait_ge(s["ot"], t + 1)
                if t >= 2:
                    dve.wait_ge(s["lo"], t - 1)
                nc.vector.tensor_tensor(heads(res[:, t % 2, :], w), heads(k.ps[:, BT, :], w), sg[:, :, c], ALU.mult).then_inc(s["res"], 1)

            @block.tensor
            def _(pe):
                def turn(t):
                    w, c = rows[t], slice(t * P, t * P + rows[t])
                    if t >= 1:
                        pe.wait_ge(s["vout"], t)
                        pe.wait_ge(s["kout"], t)
                    for h in range(GH):
                        nc.tensor.transpose(k.ps[0:w, BV, h * P:(h + 1) * P], vT[:, h, c], k.c('ident'))
                    for m in range(2):
                        ins = nc.tensor.transpose(k.ps[0:w, BK, m * P:(m + 1) * P], kd[:, m, c], k.c('ident'))
                    ins.then_inc(s["tr"], 1)

                turn(0)
                for t in range(NT + 1):
                    w, c = rows[t], slice(t * P, t * P + rows[t])
                    if t:
                        pe.wait_ge(s["attm"], t)
                    for h in range(GH):
                        ins = nc.tensor.matmul(k.ps[0:w, BA, h * P:h * P + w], ki[:, h // 2, c], q2[:, h % 2, h // 2, c], start=True, stop=True)
                    ins.then_inc(s["att"], 1)
                    if t < NT:
                        turn(t + 1)
                    pe.wait_ge(s["vout"], t + 1)
                    pe.wait_ge(s["kout"], t + 1)
                    if t < NT:
                        if t:
                            pe.wait_ge(s["state"], 1 + 2 * t)
                        for ch in range(2):
                            r = slice(ch * GC, (ch + 1) * GC)
                            for h in range(GH):
                                ins = nc.tensor.matmul(k.ps[hp(h), BD[ch], h // 2 * GV:(h // 2 + 1) * GV],
                                                       kN[r, t % 2, h * GK:(h + 1) * GK], vN[r, t % 2, h * GV:(h + 1) * GV], start=True, stop=True)
                        ins.then_inc(s["ds"], 1)
                    pe.wait_ge(s["attm"], t + 1)
                    if t:
                        pe.wait_ge(s["on"], t)
                    ob = BO
                    for h in range(GH):
                        nc.tensor.matmul(k.ps[0:w, ob, h * GV:(h + 1) * GV], att[0:w, t % 2, h * P:h * P + w], vN[0:w, t % 2, h * GV:(h + 1) * GV],
                                         start=True, stop=False)
                        if t < NT:
                            for ch in range(2):
                                n_ch = 2 * t + ch
                                pe.wait_ge(s["state"], 1 + n_ch)
                                cc = slice(t * P + ch * GC, t * P + (ch + 1) * GC)
                                ins = nc.tensor.matmul(k.ps[ch * GC:(ch + 1) * GC, ob, h * GV:(h + 1) * GV], q2[:, h % 2, h // 2, cc],
                                                       S[:, n_ch % 4, h // 2, :], start=False, stop=True)
                        else:
                            pe.wait_ge(s["s0"], 32)
                            pe.wait_ge(s["qm"], 4)
                            for b in range(NB):
                                ins = nc.tensor.matmul(k.ps[0:w, ob, h * GV:(h + 1) * GV], qm[:, h % 2, h // 2, b, :], S0[:, b, h // 2, :],
                                                       start=False, stop=(b == NB - 1))
                    ins.then_inc(s["o"], 1)
                    if t:
                        turn_out(pe, t - 1)
                pe.wait_ge(s["kdm"], 1)
                pe.wait_ge(s["attm"], NT + 1)
                pe.wait_ge(s["state"], 1 + NC)
                for b in range(NB):
                    for h in range(GH):
                        o = b % 2 * 256 + h // 2 * GV
                        ins = nc.tensor.matmul(k.ps[hp(h), b // 2, o:o + GV], kdm[:, b, h * GK:(h + 1) * GK], vN[0:TS, NT % 2, h * GV:(h + 1) * GV],
                                               start=True, stop=True)
                ins.then_inc(s["ds"], 1)
                turn_out(pe, NT)

            @block.scalar
            def _(act):
                for t in range(NT + 1):
                    w = rows[t]
                    act.wait_ge(s["tr"], t + 1)
                    if t >= 2:
                        act.wait_ge(s["o"], t - 1)
                    nc.scalar.copy(vN[0:w, t % 2, :], k.ps[0:w, BV, :]).then_inc(s["vout"], 1)
                    nc.scalar.copy(kN[0:w, t % 2, :], k.ps[0:w, BK, 0:256]).then_inc(s["kout"], 1)
                    if t:
                        after(act, t - 1)
                after(act, NT)

            @block.gpsimd
            def _(pool):
                for t in range(NT + 1):
                    w, c = rows[t], slice(t * P, t * P + rows[t])
                    pool.wait_ge(s["hi"], t + 1)
                    nc.gpsimd.tensor_tensor(k.oL[:, 8:12, c], heads(res[:, t % 2, :], w), k.oH[:, 8:12, c], ALU.subtract).then_inc(s["lo"], 1)

            @block.vector
            def _(dve):
                tt, ts, stt = nc.vector.tensor_tensor, nc.vector.tensor_scalar, nc.vector.scalar_tensor_tensor
                nc.vector.memset(S[:, 0], 0.0).then_inc(s["state"], 1)
                for m in range(2):
                    for u in range(2):
                        tt(qm[:, u, m], k.c('seqcols').rearrange("p (b t) -> p b t", b=NB),
                           q2[:, u, m, SEQ:].unsqueeze(1).broadcast_to([P, NB, TS]), ALU.mult).then_inc(s["qm"], 1)
                for t in range(NT + 1):
                    w = rows[t]
                    dve.wait_ge(s["att"], t + 1)
                    if t >= 2:
                        dve.wait_ge(s["o"], t - 1)
                    mask = k.c('gmask') if t < NT else k.c('gmask_s', TS)
                    tt(heads(att[0:w, t % 2, :], w), heads(k.ps[0:w, BA, :], w),
                       mask.unsqueeze(1).broadcast_to([w, GH, w]), ALU.mult).then_inc(s["attm"], 1)
                    if t < NT:
                        dve.wait_ge(s["ds"], t + 1)
                        for ch in range(2):
                            n_ch = 2 * t + ch
                            dve.wait_ge(s["state"], 1 + n_ch)
                            if n_ch >= 3:
                                dve.wait_ge(s["o"], (n_ch - 3) // 2 + 1)
                            for m in range(2):
                                ins = stt(S[:, (n_ch + 1) % 4, m, :], S[:, n_ch % 4, m, :], dec[:, m, n_ch:n_ch + 1],
                                          k.ps[:, BD[ch], m * GV:(m + 1) * GV], ALU.mult, ALU.add)
                            ins.then_inc(s["state"], 1)
                    else:
                        dve.wait_ge(s["kout"], NT + 1)
                        tt(kdm[:, :, :], kN[0:TS, NT % 2, :].unsqueeze(1).broadcast_to([TS, NB, 256]),
                           k.c('seqrows', TS).unsqueeze(2).broadcast_to([TS, NB, 256]), ALU.mult).then_inc(s["kdm"], 1)
                    if t:
                        finish(dve, t - 1)
                dve.wait_ge(s["ds"], NT + 1)
                dve.wait_ge(s["s0"], 32)
                flat_s0 = S0.rearrange("p b m v -> p (b m) v")
                dve.wait_ge(s["o"], NT + 1)
                tt(flat_s0, flat_s0, dec_s[:, :].unsqueeze(2).broadcast_to([P, 2 * NB, GV]), ALU.mult).then_inc(s["state"], 1)
                dve.wait_ge(s["state"], 1 + NC + 1)
                tt(S0.rearrange("p b m v -> p (b m v)"), S0.rearrange("p b m v -> p (b m v)"),
                   k.ps[:, 0:4, :].rearrange("p a n -> p (a n)"), ALU.add).then_inc(s["state"], 1)
                finish(dve, NT)


def merge(k):
    nc, d = k.nc, k.d
    loaded = [k.sem(f"mg_w{i}") for i in range(3)]
    split_hi, split_lo = k.sem("mg_hi"), k.sem("mg_lo")
    gate_mult, used, gate_out, branch_out = k.sem("mg_gmult"), k.sem("mg_used"), k.sem("mg_gout"), k.sem("mg_bout")
    added, sum_hi, sum_lo = k.sem("mg_added"), k.sem("mg_sumhi"), k.sem("mg_sumlo")
    NU = 3 * KD
    with nc.sbuf_tensor("mgw", [P, 3, 12, P], F32) as w32, nc.sbuf_tensor("mgwH", [P, 2, 12, P], F16) as wH, \
            nc.sbuf_tensor("mgwL", [P, 2, 12, P], F16) as wL, nc.sbuf_tensor("mgsg", [P, 2, T], F32) as sg, \
            nc.sbuf_tensor("mgacc", [P, 2, T], F32) as acc, nc.sbuf_tensor("mgtmp", [P, T], F32) as tmp, \
            nc.Block() as block:

        def units(eng, body, lookahead):
            if lookahead:
                with eng.Fori(0, NU // 6 - 1) as it:
                    for u in range(6):
                        body(it * 6 + u, u, it * 2 + u // 3)
                for u in range(6):
                    body(NU - 6 + u, u, KD - 2 + u // 3)
            else:
                with eng.Fori(0, NU // 6) as it:
                    for u in range(6):
                        body(it * 6 + u, u, it * 2 + u // 3)

        @block.sync
        def _(sp):
            def load(u, dt):
                z, slot = u % 3, u % 3
                sp.dma_start(w32[:, slot, 0:8, :], w_tile(d['w_in'], COL['merge'] + z * D + dt * P)).then_inc(loaded[slot], 16)
                sp.dma_start(w32[:, slot, 8:12, :], d['w_branch'][z][:, bass.ds(dt * P, P)].rearrange("(kt p) n -> p kt n", p=P)).then_inc(loaded[slot], 16)

            for u in range(3):
                load(u, 0)
            with sp.Fori(1, KD) as dt:
                for u in range(3):
                    sp.wait_ge(split_lo, dt * 3 + (u - 2))
                    load(u, dt)

        @block.tensor
        def _(pe):
            pe.sem_inc(used, 2)

            def unit(i, u, dt):
                s, z = u % 2, u % 3
                pe.wait_ge(split_lo, i + 1)
                pe.wait_ge(gate_out, i + 1)
                for kt in range(KD):
                    for w, x in ((wH, k.hH), (wH, k.hL), (wL, k.hH)):
                        for c in range(3):
                            ins = nc.tensor.matmul(k.ps[:, c, 0:CH], w[:, s, kt, :], x[:, kt, c * CH:(c + 1) * CH],
                                                   start=(kt == 0 and w is wH and x is k.hH), stop=(kt == KD - 1 and w is wL))
                ins.then_inc(gate_mult, 1)
                pe.wait_ge(branch_out, i + 2)
                for kt in range(4):
                    for w, x in ((wH, k.oH), (wH, k.oL), (wL, k.oH)):
                        for c in range(3):
                            ins = nc.tensor.matmul(k.ps[:, 3 + c, 0:CH], w[:, s, 8 + kt, :], x[:, 4 * z + kt, c * CH:(c + 1) * CH],
                                                   start=(kt == 0 and w is wH and x is k.oH), stop=(kt == 3 and w is wL))
                ins.then_inc(used, 1)

            units(pe, unit, False)

        @block.scalar
        def _(act):
            act.sem_inc(gate_out, 1)

            def split(i, u):
                act.wait_ge(used, i + 1)
                nc.scalar.activation(wH[:, u % 2, :, :], w32[:, u % 3, :, :], ACT.Copy, scale=WS).then_inc(split_hi, 1)

            def unit(i, u, dt):
                if not isinstance(i, int) or i + 1 < NU:
                    nxt = (u + 1) % 6
                    act.wait_ge(loaded[nxt % 3], (dt + (1 if nxt % 3 == 0 else 0)) * 32 + 32)
                    split(i + 1, nxt)
                act.wait_ge(gate_mult, i + 1)
                act.wait_ge(branch_out, i + 1)
                b = VB_MG + u % 3 * KD + dt
                nc.scalar.activation(cols3(sg[:, u % 2, :]), dense_out(k.ps, 0), ACT.Sigmoid, bias=k.vec[:, bass.ds(b, 1)],
                                     scale=1 / WS).then_inc(gate_out, 1)
                if u % 3 == 2:
                    act.wait_ge(added, dt * 2 + 3)
                    nc.scalar.copy(k.mH[:, bass.ds(dt, 1), :], acc[:, u // 3, :].unsqueeze(1)).then_inc(sum_hi, 1)

            act.wait_ge(loaded[0], 32)
            split(0, 0)
            units(act, unit, True)

        @block.vector
        def _(dve):
            dve.sem_inc(branch_out, 2)
            dve.sem_inc(added, 1)

            def split(i, u):
                dve.wait_ge(split_hi, i + 1)
                nc.vector.scalar_tensor_tensor(wL[:, u % 2, :, :], w32[:, u % 3, :, :], WS, wH[:, u % 2, :, :],
                                               ALU.mult, ALU.subtract).then_inc(split_lo, 1)

            def unit(i, u, dt):
                if not isinstance(i, int) or i + 1 < NU:
                    split(i + 1, (u + 1) % 6)
                z, a = u % 3, u // 3
                if z == 0:
                    dve.wait_ge(sum_lo, dt + 1)
                else:
                    dve.wait_ge(added, dt * 2 + z)
                dve.wait_ge(gate_out, i + 2)
                dve.wait_ge(used, i + 3)
                out = acc[:, a, :] if z == 0 else tmp[:, :]
                nc.vector.scalar_tensor_tensor(cols3(out), ps_branch, 1 / WS, cols3(sg[:, u % 2, :]), ALU.mult, ALU.mult).then_inc(branch_out, 1)
                if z:
                    dve.wait_ge(branch_out, i + 3)
                    nc.vector.tensor_tensor(acc[:, a, :], acc[:, a, :], tmp[:, :], ALU.add).then_inc(added, 1)

            ps_branch = dense_out(k.ps, 1)
            split(0, 0)
            units(dve, unit, True)

        @block.gpsimd
        def _(pool):
            pool.sem_inc(sum_lo, 2)
            with pool.Fori(0, KD // 2) as it:
                for a in range(2):
                    dt = it * 2 + a
                    pool.wait_ge(sum_hi, dt + 1)
                    o = bass.ds(dt, 1)
                    nc.gpsimd.tensor_tensor(k.mL[:, o, :], acc[:, a, :].unsqueeze(1), k.mH[:, o, :], ALU.subtract).then_inc(sum_lo, 1)


def square(k, act, i, sq, squared, added):
    if i >= 3:
        act.wait_ge(added, i - 2)
    out = k.ssq[:, :] if i == 0 else sq[:, i % 2, :]
    k.nc.scalar.activation(out, k.xT[:, i, :], ACT.Square).then_inc(squared, 1)


def add_square(k, dve, i, sq, squared, added):
    dve.wait_ge(squared, i + 1)
    if i >= 2:
        dve.wait_ge(added, i - 1)
    k.nc.vector.tensor_tensor(k.ssq[:, :], k.ssq[:, :], sq[:, i % 2, :], ALU.add).then_inc(added, 1)


def w_out(k):
    nc, d, xT = k.nc, k.d, k.xT
    dn, x_back, squared, added = Dense(k, "wo", KD), k.sem("wo_x"), k.sem("wo_sq"), k.sem("wo_added")
    with nc.sbuf_tensor("wosq", [P, 2, T], F32) as sq, nc.Block() as block:

        @block.sync
        def _(sp):
            for i in range(KD):
                dn.load(sp, i, i % 4, w_tile(d['w_out'], i * P), first=i < 4)
                if i == 3:
                    sp.dma_start(flat(xT[:, :, :]), k.xTd).then_inc(x_back, 16)

        @block.scalar
        def _(act):
            dn.split_hi(act, 0, 0, 0)
            for i in range(KD):
                if i + 1 < KD:
                    dn.split_hi(act, i + 1, (i + 1) % 4, (i + 1) // 4)
                act.wait_ge(dn.evacuated, i + 3)
                square(k, act, i, sq, squared, added)

        @block.vector
        def _(dve):
            dn.start_evac(dve)
            dn.split_lo(dve, 0, 0)
            dve.wait_ge(x_back, 16)
            for i in range(KD):
                if i + 1 < KD:
                    dn.split_lo(dve, i + 1, (i + 1) % 4)
                dn.wait_tile(dve, i)
                nc.vector.scalar_tensor_tensor(cols3(xT[:, i, :]), dense_out(k.ps, i % 2), 1 / WS, cols3(xT[:, i, :]),
                                               ALU.mult, ALU.add).then_inc(dn.evacuated, 1)
                if i >= 2:
                    add_square(k, dve, i - 1, sq, squared, added)
            add_square(k, dve, KD - 1, sq, squared, added)

        @block.tensor
        def _(pe):
            dn.multiply_all(pe, k.mH, k.mL)


def mlp(k):
    nc, d, xT, aH, aL = k.nc, k.d, k.xT, k.mH, k.mL
    NG = FF // D
    dn = Dense(k, "mp", 2 * KD * NG)
    hi_made, squared, lo_made = k.sem("mp_ahi"), k.sem("mp_sq"), k.sem("mp_alo")
    xsquared, xadded = k.sem("mp_xsq"), k.sem("mp_xadd")
    with nc.sbuf_tensor("mprelu", [P, 2, T], F32) as relu, nc.sbuf_tensor("mpxsq", [P, 2, T], F32) as xsq, nc.sbuf_tensor("mpsq", [P, T], F32) as sq, nc.Block() as block:

        def groups(eng, body):
            with eng.Fori(0, NG - 1) as g:
                for t in range(2 * KD):
                    body(g, t, g * 16 + t)
            for t in range(2 * KD):
                body(NG - 1, t, (NG - 1) * 16 + t)

        def last(i):
            return isinstance(i, int) and i + 1 == dn.n

        @block.sync
        def _(sp):
            def load(g, t, i):
                src = w_tile(d['mlp_w1'], g * D + t * P) if t < KD else \
                    d['mlp_w2'][bass.ds(g * D, D), (t - KD) * P:(t - KD + 1) * P].rearrange("(kt p) n -> p kt n", p=P)
                dn.load(sp, i, t % 4, src, first=isinstance(i, int) and i < 4)

            for t in range(2 * KD):
                load(0, t, t)
            with sp.Fori(1, NG) as g:
                for t in range(2 * KD):
                    load(g, t, g * 16 + t)

        @block.tensor
        def _(pe):
            dn.start_pe(pe)
            with pe.Fori(0, NG) as g:
                with pe.Fori(0, KD // 2) as j:
                    for u in range(2):
                        dn.multiply(pe, g * 16 + j * 2 + u, u, k.hH, k.hL)
                dn.multiply(pe, g * 16 + KD, 0, aH, aL, ready=lambda pe, kt: pe.wait_ge(lo_made, g * 8 + (kt + 3)))
                dn.multiply(pe, g * 16 + KD + 1, 1, aH, aL)
                with pe.Fori(1, KD // 2) as j:
                    for u in range(2):
                        dn.multiply(pe, g * 16 + j * 2 + (KD + u), u, aH, aL)

        @block.scalar
        def _(act):
            def tile(g, t, i):
                if not last(i):
                    nxt = (t + 1) % 16
                    dn.split_hi(act, i + 1, nxt % 4, g * 4 + (t + 1) // 4)
                if t < KD:
                    act.wait_ge(dn.evacuated, i + 3)
                    nc.scalar.activation(aH[:, t, :], relu[:, t % 2, :], ACT.Square).then_inc(hi_made, 1)
                elif isinstance(i, int):
                    act.wait_ge(dn.evacuated, i + 3)
                    square(k, act, t - KD, xsq, xsquared, xadded)

            dn.split_hi(act, 0, 0, 0)
            groups(act, tile)

        @block.vector
        def _(dve):
            def tile(g, t, i):
                if not last(i):
                    dn.split_lo(dve, i + 1, (t + 1) % 4)
                dn.wait_tile(dve, i)
                ps = dense_out(k.ps, t % 2)
                if t < KD:
                    dve.wait_ge(lo_made, g * 8 + (t + 1))
                    ins = nc.vector.tensor_scalar(cols3(relu[:, t % 2, :]), ps, 1 / WS, 0.0, ALU.mult, ALU.max)
                else:
                    dve.wait_ge(dn.evacuated, i + 2)
                    ins = nc.vector.scalar_tensor_tensor(cols3(xT[:, t - KD, :]), ps, 1 / WS, cols3(xT[:, t - KD, :]), ALU.mult, ALU.add)
                ins.then_inc(dn.evacuated, 1)
                if isinstance(i, int) and t >= KD + 2:
                    add_square(k, dve, t - KD - 1, xsq, xsquared, xadded)

            dn.start_evac(dve)
            dn.split_lo(dve, 0, 0)
            groups(dve, tile)
            add_square(k, dve, KD - 1, xsq, xsquared, xadded)

        @block.gpsimd
        def _(pool):
            pool.sem_inc(lo_made, 2)
            with pool.Fori(0, NG) as g:
                for t in range(KD):
                    n = g * 8 + t
                    pool.wait_ge(dn.evacuated, g * 16 + (t + 3))
                    pool.wait_ge(lo_made, n + 2)
                    nc.gpsimd.tensor_tensor(sq[:, :], relu[:, t % 2, :], relu[:, t % 2, :], ALU.mult).then_inc(squared, 1)
                    pool.wait_ge(squared, n + 1)
                    pool.wait_ge(hi_made, n + 1)
                    nc.gpsimd.tensor_tensor(aL[:, t, :], sq[:, :], aH[:, t, :], ALU.subtract).then_inc(lo_made, 1)


def final_norm(k):
    nc, d, xT = k.nc, k.d, k.xT
    summed, ms_ready, root_ready, step, scale_ready = (k.sem("y_" + n) for n in ("summed", "ms", "root", "step", "scale"))
    diag_ready, turned, out0, out1 = k.sem("y_diag"), k.sem("y_turned"), k.sem("y_out0"), k.sem("y_out1")
    stored = [k.sem(f"y_stored{i}") for i in range(2)]
    yp = d['out_y_prompt'].rearrange("b (n p) c -> (b n) p c", p=P)
    ys = d['out_y_sample'].rearrange("b t c -> (b t) c")
    NC = NT + 1
    with nc.sbuf_tensor("yn", [P, 2, D], F32) as yn, nc.sbuf_tensor("ydiag", [P, KD, P], F32) as diag, \
            nc.sbuf_tensor("yst", [P, 4, 16], F32) as st, nc.Block() as block:
        ms, root, y, t2 = (st[:, i, 0:NC] for i in range(4))

        @block.tensor
        def _(pe):
            for t in range(NC):
                w = P if t < NT else TS
                ins = nc.tensor.matmul(k.ps[0:w, 7, t:t + 1], k.ssq[:, t * P:t * P + w], k.c('ones')[:, 0:1], start=True, stop=True)
            ins.then_inc(summed, 1)
            pe.wait_ge(diag_ready, 1)
            for t in range(NC):
                w = P if t < NT else TS
                if t == 3:
                    pe.wait_ge(ms_ready, 3)
                if t >= 4:
                    pe.wait_ge(out0, t - 3)
                    pe.wait_ge(out1, t - 3)
                for kt in range(KD):
                    ins = nc.tensor.matmul(k.ps[0:w, 2 * (t % 4) + kt // 4, kt % 4 * P:(kt % 4 + 1) * P], xT[:, kt, t * P:t * P + w],
                                           diag[:, kt, :], start=True, stop=True)
                    if kt == 3:
                        ins.then_inc(turned, 1)
                ins.then_inc(turned, 1)

        @block.scalar
        def _(act):
            act.wait_ge(ms_ready, 3)
            nc.scalar.activation(root, ms, ACT.Sqrt).then_inc(root_ready, 1)
            act.wait_ge(scale_ready, 1)
            for t in range(NC):
                w = P if t < NT else TS
                act.wait_ge(turned, 2 * t + 1)
                if t >= 2:
                    act.wait_ge(stored[t % 2], 16 * (t // 2))
                nc.scalar.activation(yn[0:w, t % 2, 0:512], k.ps[0:w, 2 * (t % 4), :], ACT.Copy, scale=y[0:w, t:t + 1]).then_inc(out0, 1)

        @block.vector
        def _(dve):
            tt, ts = nc.vector.tensor_tensor, nc.vector.tensor_scalar
            tt(diag[:, :, :], k.c('ident').unsqueeze(1).broadcast_to([P, KD, P]),
               k.vec[:, VG3:VG3 + KD].unsqueeze(2).broadcast_to([P, KD, P]), ALU.mult).then_inc(diag_ready, 1)
            nc.vector.memset(ms, 1.0).then_inc(ms_ready, 1)
            dve.wait_ge(ms_ready, 1)
            dve.wait_ge(summed, 1)
            ts(ms[:, 0:NT], k.ps[:, 7, 0:NT], 1.0 / D, EPS, ALU.mult, ALU.add).then_inc(ms_ready, 1)
            ts(ms[0:TS, NT:NC], k.ps[0:TS, 7, NT:NC], 1.0 / D, EPS, ALU.mult, ALU.add).then_inc(ms_ready, 1)
            dve.wait_ge(root_ready, 1)
            made = [0]

            def settle(ins):
                made[0] += 1
                ins.then_inc(step, 1)
                dve.wait_ge(step, made[0])

            settle(nc.vector.reciprocal(y, root))
            settle(tt(t2, y, y, ALU.mult))
            settle(tt(t2, t2, ms, ALU.mult))
            settle(ts(t2, t2, -0.5, 1.5, ALU.mult, ALU.add))
            tt(y, y, t2, ALU.mult).then_inc(scale_ready, 1)
            dve.wait_ge(scale_ready, 1)
            for t in range(NC):
                w = P if t < NT else TS
                dve.wait_ge(turned, 2 * t + 2)
                if t >= 2:
                    dve.wait_ge(stored[t % 2], 16 * (t // 2))
                ts(yn[0:w, t % 2, 512:D], k.ps[0:w, 2 * (t % 4) + 1, :], y[0:w, t:t + 1], None, ALU.mult).then_inc(out1, 1)

        @block.sync
        def _(sp):
            for t in range(NC):
                sp.wait_ge(out0, t + 1)
                sp.wait_ge(out1, t + 1)
                if t < NT:
                    sp.dma_start(yp[t], yn[:, t % 2, :]).then_inc(stored[t % 2], 16)
                else:
                    sp.dma_start(ys, yn[0:TS, t % 2, :]).then_inc(stored[t % 2], 16)
            sp.wait_ge(stored[0], 16 * 5)
            sp.wait_ge(stored[1], 16 * 4)


def build(nc, d):
    k = Prog(nc, d)
    with ExitStack() as ctx:
        sb = lambda n, s, t=F32: ctx.enter_context(nc.sbuf_tensor(n, s, t))
        k.cst = sb("cst", [P, CW])
        k.c = lambda n, rows=P: k.cst[0:rows, CN[n][0]:CN[n][0] + CN[n][1]]
        k.vec = sb("vec", [P, 256])
        k.hH, k.hL = sb("hH", [P, KD, T], F16), sb("hL", [P, KD, T], F16)
        k.oH, k.oL = sb("oH", [P, 12, T], F16), sb("oL", [P, 12, T], F16)
        k.w32 = sb("w32", [P, 4, KD, P])
        k.wH, k.wL = sb("wH", [P, 2, KD, P], F16), sb("wL", [P, 2, KD, P], F16)
        k.ps = ctx.enter_context(nc.psum_tensor("ps", [P, 8, 512], F32))
        k.xTd = nc.dram_tensor("xTd", (P, KD * T), F32, kind="Internal").ap()
        k.skew = nc.dram_tensor("skew", (H, P, 384), F32, kind="Internal").ap()
        k.sums = sb("sums", [P, NT + 1])
        with nc.sbuf_tensor("xT", [P, KD, T], F32) as xT:
            k.xT = xT
            load(k)
            k.end_stage()
            norm(k, "n1", VG1, sums_by_token=True)
            k.end_stage()
        with ExitStack() as nsa:
            sb2 = lambda n, s, t=F32: nsa.enter_context(nc.sbuf_tensor(n, s, t))
            k.kcT = sb2("kcT", [P, 9, NCB])
            k.vcN = sb2("vcN", [NCB, 9, P])
            k.cmpT = sb2("cmpT", [P, 2, T])
            compress(k)
            k.end_stage()
            k.qT = sb2("qT", [P, HPG, T])
            k.kT = sb2("kT", [P, 2, T])
            k.vN = sb2("vN", [P, NT, 2, P])
            k.vS = sb2("vS", [NS, NB, 2, P])
            k.gN = sb2("gN", [P, NT + 1, 24])
            k.toep = sb2("toep", [P, H, 256])
            k.oTs = sb2("oTs", [P, 4, TS])
            project_nsa(k)
            k.end_stage()
            kparts = k.w32[:, :, :, :].rearrange("p a b c -> p (a b c)").bitcast(F16)
            k.kH, k.kL = (kparts[:, u * 4096:(u + 1) * 4096].rearrange("p (g z t) -> p g z t", g=G, z=2) for u in range(2))
            k.kcH, k.kcL = sb2("kcH", [P, G, NCB], F16), sb2("kcL", [P, G, NCB], F16)
            sample_attention(k)
            k.end_stage()
            prompt_attention(k)
            k.end_stage()
        lru(k)
        k.end_stage()
        gla(k)
        k.end_stage()
        with ExitStack() as tail:
            k.mH = tail.enter_context(nc.sbuf_tensor("mH", [P, KD, T], F16))
            k.mL = tail.enter_context(nc.sbuf_tensor("mL", [P, KD, T], F16))
            merge(k)
            k.end_stage()
            k.xT = tail.enter_context(nc.sbuf_tensor("xT2", [P, KD, T], F32))
            k.ssq = tail.enter_context(nc.sbuf_tensor("ssq", [P, T], F32))
            w_out(k)
            k.end_stage()
            norm(k, "n2", VG2)
            k.end_stage()
            mlp(k)
            k.end_stage()
            final_norm(k)


OUTS = [('y_prompt', (1, SEQ, D)), ('y_sample', (NB, NS, D)),
        ('cmp_p', (1, 1, SEQ, 2, G, DH)), ('cmp_s', (1, NB, NS, 2, G, DH)),
        ('sel_p', (1, 1, SEQ, 2, G, DH)), ('sel_s', (1, NB, NS, 2, G, DH)),
        ('win_p', (1, 1, WIN, 2, G, DH)), ('win_s', (1, NB, WIN, 2, G, DH)),
        ('conv_p', (1, 1, 3, R)), ('conv_s', (1, NB, 3, R)), ('h_p', (1, 1, R)), ('h_s', (1, NB, R)),
        ('gla_p', (1, 1, GH, GK, GV)), ('gla_s', (1, NB, GH, GK, GV))]
SQUEEZED = ('w_in', 'b_in', 'w_branch', 'w_out', 'mlp_w1', 'mlp_w2', 'cache_nsa_cmp_kv', 'cache_nsa_sel_kv',
            'state_nsa_win_kv', 'state_lru_conv', 'state_lru_h', 'state_gla', 'nsa_cmp_pe', 'nsa_cmp_w1',
            'nsa_cmp_w2', 'lru_gate_w', 'gla_alpha_w')


def kernel(**inputs):
    import concourse.bacc as bacc
    from concourse.bass_utils import run_bass_kernel_spmd

    nc = bacc.Bacc("TRN2", target_bir_lowering=False, num_devices=1)
    arrays, d = {}, {}
    for name, a in list(inputs.items()) + [('consts', shape_constants())]:
        a = np.ascontiguousarray(a)
        arrays[f"in_{name}"] = a
        ap = nc.dram_tensor(f"in_{name}", a.shape, mybir.dt.from_np(a.dtype), kind="ExternalInput").ap()
        d[name] = ap[0] if name in SQUEEZED else ap
    for name, shape in OUTS:
        d['out_' + name] = nc.dram_tensor(f"out_{name}", shape, F32, kind="ExternalOutput").ap()
    build(nc, d)
    r = run_bass_kernel_spmd(nc, [arrays], core_ids=[0])
    return tuple(r.results[0][f"out_{n}"] for n, _ in OUTS)
```

```python
from contextlib import ExitStack

import numpy as np

import concourse.bass as bass
from concourse import mybir

F32 = mybir.dt.float32
F16 = mybir.dt.float16
I32 = mybir.dt.int32
ACT = mybir.ActivationFunctionType
ALU = mybir.AluOpType
AX = mybir.AxisListType.X

P = 128
D = 1024
KD = D // P
SEQ = 1024
NB = 8
NS = 4
TS = NB * NS
T = SEQ + TS
NT = SEQ // P
CH = T // 3
PAST = 1024
PAGES = PAST // P
H, G, HPG, DH = 8, 2, 4, 64
WIN = 512
CB = 32
NCB = SEQ // CB
SB = 64
NSB = PAST // SB
R = 512
GH, GK, GV = 4, 64, 128
GC = 64
FF = 4096
EPS = 1e-6
WS = 64.0
BIG = 1e30
COL = {}
_o = 0
for _n, _w in (('q', 512), ('cmp', 256), ('sel', 256), ('win', 256), ('ngate', 24), ('lx', 512),
               ('lg', 512), ('gq', 256), ('gk', 256), ('gv', 512), ('ga', 16), ('gg', 512),
               ('merge', 3072)):
    COL[_n] = _o
    _o += _w

CN = {}
_o = 0
for _n, _w in (('ident', 128), ('ones', 128), ('winmask', 128), ('gmask', 128), ('gmask_s', 32),
               ('headsum', 128), ('tokrow', 256), ('headhot', 24), ('seqcols', 256), ('seqrows', 8),
               ('winmask_s', 4), ('blk', 16), ('bucket', 384)):
    CN[_n] = (_o, _w)
    _o += _w
CW = _o


def shape_constants():
    c = np.zeros((P, CW), np.float32)

    def put(name, a):
        o, w = CN[name]
        c[:a.shape[0], o:o + w] = a

    i, j = np.arange(P)[:, None], np.arange(P)[None, :]
    put('ident', (i == j).astype(np.float32))
    put('ones', np.ones((P, P), np.float32))
    put('winmask', np.where(j <= i, -BIG, 0.0))
    put('gmask', ((i <= j) & (i // GC == j // GC)).astype(np.float32))
    s, t = np.arange(TS)[:, None], np.arange(TS)[None, :]
    put('gmask_s', ((s <= t) & (s // NS == t // NS)).astype(np.float32))
    seq, head, tok = np.arange(P) // 32, np.arange(P) % 32 // NS, np.arange(P) % NS
    grp = head // HPG
    put('headsum', ((seq[:, None] == seq) & (grp[:, None] == grp) & (tok[:, None] == tok)).astype(np.float32))
    put('tokrow', np.concatenate([(np.arange(TS)[:, None] == (4 * hf + seq) * NS + tok).astype(np.float32)
                                  for hf in range(2)], 1))
    put('headhot', (np.arange(24)[None] % 8 == head[:, None]).astype(np.float32))
    put('seqcols', np.broadcast_to((np.arange(NB)[:, None] == np.arange(TS)[None] // NS).reshape(1, -1), (P, 256)))
    put('seqrows', (np.arange(TS)[:, None] // NS == np.arange(NB)[None]).astype(np.float32))
    put('winmask_s', np.where(np.arange(NS)[None] <= tok[:, None], -BIG, 0.0))
    put('blk', np.broadcast_to(np.arange(16.0)[None], (P, 16)))
    b = np.zeros((33, 384), np.float32)
    for col in range(384):
        d = 255 - col
        if d < 0:
            b[32, col] = 1
            continue
        n = d if d < 16 else min(31, 16 + int(np.log(max(d, 1) / 16) / np.log(8) * 16 + 1e-9))
        b[n, col] += 1
        b[31, col] -= 1
    put('bucket', b)
    return c


class Prog:

    def __init__(self, nc, d):
        self.nc, self.d = nc, d
        self.stage, self.kept, self.pool = [], [], list(nc.free_semaphores)

    def sem(self, name, keep=False):
        sems = self.kept if keep else self.stage
        sems.append(self.nc.alloc_semaphore(name, self.pool.pop(0)))
        return sems[-1]

    def end_stage(self):
        self.nc.clear_and_free_semaphores(self.stage)
        self.pool += [s.num for s in self.stage]
        self.stage, self.kept = self.kept, []


def flat(ap):
    return ap.rearrange("p a b -> p (a b)")



VB_Q, VB_CMP, VB_SEL, VB_WIN, VB_NG, VB_LX, VB_LG = 0, 4, 6, 8, 10, 11, 15
VB_GQ, VB_GK, VB_GV, VB_GA, VB_GG, VB_MG = 19, 21, 23, 27, 28, 32
VG1, VG2, VG3 = 56, 64, 72
V_LGB, V_LAM, V_CW, V_CB, V_GAB, V_GNG = 80, 88, 92, 108, 112, 114
NV = 118
V_BQ8, V_LRC = 120, 124


def load(k):
    nc, d = k.nc, k.d
    loaded, table_loaded, ident_in, table_in = k.sem("c_loaded"), k.sem("c_table"), k.sem("c_ident"), k.sem("c_pages")
    vec_turned, bias_made, cols_ready = k.sem("c_turned"), k.sem("c_bias"), k.sem("c_cols")
    spread, rows_made, rows_out, table_set = k.sem("c_spread"), k.sem("c_rows"), k.sem("c_rowsout"), k.sem("c_tset")
    xl = [k.sem(f"x_loaded{i}") for i in range(3)]
    turned, copied, summed = k.sem("x_turned"), k.sem("x_copied"), k.sem("x_summed")
    k.saved = k.sem("x_saved", keep=True)
    xp = d['x_prompt'].rearrange("b (n p) c -> (b n) p c", p=P)
    xs = d['x_sample'].rearrange("b t c -> (b t) c")
    with nc.sbuf_tensor("vrows", [P, P], F32) as vrows, nc.sbuf_tensor("tbl", [33, H], F32) as tbl, \
            nc.sbuf_tensor("tblb", [33, H, P], F32) as tblb, nc.sbuf_tensor("brow", [P, H, 384], F32) as brow, \
            nc.sbuf_tensor("xn", [P, 3, D], F32) as xn, nc.sbuf_tensor("xsq", [P, D], F32) as xsq, nc.Block() as block:

        def half(u):
            t, hf = u // 2, u % 2
            return t, hf, P if t < NT else TS

        @block.sync
        def _(sp):
            sp.dma_start(k.cst[:, :], d['consts']).then_inc(ident_in, 16)
            sp.dma_start(k.ptab[:, :], d['page_table'].rearrange("(o a) b -> o (a b)", o=1)).then_inc(table_in, 16)
            for t in range(NT + 1):
                if t >= 3:
                    sp.wait_ge(turned, 2 * (t - 2))
                    sp.wait_ge(summed, t - 2)
                if t < NT:
                    sp.dma_start(xn[:, t % 3, :], xp[t]).then_inc(xl[t % 3], 16)
                else:
                    sp.dma_start(xn[0:TS, t % 3, :], xs).then_inc(xl[t % 3], 16)
            for h in range(H):
                sp.wait_ge(rows_made, h + 1)
                sp.dma_start(k.skew[h], brow[:, h, :]).then_inc(rows_out, 16)
            sp.wait_ge(rows_out, 16 * H)
            sp.wait_ge(copied, 2 * (NT + 1))
            sp.dma_start(k.xTd, flat(k.xT[:, :, :])).then_inc(k.saved, 16)
            sp.wait_ge(table_in, 16)

        @block.gpsimd
        def _(pool):
            b = d['b_in']
            rows = [(0, b, 0, 10), (10, b, COL['ngate'], 1), (11, b, COL['lx'], 8), (19, b, COL['gq'], 8),
                    (27, b, COL['ga'], 1), (28, b, COL['gg'], 28), (56, d['norm_mix_g'], 0, 8),
                    (64, d['norm_mlp_g'], 0, 8), (72, d['norm_final_g'], 0, 8), (80, d['lru_gate_b'], 0, 8),
                    (88, d['lru_lambda'], 0, 4), (92, d['lru_conv_w'], 0, 16), (108, d['lru_conv_b'], 0, 4),
                    (112, d['gla_alpha_b'], 0, 2), (114, d['gla_norm_g'], 0, 4)]
            pool.wait_ge(table_set, 1)
            pool.dma_start(tbl[0:32, :], d['rel_bias']).then_inc(table_loaded, 16)
            for r, src, off, n in rows:
                pool.dma_start(vrows[r:r + n, :], bass.AP(tensor=src.tensor, offset=off, ap=[[P, n], [1, P]])).then_inc(loaded, 16)

        @block.tensor
        def _(pe):
            pe.wait_ge(ident_in, 16)
            for u in range(2 * (NT + 1)):
                t, hf, n = half(u)
                if hf == 0:
                    pe.wait_ge(xl[t % 3], 16 * (t // 3 + 1))
                if u >= 4:
                    pe.wait_ge(copied, u - 3)
                for j in range(4):
                    ins = nc.tensor.transpose(k.ps[:, u % 4, j * P:j * P + n], xn[0:n, t % 3, (4 * hf + j) * P:(4 * hf + j + 1) * P],
                                              k.c('ident')[0:n, 0:n])
                ins.then_inc(turned, 1)
                if 4 <= u < 4 + H:
                    h = u - 4
                    pe.wait_ge(spread, 1)
                    if h >= 2:
                        pe.wait_ge(rows_made, h - 1)
                    nc.tensor.matmul(k.ps[:, 4 + h % 2, 0:384], tblb[:, h, :], k.c('bucket', 33),
                                     start=True, stop=True).then_inc(bias_made, 1)
            pe.wait_ge(loaded, 16 * 15)
            nc.tensor.transpose(k.ps[:, 6, 0:NV], vrows[0:NV, :], k.c('ident')[0:NV, 0:NV]).then_inc(vec_turned, 1)

        @block.scalar
        def _(act):
            for u in range(2 * (NT + 1)):
                t, hf, n = half(u)
                if hf == 0:
                    act.wait_ge(xl[t % 3], 16 * (t // 3 + 1))
                    if t:
                        act.wait_ge(summed, t)
                    nc.scalar.activation(xsq[0:n, :], xn[0:n, t % 3, :], ACT.Square, accum_out=k.sums[0:n, t:t + 1]).then_inc(summed, 1)
                act.wait_ge(turned, u + 1)
                nc.scalar.copy(k.xT[:, 4 * hf:4 * hf + 4, t * P:t * P + n],
                               k.ps[:, u % 4, :].rearrange("p (j n) -> p j n", j=4)[:, :, 0:n]).then_inc(copied, 1)

        @block.vector
        def _(dve):
            nc.vector.memset(tbl[32:33, :], -BIG).then_inc(table_set, 1)
            dve.wait_ge(table_set, 1)
            dve.wait_ge(table_loaded, 16)
            nc.vector.tensor_copy(tblb[:, :, :], tbl[:, :].unsqueeze(2).broadcast_to([33, H, P])).then_inc(spread, 1)
            for h in range(H):
                dve.wait_ge(bias_made, h + 1)
                nc.vector.tensor_copy(brow[:, h, :], k.ps[:, 4 + h % 2, 0:384]).then_inc(rows_made, 1)
            dve.wait_ge(vec_turned, 1)
            nc.vector.tensor_copy(k.vec[:, 0:NV], k.ps[:, 6, 0:NV]).then_inc(cols_ready, 1)
            dve.wait_ge(cols_ready, 1)
            nc.vector.tensor_scalar(k.vec[:, V_BQ8:V_BQ8 + 4], k.vec[:, VB_Q:VB_Q + 4], DH ** -0.5, None, ALU.mult)


def dense_out(ps, b, w=CH):
    return ps[:, 3 * b:3 * b + 3, 0:w]


def cols3(ap):
    return ap.rearrange("p (c n) -> p c n", c=3)


def norm(k, name, gcol, nxt, sums_by_token=False):
    nc, xT = k.nc, k.xT
    turned, ms_ready, root_ready, step = k.sem(name + "_turned"), k.sem(name + "_ms"), k.sem(name + "_root"), k.sem(name + "_step")
    diag_ready, spread = k.sem(name + "_diag"), k.sem(name + "_spread")
    scaled, hi_ready, lo_pool, lo_dve = k.sem(name + "_scaled"), k.sem(name + "_hi"), k.sem(name + "_lop"), k.sem(name + "_lod")
    NC = NT + 1
    by_dve = (1, 3, 5)
    with nc.sbuf_tensor(name + "dg", [P, NC, P], F32) as diag, nc.sbuf_tensor(name + "tmp", [P, 4, T], F32) as tmp, \
            nc.sbuf_tensor(name + "st", [P, 4, 16], F32) as st, nc.Block() as block:
        ms, root, y, t2 = (st[:, i, 0:NC] for i in range(4))
        sums = k.sums[:, :] if sums_by_token else k.ps[:, 7, 0:NC]

        @block.sync
        def _(sp):
            nxt.load_ahead(sp)
            if sums_by_token:
                sp.wait_ge(k.saved, 16)

        @block.tensor
        def _(pe):
            if not sums_by_token:
                for t in range(NC):
                    w = P if t < NT else TS
                    ins = nc.tensor.matmul(k.ps[0:w, 7, t:t + 1], k.ssq[:, t * P:t * P + w], k.c('ones')[:, 0:1], start=True, stop=True)
                ins.then_inc(turned, 1)
            pe.wait_ge(diag_ready, 1)
            for c in range(3):
                ins = nc.tensor.matmul(k.ps[:, c, 0:CH], k.c('ones'), diag[:, :, :].rearrange("p t n -> p (t n)")[:, c * CH:(c + 1) * CH],
                                       start=True, stop=True)
            ins.then_inc(spread, 1)

        @block.scalar
        def _(act):
            act.wait_ge(ms_ready, 3)
            nc.scalar.activation(root, ms, ACT.Sqrt).then_inc(root_ready, 1)
            for kt in range(KD):
                act.wait_ge(scaled, kt + 1)
                nc.scalar.copy(k.hH[:, kt, :], tmp[:, kt % 4, :]).then_inc(hi_ready, 1)
                if kt == 3:
                    nxt.split_hi_ahead(act)

        @block.vector
        def _(dve):
            tt, ts = nc.vector.tensor_tensor, nc.vector.tensor_scalar
            nc.vector.memset(ms, 1.0).then_inc(ms_ready, 1)
            dve.wait_ge(ms_ready, 1)
            if not sums_by_token:
                dve.wait_ge(turned, 1)
            ts(ms[:, 0:NT], sums[:, 0:NT], 1.0 / D, EPS, ALU.mult, ALU.add).then_inc(ms_ready, 1)
            ts(ms[0:TS, NT:NC], sums[0:TS, NT:NC], 1.0 / D, EPS, ALU.mult, ALU.add).then_inc(ms_ready, 1)
            dve.wait_ge(root_ready, 1)
            made = [0]

            def settle(ins):
                made[0] += 1
                ins.then_inc(step, 1)
                dve.wait_ge(step, made[0])

            settle(nc.vector.reciprocal(y, root))
            settle(tt(t2, y, y, ALU.mult))
            settle(tt(t2, t2, ms, ALU.mult))
            settle(ts(t2, t2, -0.5, 1.5, ALU.mult, ALU.add))
            settle(tt(y, y, t2, ALU.mult))
            tt(diag[:, :, :], k.c('ident').unsqueeze(1).broadcast_to([P, NC, P]), y.unsqueeze(2).broadcast_to([P, NC, P]),
               ALU.mult).then_inc(diag_ready, 1)
            dve.wait_ge(spread, 1)

            def low(kt):
                dve.wait_ge(hi_ready, kt + 1)
                tt(k.hL[:, kt, :], tmp[:, kt % 4, :], k.hH[:, kt, :], ALU.subtract).then_inc(lo_dve, 1)

            for kt in range(KD):
                if kt >= 4:
                    old = kt - 4
                    if old in by_dve:
                        dve.wait_ge(lo_dve, by_dve.index(old) + 1)
                    else:
                        dve.wait_ge(lo_pool, old // 2 + 1)
                nc.vector.scalar_tensor_tensor(cols3(tmp[:, kt % 4, :]), cols3(xT[:, kt, :]), k.vec[:, gcol + kt:gcol + kt + 1],
                                               dense_out(k.ps, 0), ALU.mult, ALU.mult).then_inc(scaled, 1)
                if kt - 1 in by_dve:
                    low(kt - 1)
                if kt == 4:
                    nxt.split_lo_ahead(dve)

        @block.gpsimd
        def _(pool):
            for kt in range(KD):
                if kt not in by_dve:
                    pool.wait_ge(hi_ready, kt + 1)
                    nc.gpsimd.tensor_tensor(k.hL[:, kt, :], tmp[:, kt % 4, :], k.hH[:, kt, :], ALU.subtract).then_inc(lo_pool, 1)


class Dense:

    def __init__(self, k, name, n, ahead=None):
        self.k, self.n, self.ahead = k, n, ahead
        keep = ahead is not None
        self.loaded = [k.sem(f"{name}_w{i}", keep) for i in range(4)]
        self.hi, self.lo = k.sem(name + "_hi", keep), k.sem(name + "_lo", keep)
        if keep:
            self.multiplied, self.evacuated = k.sem(name + "_mult", keep), k.sem(name + "_evac", keep)
            return
        self.multiplied, self.evacuated = k.sem(name + "_mult"), k.sem(name + "_evac")

    def load_ahead(self, sp):
        for slot, src in enumerate(self.ahead):
            sp.dma_start(self.k.w32[:, slot, :, :], src).then_inc(self.loaded[slot], 16)

    def split_hi_ahead(self, act):
        act.wait_ge(self.loaded[0], 16)
        self.k.nc.scalar.activation(self.k.wH[:, 0, :, :], self.k.w32[:, 0, :, :], ACT.Copy, scale=WS).then_inc(self.hi, 1)

    def split_lo_ahead(self, dve):
        dve.wait_ge(self.hi, 1)
        self.k.nc.vector.scalar_tensor_tensor(self.k.wL[:, 0, :, :], self.k.w32[:, 0, :, :], WS, self.k.wH[:, 0, :, :],
                                              ALU.mult, ALU.subtract).then_inc(self.lo, 1)

    def load(self, sp, i, slot, src, first=False):
        if first and self.ahead:
            return
        if not first:
            sp.wait_ge(self.lo, i - 3)
        sp.dma_start(self.k.w32[:, slot, :, :], src).then_inc(self.loaded[slot], 16)

    def start_pe(self, pe):
        pe.sem_inc(self.multiplied, 2)

    def start_evac(self, eng):
        eng.sem_inc(self.evacuated, 2)

    def split_hi(self, act, i, slot, turn):
        if self.ahead and isinstance(i, int) and i == 0:
            return
        act.wait_ge(self.loaded[slot], turn * 16 + 16)
        act.wait_ge(self.multiplied, i + 1)
        self.k.nc.scalar.activation(self.k.wH[:, slot % 2, :, :], self.k.w32[:, slot, :, :], ACT.Copy,
                                    scale=WS).then_inc(self.hi, 1)

    def split_lo(self, dve, i, slot):
        if self.ahead and isinstance(i, int) and i == 0:
            return
        dve.wait_ge(self.hi, i + 1)
        self.k.nc.vector.scalar_tensor_tensor(self.k.wL[:, slot % 2, :, :], self.k.w32[:, slot, :, :], WS,
                                              self.k.wH[:, slot % 2, :, :], ALU.mult, ALU.subtract).then_inc(self.lo, 1)

    def multiply(self, pe, i, parity, inH, inL, ready=None):
        k, nc = self.k, self.k.nc
        pe.wait_ge(self.lo, i + 1)
        pe.wait_ge(self.evacuated, i + 1)
        wH, wL = k.wH[:, parity], k.wL[:, parity]
        for kt in range(KD):
            if ready is not None:
                ready(pe, kt)
            for w, x in ((wH, inH), (wH, inL), (wL, inH)):
                for c in range(3):
                    ins = nc.tensor.matmul(k.ps[:, 3 * parity + c, 0:CH], w[:, kt, :], x[:, kt, c * CH:(c + 1) * CH],
                                           start=(kt == 0 and x is inH and w is wH), stop=(kt == KD - 1 and w is wL))
        ins.then_inc(self.multiplied, 1)

    def multiply_all(self, pe, inH, inL):
        self.start_pe(pe)
        if self.n >= 4:
            with pe.Fori(0, self.n // 2) as j:
                self.multiply(pe, j * 2, 0, inH, inL)
                self.multiply(pe, j * 2 + 1, 1, inH, inL)
        else:
            self.multiply(pe, 0, 0, inH, inL)
            self.multiply(pe, 1, 1, inH, inL)
        if self.n % 2:
            self.multiply(pe, self.n - 1, 0, inH, inL)

    def wait_tile(self, eng, i):
        eng.wait_ge(self.multiplied, i + 3)


def w_tile(w, col, k0=0):
    return w[k0:k0 + D, bass.ds(col, P)].rearrange("(kt p) n -> p kt n", p=P)


def compress(k, dn, nxt):
    nc, d = k.nc, k.d
    cmpT = k.cmpT
    WAVES, WB = 2, 4 * NCB
    PR = CB // 2
    TILES = 4 * PAGES // 2
    NBLK = (NB + 1) * NCB
    w_in, page_turned = k.sem("cb_win"), k.sem("cb_turned")
    page_in = [[k.sem(f"cb_page{a}_{s}") for s in range(8)] for a in range(2)]
    tile_out = [k.sem("cb_outs"), k.sem("cb_outv")]
    hid_done, hid_out, prompt_copied = k.sem("cb_hid"), k.sem("cb_hidout"), k.sem("cb_prompt")
    pe_turned, pe_copied, gelu_done, out_done, copied = (k.sem("cb_peturn"), k.sem("cb_pecopy"), k.sem("cb_gelu"),
                                                         k.sem("cb_out"), k.sem("cb_copied"))
    with nc.sbuf_tensor("w1p", [P, 2, PR, DH], F32) as w1, nc.sbuf_tensor("w2p", [DH, 2, DH], F32) as w2, \
            nc.sbuf_tensor("x2", [P, 2, G, WB * PR], F32) as x2, nc.sbuf_tensor("pen", [PR, 2, 2, DH], F32) as pen, \
            nc.Block() as block:
        ptab = k.ptab
        cache = d['cache_nsa_cmp_kv'].rearrange("n (q t) z g c -> q n (t z g c)", t=2)
        spare, spare2 = (flat(o[:, :, :]).bitcast(F32) for o in (k.oH, k.oL))
        pages = spare[:, 0:4096].rearrange("p (s n) -> p s n", s=8)
        xp = spare[:, 4096:4096 + 2 * (G * SEQ // 2 + PR)].rearrange("p (z n) -> p z n", z=2)
        hraw = spare2[0:DH, 0:2 * G * NBLK].rearrange("p (z g n) -> p z g n", z=2, g=G)
        hid = spare2[0:DH, 1200:1200 + 2 * G * NBLK].rearrange("p (z g n) -> p z g n", z=2, g=G)
        pos = spare2[0:DH, 2400:2402]

        def half_tiles(eng, a):
            with eng.Fori(0, NB // 2) as it:
                for s in range(8):
                    eng.wait_ge(page_turned, it * 8 + (s + 1))
                    page = eng.value_load(ptab[0:1, bass.ds(it * 16 + (2 * s + a), 1)], min_val=0, max_val=cache.shape[1] - 1)
                    eng.dma_start(pages[a * DH:(a + 1) * DH, s, :], cache[:, bass.ds(page, 1), :].rearrange("p o c -> p (o c)")).then_inc(page_in[a][s], 16)

        @block.sync
        def _(sp):
            for i in range(2):
                dn.load(sp, i, i, w_tile(d['w_in'], COL['cmp'] + i * P), first=True)
            half_tiles(sp, 0)
            sp.wait_ge(dn.lo, 2)
            nxt.load_ahead(sp)

        @block.gpsimd
        def _(pool):
            for z in range(2):
                pool.dma_start(pen[:, z, :, :], d['nsa_cmp_pe'].rearrange("(r t) z c -> z r t c", t=2)[z]).then_inc(w_in, 16)
                pool.dma_start(w1[:, z, :, :], d['nsa_cmp_w1'][z].rearrange("(r q) e -> q r e", q=P)).then_inc(w_in, 16)
                pool.dma_start(w2[:, z, :], d['nsa_cmp_w2'][z]).then_inc(w_in, 16)
            half_tiles(pool, 1)

        @block.tensor
        def _(pe):
            pe.sem_inc(page_turned, 8)
            pe.sem_inc(hid_done, 2)
            dn.multiply_all(pe, k.hH, k.hL)
            pe.wait_ge(dn.evacuated, 4)
            with pe.Fori(0, WAVES) as wv:
                for n in range(TILES):
                    s = n % 8
                    for a in range(2):
                        pe.wait_ge(page_in[a][s], wv * 32 + (n // 8 * 16 + 16))
                    m = n // 2
                    if n % 2 == 0:
                        for eng in range(2):
                            pe.wait_ge(tile_out[eng], wv * 16 + (2 * m + 2))
                    for tz in range(4):
                        ins = nc.tensor.transpose(k.ps[:, n % 4, tz * P:(tz + 1) * P], pages[:, s, tz * P:(tz + 1) * P], k.c('ident'))
                    ins.then_inc(page_turned, 1)
                pe.wait_ge(w_in, 96)
                pe.wait_ge(tile_out[0], wv * 16 + 20)
                pe.wait_ge(tile_out[1], wv * 16 + 20)
                pe.wait_ge(hid_out, wv * 2 + 2)
                for z in range(2):
                    for r in range(PR):
                        ins = nc.tensor.matmul(k.ps[0:DH, 4 + z, 0:G * WB], w1[:, z, r, :], x2[:, z, :, r::PR],
                                               start=(r == 0), stop=(r == PR - 1))
                    ins.then_inc(hid_done, 1)
            for z in range(2):
                ins = nc.tensor.transpose(k.ps[:, 6, z * PR:(z + 1) * PR], pen[:, z, :, :].rearrange("r t c -> r (t c)"), k.c('ident')[0:PR, 0:PR])
            ins.then_inc(pe_turned, 1)
            pe.wait_ge(pe_copied, 1)
            pe.wait_ge(prompt_copied, 4)
            pe.wait_ge(hid_out, 2 * WAVES + 2)
            for z in range(2):
                for r in range(PR):
                    ins = nc.tensor.matmul(k.ps[0:DH, 4 + z, 0:G * NCB + 1], w1[:, z, r, :], xp[:, z, r::PR],
                                           start=(r == 0), stop=(r == PR - 1))
                ins.then_inc(hid_done, 1)
            pe.wait_ge(gelu_done, 2)
            for g in range(G):
                ins = nc.tensor.matmul(k.ps[g * DH:(g + 1) * DH, 0, 0:NBLK], w2[:, 0, :], hid[:, 0, g, :], start=True, stop=True)
            ins.then_inc(out_done, 1)
            for s in range(NB + 1):
                for g in range(G):
                    o = s % 4 * P + g * DH
                    ins = nc.tensor.matmul(k.ps[0:NCB, 1 + s // 4, o:o + DH], hid[:, 1, g, s * NCB:(s + 1) * NCB], w2[:, 1, :],
                                           start=True, stop=True)
            ins.then_inc(out_done, 1)

        def tiles_out(eng, copy, wv, g):
            eng.wait_ge(hid_done, wv * 2 + 2)
            for m in range(TILES // 2):
                eng.wait_ge(page_turned, wv * TILES + (2 * m + 2 + 8))
                for t in range(2):
                    src = k.ps[g * DH:(g + 1) * DH, 2 * (m % 2):2 * (m % 2) + 2, t * 2 * P:(t + 1) * 2 * P]
                    copy(x2[t * DH:(t + 1) * DH, :, g, m * 2 * P:(m + 1) * 2 * P].rearrange("p z (b n) -> p z b n", b=2),
                         src.rearrange("p b (z n) -> p z b n", z=2)).then_inc(tile_out[g], 1)

        @block.scalar
        def _(act):
            dn.start_evac(act)
            act.sem_inc(hid_out, 2)
            act.sem_inc(tile_out[0], 4)
            for i in range(2):
                dn.split_hi(act, i, i, 0)
            for i in range(2):
                dn.wait_tile(act, i)
                nc.scalar.activation(cols3(cmpT[:, i, :]), dense_out(k.ps, i), ACT.Identity,
                                     bias=k.vec[:, VB_CMP + i:VB_CMP + i + 1], scale=1 / WS).then_inc(dn.evacuated, 1)
            with act.Fori(0, WAVES) as wv:
                tiles_out(act, nc.scalar.copy, wv, 0)
                for z in range(2):
                    act.wait_ge(hid_done, wv * 2 + (z + 3))
                    nc.scalar.copy(hraw[:, z, :, bass.ds(wv * WB, WB)], k.ps[0:DH, 4 + z, 0:G * WB].rearrange("p (g n) -> p g n", g=G)).then_inc(hid_out, 1)
            for z in range(2):
                act.wait_ge(hid_done, 2 + 2 * WAVES + z + 1)
                nc.scalar.copy(hraw[:, z, :, NB * NCB:], k.ps[0:DH, 4 + z, 0:G * NCB].rearrange("p (g n) -> p g n", g=G)).then_inc(copied, 1)
                nc.scalar.copy(pos[:, z:z + 1], k.ps[0:DH, 4 + z, G * NCB:G * NCB + 1]).then_inc(copied, 1)
            act.wait_ge(copied, 4)
            act.wait_ge(hid_out, 2 + 2 * WAVES)
            for z in range(2):
                nc.scalar.activation(hid[:, z], hraw[:, z], ACT.Gelu_apprx_tanh, bias=pos[:, z:z + 1]).then_inc(gelu_done, 1)
            act.wait_ge(out_done, 1)
            nc.scalar.copy(k.kcT[:, :, :].rearrange("p s n -> p (s n)"), k.ps[:, 0, 0:NBLK])
            act.wait_ge(dn.multiplied, 4)
            nxt.split_hi_ahead(act)

        @block.vector
        def _(dve):
            dve.sem_inc(tile_out[1], 4)
            for i in range(2):
                dn.split_lo(dve, i, i)
            dve.wait_ge(dn.evacuated, 4)
            for g in range(G):
                for t in range(2):
                    nc.vector.tensor_copy(xp[t * DH:(t + 1) * DH, :, g * SEQ // 2:(g + 1) * SEQ // 2],
                                          cmpT[g * DH:(g + 1) * DH, :, t:SEQ:2]).then_inc(prompt_copied, 1)
            with dve.Fori(0, WAVES) as wv:
                tiles_out(dve, nc.vector.tensor_copy, wv, 1)
            dve.wait_ge(pe_turned, 1)
            nc.vector.tensor_copy(xp[:, :, SEQ:], k.ps[:, 6, 0:2 * PR].rearrange("p (z l) -> p z l", z=2)).then_inc(pe_copied, 1)
            dve.wait_ge(out_done, 2)
            nc.vector.tensor_copy(k.vcN[:, 0:8, :], k.ps[0:NCB, 1:3, :].rearrange("p b (s n) -> p (b s) n", n=P))
            nc.vector.tensor_copy(k.vcN[:, 8, :], k.ps[0:NCB, 3, 0:P])
            dve.wait_ge(dn.multiplied, 4)
            nxt.split_lo_ahead(dve)


def project_nsa(k, dn):
    nc, d = k.nc, k.d
    cols = [COL['q'] + m * P for m in range(4)] + [COL['sel'], COL['sel'] + P, COL['win'], COL['win'] + P, COL['ngate']]
    n = len(cols)
    assert n == dn.n
    other, new_turned = k.sem("na_other"), k.sem("na_new")
    with nc.sbuf_tensor("vT", [P, 2, T], F32) as vT, nc.sbuf_tensor("gT", [24, T], F32) as gT, \
            nc.sbuf_tensor("nat", [P, 3, 768], F32) as nat:
        with nc.Block() as block:

            @block.sync
            def _(sp):
                for i in range(n):
                    dn.load(sp, i, i % 4, w_tile(d['w_in'], cols[i]), first=i < 4)
                for b in range(3):
                    key_pages(k, sp, b, 0, PAGES)
                    window_keys(k, sp, b)
                sp.dma_start(k.toep[:, :, :], bass.AP(tensor=k.skew.tensor, offset=P - 1,
                                                      ap=[[383, P], [384 * P, H], [1, 256]])).then_inc(other, 16)
                win_state = d['state_nsa_win_kv'].rearrange("b s z g c -> b (s z g c)")
                win_out = d['out_win_s'][0].rearrange("b s z g c -> b (s z g c)")
                sp.dma_start(win_out[:, 0:(WIN - NS) * 256], win_state[:, NS * 256:]).then_inc(other, 16)

            @block.scalar
            def _(act):
                dn.start_evac(act)
                dn.split_hi(act, 0, 0, 0)
                for i in range(n):
                    if i + 1 < n:
                        dn.split_hi(act, i + 1, (i + 1) % 4, (i + 1) // 4)
                    dn.wait_tile(act, i)
                    ps = dense_out(k.ps, i % 2)
                    if i < 4:
                        for u in range(2):
                            g, hh = i // 2, (2 * i + u) % HPG
                            r = slice(u * DH, (u + 1) * DH)
                            ins = nc.scalar.activation(cols3(k.qT[g * DH:(g + 1) * DH, hh, :]), ps[r], ACT.Identity,
                                                       bias=k.vec[r, V_BQ8 + i:V_BQ8 + i + 1], scale=DH ** -0.5 / WS)
                    elif i < 8:
                        out = (k.kT[:, 0, :], vT[:, 0, :], k.kT[:, 1, :], vT[:, 1, :])[i - 4]
                        b = VB_SEL + i - 4
                        ins = nc.scalar.activation(cols3(out), ps, ACT.Identity, bias=k.vec[:, b:b + 1], scale=1 / WS)
                    else:
                        ins = nc.scalar.activation(cols3(gT[:, :]), ps[0:24], ACT.Sigmoid, bias=k.vec[0:24, VB_NG:VB_NG + 1],
                                                   scale=1 / WS)
                    ins.then_inc(dn.evacuated, 1)

            @block.vector
            def _(dve):
                for i in range(n):
                    dn.split_lo(dve, i, i % 4)

            @block.tensor
            def _(pe):
                dn.multiply_all(pe, k.hH, k.hL)

        turned, first_out, second_out, vals_kept = k.sem("na_turned"), k.sem("na_out1"), k.sem("na_out2"), k.sem("na_kept")
        stored = [k.sem(f"na_stored{i}") for i in range(3)]
        with nc.Block() as block:
            rows = [P] * NT + [TS]
            outs = [(d['out_cmp_p'], d['out_cmp_s']), (d['out_sel_p'], d['out_sel_s']), (d['out_win_p'], d['out_win_s'])]

            def stores(t):
                if t == NT:
                    return [(outs[j][1][0], j) for j in range(3)]
                return [(outs[j][0][0, 0], j) for j in range(3) if j < 2 or t >= (SEQ - WIN) // P]

            @block.tensor
            def _(pe):
                for t in range(NT + 1):
                    m = rows[t]
                    if t >= 4:
                        pe.wait_ge(first_out, t - 3)
                        pe.wait_ge(second_out, t - 3)
                    for j, src in enumerate((k.cmpT[:, 0], k.cmpT[:, 1], k.kT[:, 0], vT[:, 0], k.kT[:, 1], vT[:, 1])):
                        nc.tensor.transpose(k.ps[0:m, 2 * (t % 4) + j // 4, (j % 4) * P:(j % 4 + 1) * P],
                                            src[:, t * P:t * P + m], k.c('ident'))
                    nc.tensor.transpose(k.ps[0:m, 2 * (t % 4) + 1, 256:280], gT[:, t * P:t * P + m],
                                        k.c('ident')[0:24, 0:24]).then_inc(turned, 1)
                pe.wait_ge(first_out, 8)
                pe.wait_ge(second_out, 8)
                for b in range(NB):
                    for z in range(2):
                        c = (2 * b + z) * P
                        ins = nc.tensor.transpose(k.ps[0:NS, 2 + c // 512, c % 512:c % 512 + P],
                                                  vT[:, z, SEQ + b * NS:SEQ + (b + 1) * NS], k.c('ident'))
                ins.then_inc(new_turned, 1)

            @block.scalar
            def _(act):
                for t in range(NT + 1):
                    act.wait_ge(turned, t + 1)
                    if t >= 3:
                        act.wait_ge(stored[t % 3], 16 * sum(len(stores(u)) for u in range(t % 3, t, 3)))
                        act.wait_ge(vals_kept, t - 2)
                    nc.scalar.copy(nat[0:rows[t], t % 3, 0:512], k.ps[0:rows[t], 2 * (t % 4), :]).then_inc(first_out, 1)

            @block.vector
            def _(dve):
                for t in range(NT + 1):
                    dve.wait_ge(turned, t + 1)
                    if t >= 3:
                        dve.wait_ge(stored[t % 3], 16 * sum(len(stores(u)) for u in range(t % 3, t, 3)))
                        dve.wait_ge(vals_kept, t - 2)
                    m, b = rows[t], 2 * (t % 4) + 1
                    nc.vector.tensor_copy(nat[0:m, t % 3, 512:768], k.ps[0:m, b, 0:256])
                    nc.vector.tensor_copy(k.gN[0:m, t, :], k.ps[0:m, b, 256:280]).then_inc(second_out, 1)
                dve.wait_ge(new_turned, 1)
                nc.vector.tensor_copy(k.vS[:, :, :, :].rearrange("t b z n -> t (b z n)"),
                                      k.ps[0:NS, 2:6, :].rearrange("t b n -> t (b n)"))

            @block.sync
            def _(sp):
                for t in range(NT + 1):
                    sp.wait_ge(first_out, t + 1)
                    sp.wait_ge(second_out, t + 1)
                    for out, j in stores(t):
                        src = nat[0:rows[t], t % 3, j * 256:(j + 1) * 256]
                        if t < NT:
                            r = t * P - (SEQ - WIN if j == 2 else 0)
                            sp.dma_start(out.rearrange("s z g c -> s (z g c)")[r:r + P], src).then_inc(stored[t % 3], 16)
                        elif j < 2:
                            sp.dma_start(out.rearrange("b s z g c -> (b s) (z g c)"), src).then_inc(stored[t % 3], 16)
                        else:
                            new = out.rearrange("b s z g c -> b s (z g c)")
                            for b in range(NB):
                                sp.dma_start(new[b, WIN - NS:WIN], nat[b * NS:(b + 1) * NS, t % 3, 512:768]).then_inc(other, 16)
                for r in range(3):
                    n_st = sum(len(stores(u)) - (u == NT) for u in range(r, NT + 1, 3))
                    sp.wait_ge(stored[r], 16 * n_st)
                sp.wait_ge(other, 16 * (2 + NB))

            @block.gpsimd
            def _(pool):
                for t in range(NT):
                    pool.wait_ge(first_out, t + 1)
                    pool.wait_ge(second_out, t + 1)
                    nc.gpsimd.tensor_copy(k.vN[:, t, 0, :], nat[:, t % 3, 384:512])
                    nc.gpsimd.tensor_copy(k.vN[:, t, 1, :], nat[:, t % 3, 640:768]).then_inc(vals_kept, 1)


def sample_keys(k, b):
    buf, o = ((k.oH, 0), (k.oH, 12 * P), (k.oL, 3700))[b % 3]
    return flat(buf[:, :, :]).bitcast(F32)[:, o:o + 12 * P].rearrange("p (j n) -> p j n", j=12)


def key_pages(k, eng, b, a0, a1):
    cache = k.d['cache_nsa_sel_kv'].rearrange("n p z g c -> p n z (g c)")
    with eng.Fori(a0, a1) as j:
        page = eng.value_load(k.ptab[0:1, bass.ds(j + b * PAGES, 1)], min_val=0, max_val=cache.shape[1] - 1)
        eng.dma_start(sample_keys(k, b)[:, bass.ds(j, 1), :].rearrange("p o n -> p (o n)"),
                      cache[:, bass.ds(page, 1), 0, :].rearrange("p o n -> p (o n)")).then_inc(k.key_in[b % 3], 16)


def window_keys(k, eng, b):
    state = k.d['state_nsa_win_kv'].rearrange("b (j p) z g c -> b z p j (g c)", p=P)
    eng.dma_start(sample_keys(k, b)[:, PAGES:12, :], state[b, 0]).then_inc(k.key_in[b % 3], 16)


def sample_attention(k):
    nc, d = k.nc, k.d
    HS = 4
    WT = WIN // P
    NK = PAST + NS
    names = ("q", "bias", "kturn", "kcopy", "score", "gate", "csoft", "imp", "sprep", "smax", "wprep",
             "wmax", "exp", "pturn", "pcopy", "o", "fac", "comb", "oturn", "page", "first", "cprep",
             "cturn", "ccopy", "khigh")
    s = {n: k.sem("sa_" + n) for n in names}
    key_in = k.key_in
    val_in = [k.sem(f"sa_val{i}") for i in range(2)]
    val_sync = [k.sem(f"sa_vals{i}") for i in range(2)]
    with ExitStack() as es:
        sb = lambda n, sh, t=F32: es.enter_context(nc.sbuf_tensor("sa" + n, sh, t))
        spare = flat(k.oH[:, :, :]).bitcast(F32)
        spare2 = flat(k.oL[:, :, :]).bitcast(F32)
        kT = spare[:, 3072:3072 + 3072].rearrange("p (u n) -> p u n", u=2)
        vals = sb("vals", [P, HS, 12, P])
        Ss = spare2[:, 0:NK]
        Ws = spare2[:, NK:NK + WIN + NS]
        Cs = spare2[:, 1600:1632]
        PT = spare2[:, 1632:1632 + 14 * P].rearrange("p (j n) -> p j n", j=14)
        comb = spare2[:, 3500:3628]
        qbd, bias = sb("qbd", [P, NB, 32]), sb("bias", [P, 132])
        st = sb("st", [P, 64])
        imp, drop = sb("imp", [P, 16]), sb("drop", [P, 32])
        ctab, xs = sb("ctab", [P, 24]), sb("xs", [P, 120])
        PTc = sb("PTc", [NCB, P])
        ptab = k.ptab
        cache = d['cache_nsa_sel_kv'].rearrange("n p z g c -> p n z (g c)")
        state = d['state_nsa_win_kv'].rearrange("b (j p) z g c -> b z p j (g c)", p=P)
        block = es.enter_context(nc.Block())
        NEG_C, NEG_S, NEG_W, SUM_C, SUM_S, SUM_W, F_C, F_S, F_W, G3, TMP, CSUM = 0, 1, 2, 3, 4, 5, 6, 7, 8, 9, 12, 14
        col = lambda c, w=1: st[:, c:c + w]

        KA, VA = 5, 2

        def val_pages(eng, b, a0, a1, arrived):
            with eng.Fori(a0, a1) as j:
                page = eng.value_load(ptab[0:1, bass.ds(j + b * PAGES, 1)], min_val=0, max_val=cache.shape[1] - 1)
                eng.dma_start(vals[:, b % HS, bass.ds(j, 1), :].rearrange("p o n -> p (o n)"),
                              cache[:, bass.ds(page, 1), 1, :].rearrange("p o n -> p (o n)")).then_inc(arrived[b // HS], 16)

        @block.sync
        def _(sp):
            for u in range(HS):
                sp.dma_start(bias[32 * u:32 * u + 32, :], bass.AP(tensor=k.skew.tensor, offset=P - 1,
                                                                   ap=[[384 * P, H], [383, NS], [1, 132]])).then_inc(s["bias"], 16)
            for b in range(NB):
                if b >= 3:
                    sp.wait_ge(s["kturn"], 3 * (b - 2))
                    key_pages(k, sp, b, 0, KA)
                if b < HS:
                    val_pages(sp, b, 0, VA, val_sync)
            sp.wait_ge(s["o"], 1)
            for b in range(HS, NB):
                val_pages(sp, b, 0, VA, val_sync)

        @block.gpsimd
        def _(pool):
            for b in range(NB):
                if b >= HS:
                    pool.wait_ge(s["o"], 1)
                val_pages(pool, b, VA, PAGES, val_in)
                pool.dma_start(vals[:, b % HS, PAGES:12, :], state[b, 1]).then_inc(val_in[b // HS], 16)

        BT, BS, BW, BX, BO = 0, 2, 4, 5, 7
        XC, XSN, XWN, XI, XG = 0, 32, 36, 64, 96

        @block.tensor
        def _(pe):
            pe.wait_ge(s["q"], 2)
            for hf in range(2):
                for u in range(HS):
                    b = hf * HS + u
                    pe.wait_ge(key_in[b % 3], 16 * 9 * (b // 3 + 1))
                    for q in range(3):
                        n = 3 * b + q
                        if n >= 2:
                            pe.wait_ge(s["kcopy"], n - 1)
                        for j in range(4):
                            ins = nc.tensor.transpose(k.ps[:, BT + n % 2, j * P:(j + 1) * P], sample_keys(k, b)[:, 4 * q + j, :],
                                                      k.c('ident'))
                        ins.then_inc(s["kturn"], 1)
                    if hf and u == 0:
                        pe.wait_ge(s["sprep"], 2 * hf)
                        pe.wait_ge(s["wprep"], 1)
                        pe.wait_ge(s["cprep"], 2 * hf)
                        pe.wait_ge(s["fac"], 1)
                    r = slice(32 * u, 32 * u + 32)
                    nc.tensor.matmul(k.ps[r, BX, XC:XC + NCB], qbd[:, b, :], k.kcT[:, b, :], start=True, stop=True)
                    new = slice(SEQ + b * NS, SEQ + (b + 1) * NS)
                    nc.tensor.matmul(k.ps[r, BX, XSN:XSN + NS], qbd[:, b, :], k.kT[:, 0, new], start=True, stop=True)
                    nc.tensor.matmul(k.ps[r, BX, XWN:XWN + NS], qbd[:, b, :], k.kT[:, 1, new], start=True, stop=True)
                    for q in range(3):
                        pe.wait_ge(s["kcopy"], 3 * b + q + 1)
                        ins = nc.tensor.matmul(k.ps[r, BS + q if q < 2 else BW, :], qbd[:, b, :], kT[:, b % 2, q * 512:(q + 1) * 512],
                                               start=True, stop=True)
                    ins.then_inc(s["score"], 1)
                nc.tensor.matmul(k.ps[:, BX, XG:XG + 24], k.c('tokrow', TS)[:, hf * P:(hf + 1) * P], k.gN[0:TS, NT, :],
                                 start=True, stop=True).then_inc(s["gate"], 1)
                pe.wait_ge(s["csoft"], hf + 1)
                nc.tensor.matmul(k.ps[:, BX, XI:XI + NCB], k.c('headsum'), Cs, start=True, stop=True).then_inc(s["imp"], 1)
                nc.tensor.transpose(k.ps[0:NCB, 6, 0:P], Cs, k.c('ident')).then_inc(s["cturn"], 1)
                pe.wait_ge(s["ccopy"], hf + 1)
                if hf:
                    pe.wait_ge(s["comb"], 1)
                for u in range(HS):
                    b = hf * HS + u
                    nc.tensor.matmul(k.ps[32 * u:32 * u + 32, BO, 0:P], PTc[:, 32 * u:32 * u + 32], k.vcN[:, b, :],
                                     start=True, stop=True)
                pe.wait_ge(s["kcopy"], 3 * (hf * HS + HS))
                for q in range(4):
                    pe.wait_ge(s["exp"], 3 * hf + (2 if q < 2 else 3))
                    n = 4 * hf + q
                    if n >= 2:
                        pe.wait_ge(s["pcopy"], n - 1)
                    if q < 3:
                        for j in range(4):
                            src = Ss[:, (4 * q + j) * P:(4 * q + j + 1) * P] if q < 2 else Ws[:, j * P:(j + 1) * P]
                            ins = nc.tensor.transpose(k.ps[:, BT + q % 2, j * P:(j + 1) * P], src, k.c('ident'))
                    else:
                        nc.tensor.transpose(k.ps[0:NS, BT + 1, 0:P], Ss[:, PAST:NK], k.c('ident'))
                        ins = nc.tensor.transpose(k.ps[0:NS, BT + 1, P:2 * P], Ws[:, WIN:WIN + NS], k.c('ident'))
                    ins.then_inc(s["pturn"], 1)
                pe.wait_ge(val_in[hf], 16 * (9 - VA) * HS)
                pe.wait_ge(val_sync[hf], 16 * VA * HS)
                pe.wait_ge(s["pcopy"], 4 * hf + 4)
                for u in range(HS):
                    b, r = hf * HS + u, slice(32 * u, 32 * u + 32)
                    for z, tiles in ((0, range(0, 8)), (1, range(8, 12))):
                        out = k.ps[r, BO, (z + 1) * P:(z + 2) * P]
                        for j in tiles:
                            nc.tensor.matmul(out, PT[:, j, r], vals[:, u, j, :], start=(j == tiles[0]), stop=False)
                        ins = nc.tensor.matmul(out, PT[0:NS, 12 + z, r], k.vS[:, b, z, :], start=False, stop=True)
                ins.then_inc(s["o"], 1)
                pe.wait_ge(s["comb"], hf + 1)
                nc.tensor.transpose(k.ps[:, 6, P:2 * P], comb, k.c('ident')).then_inc(s["oturn"], 1)

        @block.scalar
        def _(act):
            def other_keys(b):
                window_keys(k, act, b)
                key_pages(k, act, b, KA, PAGES)

            for hf in range(2):
                for b in range(hf * HS, hf * HS + HS):
                    for q in range(3):
                        act.wait_ge(s["kturn"], 3 * b + q + 1)
                        if b >= 2:
                            act.wait_ge(s["score"], b - 1)
                        nc.scalar.copy(kT[:, b % 2, q * 512:(q + 1) * 512], k.ps[:, BT + (3 * b + q) % 2, :]).then_inc(s["kcopy"], 1)
                    if b + 3 < NB:
                        other_keys(b + 3)
                act.wait_ge(s["cprep"], 2 * hf + 2)
                nc.scalar.activation(Cs, xs[:, XC:XC + NCB], ACT.Exp, bias=col(NEG_C), accum_out=col(SUM_C)).then_inc(s["exp"], 1)
                act.wait_ge(s["smax"], hf + 1)
                nc.scalar.activation(Ss, Ss, ACT.Exp, bias=col(NEG_S), accum_out=col(SUM_S)).then_inc(s["exp"], 1)
                act.wait_ge(s["wmax"], hf + 1)
                nc.scalar.activation(Ws, Ws, ACT.Exp, bias=col(NEG_W), accum_out=col(SUM_W)).then_inc(s["exp"], 1)
                for q in range(4):
                    act.wait_ge(s["pturn"], 4 * hf + q + 1)
                    if q < 3:
                        ins = nc.scalar.copy(PT[:, 4 * q:4 * q + 4, :].rearrange("p j n -> p (j n)"), k.ps[:, BT + q % 2, :])
                    else:
                        ins = nc.scalar.copy(PT[0:NS, 12:14, :].rearrange("p j n -> p (j n)"), k.ps[0:NS, BT + 1, 0:2 * P])
                    ins.then_inc(s["pcopy"], 1)

        @block.vector
        def _(dve):
            tt, ts, stt, red = nc.vector.tensor_tensor, nc.vector.tensor_scalar, nc.vector.scalar_tensor_tensor, nc.vector.tensor_reduce
            nc.vector.memset(qbd[:, :, :], 0.0).then_inc(s["first"], 1)
            dve.wait_ge(s["first"], 1)
            for g in range(G):
                r = slice(g * DH, (g + 1) * DH)
                for hh in range(HPG):
                    ins = nc.vector.tensor_copy(qbd[r, :, (g * HPG + hh) * NS:(g * HPG + hh + 1) * NS],
                                                k.qT[r, hh, SEQ:].rearrange("p (b t) -> p b t", b=NB))
                ins.then_inc(s["q"], 1)
            half = [slice(g * DH, (g + 1) * DH) for g in range(G)]
            for g in range(G):
                for u in range(G):
                    nc.vector.tensor_copy(k.kH[half[u], g], k.kT[half[g], :, 0:SEQ]).then_inc(s["khigh"], 1)
                    nc.vector.tensor_copy(k.kcH[half[u], g, :], k.kcT[half[g], 8, :]).then_inc(s["khigh"], 1)
            dve.wait_ge(s["khigh"], 8)
            for g in range(G):
                for u in range(G):
                    tt(k.kL[half[u], g], k.kT[half[g], :, 0:SEQ], k.kH[half[g], g], ALU.subtract)
                    tt(k.kcL[half[u], g, :], k.kcT[half[g], 8, :], k.kcH[half[g], g, :], ALU.subtract)
            dve.wait_ge(s["bias"], 64)
            step = [0]

            def done(ins):
                step[0] += 1
                ins.then_inc(s["page"], 1)
                dve.wait_ge(s["page"], step[0])

            for hf in range(2):
                dve.wait_ge(s["score"], HS * (hf + 1))
                dve.wait_ge(s["gate"], hf + 1)
                nc.vector.tensor_copy(xs[:, XG:XG + 24], k.ps[:, BX, XG:XG + 24])
                done(nc.vector.tensor_copy(xs[:, 0:40], k.ps[:, BX, 0:40]))
                c4 = xs[:, XC + NCB - 4:XC + NCB]
                tt(c4, c4, bias[:, CB - 1:P:CB], ALU.add).then_inc(s["cprep"], 1)
                dve.wait_ge(s["cprep"], 2 * hf + 1)
                red(col(NEG_C), xs[:, XC:XC + NCB], AX, ALU.max, negate=True).then_inc(s["cprep"], 1)
                if hf:
                    dve.wait_ge(s["pcopy"], 4)
                done(nc.vector.tensor_copy(Ws[:, 0:WIN], k.ps[:, BW, :]))
                done(tt(Ws[:, 0:NS], Ws[:, 0:NS], k.c('winmask_s'), ALU.add))
                done(tt(Ws[:, WIN - P:WIN], Ws[:, WIN - P:WIN], bias[:, 0:P], ALU.add))
                done(tt(Ws[:, WIN:WIN + NS], xs[:, XWN:XWN + NS], bias[:, P:P + NS], ALU.add))
                ins = red(col(NEG_W), Ws, AX, ALU.max, negate=True)
                ins.then_inc(s["wmax"], 1)
                dve.sem_inc(s["wprep"], 1)
                dve.wait_ge(s["exp"], 3 * hf + 1)
                done(nc.vector.reciprocal(col(CSUM), col(SUM_C)))
                ts(Cs, Cs, col(CSUM), None, ALU.mult).then_inc(s["csoft"], 1)
                dve.wait_ge(s["imp"], hf + 1)
                done(red(imp[:, :], k.ps[:, BX, XI:XI + NCB].rearrange("p (b c) -> p b c", c=2), AX, ALU.add))
                done(red(col(TMP), imp[:, 1:15], AX, ALU.min))
                done(stt(drop[:, 1:15], imp[:, 1:15], col(TMP), k.c('blk')[:, 1:15], ALU.is_equal, ALU.mult))
                done(red(col(TMP), drop[:, 1:15], AX, ALU.max))
                done(ts(drop[:, 16:32], k.c('blk'), col(TMP), -BIG, ALU.is_equal, ALU.mult))
                done(tt(Ss[:, 0:PAST].rearrange("p (b n) -> p b n", n=SB), k.ps[:, BS:BS + 2, :].rearrange("p u (b n) -> p (u b) n", n=SB),
                        drop[:, 16:32].unsqueeze(2).broadcast_to([P, 16, SB]), ALU.add))
                done(tt(Ss[:, PAST - P:PAST], Ss[:, PAST - P:PAST], bias[:, 0:P], ALU.add))
                done(tt(Ss[:, PAST:NK], xs[:, XSN:XSN + NS], bias[:, P:P + NS], ALU.add))
                dve.sem_inc(s["sprep"], 2)
                red(col(NEG_S), Ss, AX, ALU.max, negate=True).then_inc(s["smax"], 1)
                dve.wait_ge(s["cturn"], hf + 1)
                nc.vector.tensor_copy(PTc[:, :], k.ps[0:NCB, 6, 0:P]).then_inc(s["ccopy"], 1)
                done(tt(ctab[:, :], xs[:, XG:XG + 24], k.c('headhot'), ALU.mult))
                done(red(col(G3, 3), ctab[:, :].rearrange("p (z h) -> p z h", z=3), AX, ALU.add))
                dve.wait_ge(s["exp"], 3 * hf + 3)
                done(nc.vector.reciprocal(col(TMP, 2), col(SUM_S, 2)))
                tt(col(F_S, 2), col(G3 + 1, 2), col(TMP, 2), ALU.mult).then_inc(s["fac"], 1)
                dve.wait_ge(s["fac"], hf + 1)
                dve.wait_ge(s["o"], hf + 1)
                done(ts(comb, k.ps[:, BO, 0:P], col(G3), None, ALU.mult))
                done(stt(comb, k.ps[:, BO, P:2 * P], col(F_S), comb, ALU.mult, ALU.add))
                stt(comb, k.ps[:, BO, 2 * P:3 * P], col(F_W), comb, ALU.mult, ALU.add).then_inc(s["comb"], 1)
                dve.wait_ge(s["oturn"], hf + 1)
                for h in range(H):
                    g, m, odd = h // HPG, h // 2, h % 2
                    nc.vector.tensor_copy(k.oTs[odd * DH:(odd + 1) * DH, m, hf * 16:hf * 16 + 16].rearrange("p (u t) -> p u t", u=HS),
                                          k.ps[g * DH:(g + 1) * DH, 6, P:2 * P].rearrange("p (u r) -> p u r", u=HS)[:, :, h * NS:(h + 1) * NS])


def prompt_attention(k, nxt):
    nc, d = k.nc, k.d
    C, S, W = range(3)
    jobs = []
    for i in range(NT):
        for g in range(G):
            for kind in (C, S, W):
                first = {C: 0, S: 0, W: max(0, i - WIN // P)}[kind]
                jobs.append((i, g, kind, [0] if kind == C else list(range(first, i + 1))))
    NJ = len(jobs)
    groups, count = [], [0, 0]
    for i, g, kind, tiles in jobs:
        mine = []
        for a in range(0, len(tiles), 4):
            bank = (count[0] + count[1]) % 2
            mine.append((bank, count[bank], count[0] + count[1], tiles[a:a + 4], a))
            count[bank] += 1
        groups.append(mine)
    NG = count[0] + count[1]
    STEPS = 2 * NJ + NJ // 3
    spare = flat(k.oL[:, :, :]).bitcast(F32)
    prob = spare[:, 0:3 * SEQ].rearrange("p (u n) -> p u n", u=3)
    probT = spare[:, 3 * SEQ:6 * SEQ].rearrange("p (u t n) -> p u t n", u=3, t=NT)
    kH, kL, kcH, kcL = k.kH, k.kL, k.kcH, k.kcL
    qP = flat(k.oH[:, :, :])[:, 0:H * SEQ].rearrange("p (h t) -> p h t", h=H)
    with nc.sbuf_tensor("pastat", [P, 3, 12], F32) as stat, \
            nc.sbuf_tensor("oacc", [P, NT, R], F32) as oacc:
        scored, maxed, exped = k.sem("pa_scored"), k.sem("pa_maxed"), k.sem("pa_exped")
        turned, out_done, combined, step = k.sem("pa_turned"), k.sem("pa_o"), k.sem("pa_comb"), k.sem("pa_step")
        out = [k.sem("pa_out0"), k.sem("pa_out1")]
        C_SCORED, C_EXPED, C_TURNED, C_OUT, C_O, C_COMB = 2, 2, 5, 1, 3, 2
        NEG, SUM, FAC = range(3)

        def width(j):
            i, g, kind, tiles = jobs[j]
            return 4 * (i + 1) if kind == C else P * len(tiles)

        def scores(j):
            b = 2 * (j % 2)
            w = width(j)
            return k.ps[:, b:b + 2, :].rearrange("p b n -> p (b n)")[:, 0:w]

        def turned_rows(j):
            return width(j) if jobs[j][2] == C else P

        q_high = [k.sem(f"pa_qhigh{g}") for g in range(G)]
        q_low = [k.sem(f"pa_qlow{g}") for g in range(G)]
        q_made = k.sem("pa_qmade")
        with nc.Block() as block:
            half = [slice(g * DH, (g + 1) * DH) for g in range(G)]

            def high(copy, g, hh):
                return copy(qP[half[g], g * HPG + hh, :], k.qT[half[g], hh, 0:SEQ])

            def low(eng, g, hh):
                return eng.tensor_tensor(qP[half[1 - g], g * HPG + hh, :], k.qT[half[g], hh, 0:SEQ], qP[half[g], g * HPG + hh, :], ALU.subtract)

            @block.gpsimd
            def _(pool):
                pool.wait_ge(q_high[0], 1)
                low(nc.gpsimd, 0, 0).then_inc(q_low[0], 1)
                pool.sem_inc(q_made, 1)
                for hh in range(1, HPG):
                    for g in range(G):
                        high(nc.gpsimd.tensor_copy, g, hh).then_inc(q_made, 1)
                    pool.wait_ge(q_made, 4 * hh - 1)
                    for g in range(G):
                        low(nc.gpsimd, g, hh).then_inc(q_made, 1)

            @block.tensor
            def _(pe):
                pe.sem_inc(scored, C_SCORED)
                pe.sem_inc(turned, C_TURNED)
                pe.sem_inc(out_done, C_O)

                def score(hh, j):
                    i, g, kind, tiles = jobs[j]
                    pe.wait_ge(exped, hh * NJ + (j - 1 + C_EXPED))
                    w = width(j)
                    for a in range(0, w, 512):
                        n = min(512, w - a)
                        q = qP[:, bass.ds(hh + g * HPG, 1), i * P:(i + 1) * P].rearrange("p o n -> p (o n)")
                        for part, (whole, blocks) in enumerate(((kH, kcH), (kL, kcL))):
                            keys = blocks[:, g, 0:w] if kind == C else whole[:, g, kind - 1, tiles[0] * P + a:tiles[0] * P + a + n]
                            ins = nc.tensor.matmul(scores(j)[:, a:a + n], q, keys, start=(part == 0), stop=(part == 1))
                    ins.then_inc(scored, 1)

                def turn(hh, j):
                    pe.wait_ge(exped, hh * NJ + (j + 1 + C_EXPED))
                    n = turned_rows(j)
                    for bank, nth, _, tiles, a in groups[j]:
                        pe.wait_ge(out[bank], hh * count[bank] + (nth - 1 + 1 + C_OUT))
                        for u in range(len(tiles)):
                            ins = nc.tensor.transpose(k.ps[0:n, 4 + bank, u * P:(u + 1) * P],
                                                      prob[:, j % 3, (a + u) * P:(a + u) * P + n], k.c('ident'))
                        ins.then_inc(turned, 1)

                def values(hh, j):
                    i, g, kind, tiles = jobs[j]
                    for bank, nth, _, _, _ in groups[j]:
                        pe.wait_ge(out[bank], hh * count[bank] + (nth + 1 + C_OUT))
                    pe.wait_ge(combined, hh * NJ + (j - 1 + C_COMB))
                    n = turned_rows(j)
                    for u, t in enumerate(tiles):
                        v = k.vcN[0:n, 8, g * DH:(g + 1) * DH] if kind == C else k.vN[:, t, kind - 1, g * DH:(g + 1) * DH]
                        ins = nc.tensor.matmul(k.ps[:, 6 + j % 2, 0:DH], probT[0:n, j % 3, u, :], v,
                                               start=(u == 0), stop=(u == len(tiles) - 1))
                    ins.then_inc(out_done, 1)

                for g in range(G):
                    pe.wait_ge(q_low[g], 1)
                with pe.Fori(0, HPG) as hh:
                    pe.wait_ge(q_made, hh * 4 + 1)
                    for j in range(NJ + 4):
                        if j < NJ:
                            score(hh, j)
                        if j >= 4:
                            values(hh, j - 4)
                        if 2 <= j < NJ + 2:
                            turn(hh, j - 2)

            def turned_out(eng, copy, hh, j):
                n = turned_rows(j)
                for bank, nth, order, tiles, a in groups[j]:
                    eng.wait_ge(turned, hh * NG + (order + 1 + C_TURNED))
                    eng.wait_ge(out_done, hh * NJ + (j - 2 + C_O))
                    w = len(tiles) * P
                    copy(probT[0:n, j % 3, a:a + len(tiles), :].rearrange("p u n -> p (u n)"),
                         k.ps[0:n, 4 + bank, 0:w]).then_inc(out[bank], 1)

            @block.scalar
            def _(act):
                high(nc.scalar.copy, 0, 0).then_inc(q_high[0], 1)
                act.sem_inc(exped, C_EXPED)
                act.sem_inc(out[0], C_OUT)
                act.sem_inc(out[1], C_OUT)
                with act.Fori(0, HPG) as hh:
                    for j in range(NJ + 2):
                        if j >= 2:
                            turned_out(act, nc.scalar.copy, hh, j - 2)
                        if j < NJ:
                            act.wait_ge(maxed, hh * NJ + (j + 1))
                            before = groups[j - 3][-1][2] + 1 - (0 if j >= 3 else NG)
                            act.wait_ge(turned, hh * NG + (before + C_TURNED))
                            nc.scalar.activation(prob[:, j % 3, 0:width(j)], scores(j), ACT.Exp, bias=stat[:, NEG, j % 12:j % 12 + 1],
                                                 accum_out=stat[:, SUM, j % 12:j % 12 + 1]).then_inc(exped, 1)

            @block.vector
            def _(dve):
                high(nc.vector.tensor_copy, 1, 0).then_inc(q_high[1], 1)
                dve.wait_ge(q_high[1], 1)
                low(nc.vector, 1, 0).then_inc(q_low[1], 1)
                dve.sem_inc(combined, C_COMB)
                done = [0]

                def settle(hh, ins):
                    done[0] += 1
                    ins.then_inc(step, 1)
                    dve.wait_ge(step, hh * STEPS + done[0])

                def maximum(hh, j):
                    i, g, kind, tiles = jobs[j]
                    dve.wait_ge(scored, hh * NJ + (j + 1 + C_SCORED))
                    sc, w = scores(j), width(j)
                    near = min(2, i + 1)
                    bias = k.toep[:, bass.ds(hh + g * HPG, 1), (2 - near) * P:2 * P].rearrange("p o n -> p (o n)")
                    if kind == C:
                        part = sc[:, w - 4 * near:w]
                        ins = nc.vector.tensor_tensor(part, part, bias[:, CB - 1::CB], ALU.add)
                    else:
                        if kind == W and len(tiles) == WIN // P + 1:
                            nc.vector.tensor_tensor(sc[:, 0:P], sc[:, 0:P], k.c('winmask'), ALU.add)
                        part = sc[:, w - near * P:w]
                        ins = nc.vector.tensor_tensor(part, part, bias, ALU.add)
                    settle(hh, ins)
                    neg = stat[:, NEG, j % 12:j % 12 + 1]
                    ins = nc.vector.tensor_reduce(neg, sc, AX, ALU.max, negate=True)
                    if kind == C:
                        settle(hh, ins)
                        ins = nc.vector.tensor_scalar(neg, neg, 1e20, None, ALU.min)
                    ins.then_inc(maxed, 1)

                def factors(hh, j):
                    i, g = jobs[j][0], jobs[j][1]
                    dve.wait_ge(exped, hh * NJ + (j + 1 + C_EXPED))
                    three = slice((j - 2) % 12, (j - 2) % 12 + 3)
                    fac = stat[:, FAC, three]
                    settle(hh, nc.vector.tensor_scalar(fac, stat[:, SUM, three], 1e-30, None, ALU.max))
                    settle(hh, nc.vector.reciprocal(fac, fac))
                    gate = k.gN[:, i, :].rearrange("p (z h) -> p z h", z=3)[:, :, bass.ds(hh + g * HPG, 1)].rearrange("p z o -> p (z o)")
                    settle(hh, nc.vector.tensor_tensor(fac, gate, fac, ALU.mult))

                def combine(hh, j):
                    i, g, kind, tiles = jobs[j]
                    dve.wait_ge(out_done, hh * NJ + (j + 1 + C_O))
                    o = k.ps[:, 6 + j % 2, 0:DH]
                    fac = stat[:, FAC, j % 12:j % 12 + 1]
                    acc = oacc[:, i, bass.ds((hh + g * HPG) * DH, DH)]
                    if kind == C:
                        ins = nc.vector.tensor_scalar(acc, o, fac, None, ALU.mult)
                    else:
                        dve.wait_ge(combined, hh * NJ + (j + C_COMB))
                        ins = nc.vector.scalar_tensor_tensor(acc, o, fac, acc, ALU.mult, ALU.add)
                    ins.then_inc(combined, 1)

                with dve.Fori(0, HPG) as hh:
                    for j in range(NJ + 5):
                        if j >= 5:
                            combine(hh, j - 5)
                        if j % 3 == 1 and 1 < j < NJ + 2:
                            factors(hh, j - 2)
                        if j < NJ:
                            maximum(hh, j)
                    assert done[0] == STEPS

        t_turned, t_hi, t_lo = k.sem("pt_turned"), k.sem("pt_hi"), k.sem("pt_lo")
        with nc.Block() as block:

            @block.sync
            def _(sp):
                nxt.load_ahead(sp)

            @block.tensor
            def _(pe):
                for t in range(NT):
                    if t >= 4:
                        pe.wait_ge(t_lo, t - 3)
                    for m in range(4):
                        ins = nc.tensor.transpose(k.ps[:, t % 4, m * P:(m + 1) * P], oacc[:, t, m * P:(m + 1) * P], k.c('ident'))
                    ins.then_inc(t_turned, 1)

            def tile(buf, t):
                return buf[:, 0:4, t * P:(t + 1) * P]

            def bank(t):
                return k.ps[:, t % 4, :].rearrange("p (m n) -> p m n", m=4)

            @block.scalar
            def _(act):
                for t in range(NT):
                    act.wait_ge(t_turned, t + 1)
                    nc.scalar.copy(tile(k.oH, t), bank(t)).then_inc(t_hi, 1)
                nc.scalar.copy(k.oH[:, 0:4, SEQ:], k.oTs[:, :, :]).then_inc(t_hi, 1)
                nxt.split_hi_ahead(act)

            @block.vector
            def _(dve):
                for t in range(NT):
                    dve.wait_ge(t_hi, t + 1)
                    nc.vector.tensor_tensor(tile(k.oL, t), bank(t), tile(k.oH, t), ALU.subtract).then_inc(t_lo, 1)
                dve.wait_ge(t_hi, NT + 1)
                nc.vector.tensor_tensor(k.oL[:, 0:4, SEQ:], k.oTs[:, :, :], k.oH[:, 0:4, SEQ:], ALU.subtract)
                nxt.split_lo_ahead(dve)


def lru(k, dn, nxt):
    nc, d = k.nc, k.d
    MT = R // P
    CWD = 4
    n = 2 * MT
    assert n == dn.n
    s = {x: k.sem("lr_" + x) for x in ("in", "cleared", "gw", "sturn", "conv", "gate", "gsig", "expo", "tanh", "quot", "root",
             "beta", "prod", "hi", "lam", "lexp", "step", "pack", "pturn", "pout", "stored", "taps")}
    with ExitStack() as es:
        sb = lambda nm, sh, t=F32: es.enter_context(nc.sbuf_tensor("lr" + nm, sh, t))
        xin, xs = sb("xin", [P, MT, 3 + SEQ]), sb("xs", [P, MT, NB, 3 + NS])
        gg, xc = sb("gg", [P, MT, T]), sb("xc", [P, MT, T])
        rg, ig = sb("rg", [P, MT, T]), sb("ig", [P, MT, T])
        gw = sb("gw", [P, 2, MT, P])
        srow, h0, lam = sb("srow", [32, R]), sb("h0", [P, MT, NB]), sb("lam", [P, 6, MT])
        a5, b5, h5 = sb("a5", [P, NB, NS + 1]), sb("b5", [P, NB, NS + 1]), sb("h5", [P, MT, NB, NS + 1])
        pack, prow = sb("pack", [P, MT, 36]), sb("prow", [36, R])
        vec = lambda c: k.vec[:, c:c + 1]
        with nc.Block() as block:

            @block.sync
            def _(sp):
                sp.dma_start(srow[0:24, :], d['state_lru_conv'].rearrange("b j c -> (b j) c")).then_inc(s["in"], 16)
                sp.dma_start(srow[24:32, :], d['state_lru_h']).then_inc(s["in"], 16)
                for i in range(n):
                    dn.load(sp, i, i % 4, w_tile(d['w_in'], COL['lg' if i >= MT else 'lx'] + i % MT * P), first=i < 4)
                sp.wait_ge(s["cleared"], 1)
                for z in range(2):
                    for u in range(2):
                        r = slice(u * 64, (u + 1) * 64)
                        sp.dma_start(gw[r, z, :, r], d['lru_gate_w'][z].rearrange("(m u) c e -> u c m e", u=2)[u]).then_inc(s["gw"], 16)
                sp.wait_ge(dn.lo, n)
                nxt.load_ahead(sp)
                sp.wait_ge(s["pout"], 1)
                for rows, out in ((prow[0:3, :], d['out_conv_p'][0, 0]), (prow[3:27, :], d['out_conv_s'][0].rearrange("b j c -> (b j) c")),
                                  (prow[27:28, :], d['out_h_p'][0]), (prow[28:36, :], d['out_h_s'][0])):
                    sp.dma_start(out, rows).then_inc(s["stored"], 16)
                sp.wait_ge(s["stored"], 64)

            @block.scalar
            def _(act):
                def gates(m):
                    for z in range(2):
                        for c in range(3):
                            u = 6 * m + 3 * z + c
                            act.wait_ge(s["gate"], u + 1)
                            nc.scalar.activation((rg, ig)[z][:, m, c * CH:(c + 1) * CH], k.ps[:, 6 + u % 2, 0:CH], ACT.Sigmoid,
                                                 bias=vec(V_LGB + 4 * z + m)).then_inc(s["gsig"], 1)

                def decay(m):
                    act.wait_ge(s["lam"], 2)
                    act.wait_ge(s["beta"], m + 1)
                    act.wait_ge(s["gsig"], 6 * m + 3)
                    nc.scalar.activation(xc[:, m, :], rg[:, m, :], ACT.Exp, scale=vec(V_LRC + m)).then_inc(s["expo"], 1)
                    nc.scalar.activation(rg[:, m, :], rg[:, m, :], ACT.Tanh, scale=lam[:, 0, m:m + 1]).then_inc(s["tanh"], 1)

                dn.start_evac(act)
                dn.split_hi(act, 0, 0, 0)
                for i in range(n):
                    if i + 1 < n:
                        dn.split_hi(act, i + 1, (i + 1) % 4, (i + 1) // 4)
                    if i == 0:
                        act.wait_ge(s["lam"], 1)
                        nc.scalar.activation(lam[:, 2, :], lam[:, 0, :], ACT.Exp, scale=-1.0).then_inc(s["lexp"], 1)
                    if i >= MT + 2:
                        decay(2 * (i - MT - 2))
                        decay(2 * (i - MT - 2) + 1)
                    if i == n - 1:
                        for m in range(MT):
                            act.wait_ge(s["quot"], m + 1)
                            nc.scalar.activation(rg[:, m, :], rg[:, m, :], ACT.Sqrt).then_inc(s["root"], 1)
                    dn.wait_tile(act, i)
                    m = i % MT
                    if i >= MT:
                        nc.scalar.activation(cols3(gg[:, m, :]), dense_out(k.ps, i % 2), ACT.Gelu_apprx_tanh,
                                             bias=k.vec[:, VB_LG + m:VB_LG + m + 1], scale=1 / WS).then_inc(dn.evacuated, 1)
                    else:
                        nc.scalar.activation(cols3(rg[:, m, :]), dense_out(k.ps, i % 2), ACT.Identity,
                                             bias=k.vec[:, VB_LX + m:VB_LX + m + 1], scale=1 / WS).then_inc(dn.evacuated, 1)
                    if 2 <= i < MT + 2:
                        gates(i - 2)
                nxt.split_hi_ahead(act)
                for m in range(MT):
                    act.wait_ge(s["prod"], m + 1)
                    nc.scalar.copy(k.oH[:, 4 + m, :], gg[:, m, :]).then_inc(s["hi"], 1)

            @block.vector
            def _(dve):
                tt, ts, stt = nc.vector.tensor_tensor, nc.vector.tensor_scalar, nc.vector.scalar_tensor_tensor
                step = [0]

                def settle(ins):
                    step[0] += 1
                    ins.then_inc(s["step"], 1)
                    dve.wait_ge(s["step"], step[0])

                def states_in():
                    dve.wait_ge(s["sturn"], 1)
                    states = k.ps[:, 7, 0:P].rearrange("p (m r) -> p m r", m=MT)
                    nc.vector.tensor_copy(h0[:, :, :], states[:, :, 24:32])
                    for m in range(MT):
                        ins = nc.vector.tensor_copy(xs[:, m, :, 0:3], states[:, m, 0:24].rearrange("p (b j) -> p b j", b=NB))
                    settle(ins)

                def convolve(m):
                    dve.wait_ge(dn.evacuated, m + 1 + 2)
                    nc.vector.tensor_copy(xin[:, m, 3:], rg[:, m, 0:SEQ])
                    settle(nc.vector.tensor_copy(xs[:, m, :, 3:], rg[:, m, SEQ:].rearrange("p (b t) -> p b t", b=NB)))
                    xcs = xc[:, m, SEQ:].rearrange("p (b t) -> p b t", b=NB)
                    ts(xc[:, m, 0:SEQ], xin[:, m, 0:SEQ], vec(V_CW + m), vec(V_CB + m), ALU.mult, ALU.add).then_inc(s["taps"], 1)
                    ts(xcs, xs[:, m, :, 0:NS], vec(V_CW + m), vec(V_CB + m), ALU.mult, ALU.add).then_inc(s["taps"], 1)
                    for j in range(1, CWD):
                        dve.wait_ge(s["taps"], 8 * m + 2 * j)
                        ins = stt(xc[:, m, 0:SEQ], xin[:, m, j:j + SEQ], vec(V_CW + 4 * j + m), xc[:, m, 0:SEQ], ALU.mult, ALU.add)
                        ins.then_inc(s["taps"], 1)
                        ins = stt(xcs, xs[:, m, :, j:j + NS], vec(V_CW + 4 * j + m), xcs, ALU.mult, ALU.add)
                        ins.then_inc(s["taps"], 1)
                    dve.wait_ge(s["taps"], 8 * m + 8)
                    nc.vector.tensor_copy(pack[:, m, 0:3], xin[:, m, SEQ:SEQ + 3])
                    ins = nc.vector.tensor_copy(pack[:, m, 3:27].rearrange("p (b j) -> p b j", b=NB), xs[:, m, :, NS:NS + 3])
                    ins.then_inc(s["conv"], 1)

                def gated(m):
                    dve.wait_ge(s["gsig"], 6 * m + 6)
                    tt(ig[:, m, :], ig[:, m, :], xc[:, m, :], ALU.mult).then_inc(s["beta"], 1)

                def one_less_square(m):
                    dve.wait_ge(s["expo"], m + 1)
                    dve.wait_ge(s["tanh"], m + 1)
                    sq, sqs = xin[:, m, 0:SEQ], h5[:, m, :, 0:NS]
                    a_s, us = (v[:, m, SEQ:].rearrange("p (b t) -> p b t", b=NB) for v in (xc, rg))
                    tt(sq, xc[:, m, 0:SEQ], xc[:, m, 0:SEQ], ALU.mult)
                    settle(tt(sqs, a_s, a_s, ALU.mult))
                    stt(rg[:, m, 0:SEQ], sq, 1.0, rg[:, m, 0:SEQ], ALU.add, ALU.mult)
                    stt(us, sqs, 1.0, us, ALU.add, ALU.mult).then_inc(s["quot"], 1)

                dn.split_lo(dve, 0, 0)
                dn.split_lo(dve, 1, 1)
                dve.wait_ge(s["cleared"], 2)
                states_in()
                LV = k.vec[:, V_LAM:V_LAM + MT]
                settle(ts(lam[:, 0, :], LV, -1.0, None, ALU.mult))
                settle(tt(lam[:, 0, :], LV, lam[:, 0, :], ALU.max))
                ts(lam[:, 1, :], LV, -1.0, 0.0, ALU.mult, ALU.max).then_inc(s["lam"], 1)
                dve.wait_ge(s["lexp"], 1)
                z, w, w2, poly = lam[:, 2, :], lam[:, 3, :], lam[:, 4, :], lam[:, 5, :]
                settle(ts(w, z, 2.0, None, ALU.add))
                settle(nc.vector.reciprocal(w, w))
                settle(tt(w, w, z, ALU.mult))
                settle(tt(w2, w, w, ALU.mult))
                settle(ts(poly, w2, 1 / 17, 1 / 15, ALU.mult, ALU.add))
                for q in (13, 11, 9, 7, 5, 3, 1):
                    settle(tt(poly, poly, w2, ALU.mult))
                    settle(ts(poly, poly, 1 / q, None, ALU.add))
                settle(tt(poly, poly, w, ALU.mult))
                settle(stt(poly, poly, 2.0, lam[:, 1, :], ALU.mult, ALU.add))
                settle(ts(k.vec[:, V_LRC:V_LRC + MT], poly, -8.0, None, ALU.mult))
                ts(lam[:, 0, :], poly, 8.0, None, ALU.mult).then_inc(s["lam"], 1)

                for i in range(2, n):
                    dn.split_lo(dve, i, i % 4)
                    if i < MT + 2:
                        convolve(i - 2)
                    else:
                        gated(2 * (i - MT - 2))
                        gated(2 * (i - MT - 2) + 1)
                for m in range(MT):
                    one_less_square(m)
                settle(nc.vector.memset(a5[:, :, 0:1], 0.0))
                for m in range(MT):
                    dve.wait_ge(s["root"], m + 1)
                    settle(tt(ig[:, m, :], ig[:, m, :], rg[:, m, :], ALU.mult))
                    nc.vector.tensor_copy(b5[:, :, 0:1], h0[:, m, :].unsqueeze(2))
                    nc.vector.tensor_copy(b5[:, :, 1:], ig[:, m, SEQ:].rearrange("p (b t) -> p b t", b=NB))
                    settle(nc.vector.tensor_copy(a5[:, :, 1:], xc[:, m, SEQ:].rearrange("p (b t) -> p b t", b=NB)))
                    nc.vector.tensor_tensor_scan(rg[:, m, 0:SEQ], xc[:, m, 0:SEQ], ig[:, m, 0:SEQ], 0.0, ALU.mult, ALU.add)
                    settle(nc.vector.tensor_tensor_scan(h5[:, m, :, :].rearrange("p b t -> p (b t)"), a5[:, :, :].rearrange("p b t -> p (b t)"),
                                                        b5[:, :, :].rearrange("p b t -> p (b t)"), 0.0, ALU.mult, ALU.add))
                    nc.vector.tensor_copy(pack[:, m, 27:28], rg[:, m, SEQ - 1:SEQ])
                    nc.vector.tensor_copy(pack[:, m, 28:36], h5[:, m, :, NS]).then_inc(s["pack"], 1)
                    dve.wait_ge(dn.evacuated, MT + m + 1 + 2)
                    tt(gg[:, m, 0:SEQ], gg[:, m, 0:SEQ], rg[:, m, 0:SEQ], ALU.mult)
                    gs = gg[:, m, SEQ:].rearrange("p (b t) -> p b t", b=NB)
                    tt(gs, gs, h5[:, m, :, 1:], ALU.mult).then_inc(s["prod"], 1)
                dve.wait_ge(s["pturn"], 1)
                nc.vector.tensor_copy(prow[:, :], k.ps[0:36, 7, :]).then_inc(s["pout"], 1)
                nxt.split_lo_ahead(dve)

            @block.tensor
            def _(pe):
                pe.wait_ge(s["in"], 32)
                for m in range(MT):
                    ins = nc.tensor.transpose(k.ps[:, 7, m * 32:(m + 1) * 32], srow[:, m * P:(m + 1) * P], k.c('ident')[0:32, 0:32])
                ins.then_inc(s["sturn"], 1)
                dn.start_pe(pe)
                for i in range(n):
                    dn.multiply(pe, i, i % 2, k.hH, k.hL)
                    m = i - 2
                    if not 0 <= m < MT:
                        continue
                    if m == 0:
                        pe.wait_ge(s["gw"], 64)
                    pe.wait_ge(s["conv"], m + 1)
                    for z in range(2):
                        for c in range(3):
                            u = 6 * m + 3 * z + c
                            if u >= 2:
                                pe.wait_ge(s["gsig"], u - 1)
                            nc.tensor.matmul(k.ps[:, 6 + u % 2, 0:CH], gw[:, z, m, :], xc[:, m, c * CH:(c + 1) * CH],
                                             start=True, stop=True).then_inc(s["gate"], 1)
                pe.wait_ge(s["pack"], MT)
                pe.wait_ge(s["gsig"], 6 * MT)
                for m in range(MT):
                    ins = nc.tensor.transpose(k.ps[0:36, 7, m * P:(m + 1) * P], pack[:, m, :], k.c('ident'))
                ins.then_inc(s["pturn"], 1)

            @block.gpsimd
            def _(pool):
                nc.gpsimd.memset(gw[:, :, :, :], 0.0).then_inc(s["cleared"], 1)
                nc.gpsimd.memset(xin[:, :, 0:3], 0.0).then_inc(s["cleared"], 1)
                for m in range(MT):
                    pool.wait_ge(s["hi"], m + 1)
                    nc.gpsimd.tensor_tensor(k.oL[:, 4 + m, :], gg[:, m, :], k.oH[:, 4 + m, :], ALU.subtract)


def gla(k, dn):
    nc, d = k.nc, k.d
    n = 13
    cols = [COL['ga']] + [COL['gq'] + i * P for i in range(8)] + [COL['gg'] + i * P for i in range(4)]
    assert n == dn.n
    NC = SEQ // GC
    s = {x: k.sem("gl_" + x) for x in ("aw", "x", "abs", "exp", "ln", "g", "cum", "alpha", "init", "step", "e1", "em", "ed", "tr",
             "vout", "kout", "att", "attm", "ds", "state", "o", "sq", "ms", "root", "on", "ot", "res",
             "hi", "lo", "s0", "qm", "kdm", "stored", "q2")}
    with ExitStack() as es:
        sb = lambda nm, sh, t=F32: es.enter_context(nc.sbuf_tensor("gl" + nm, sh, t))
        kk, vT, sg = sb("k", [P, 2, T]), sb("v", [P, 4, T]), sb("sg", [P, 4, T])
        q2 = sb("q", [P, 2, 2, T])
        q = q2[:, 1]
        aT, aw, reset = sb("aT", [16, T]), sb("aw", [16, 256]), sb("reset", [P, T])
        ki, kd = sb("ki", [P, 2, T]), sb("kd", [P, 2, T])
        gx = k.oH[:, 8:12, :].rearrange("p a b -> p (a b)").bitcast(F32).rearrange("p (m t) -> p m t", m=2)
        bc = k.oL[:, 8:12, :].rearrange("p a b -> p (a b)").bitcast(F32).rearrange("p (m t) -> p m t", m=2)
        dec, dec_s = sb("dec", [P, 2, NC]), sb("decs", [P, 2 * NB])

        def chunks(ap):
            return ((ap[:, 0:SEQ].rearrange("p (c t) -> p c t", t=GC), ap[:, GC - 1:SEQ:GC]),
                    (ap[:, SEQ:].rearrange("p (c t) -> p c t", t=NS), ap[:, SEQ + NS - 1::NS]))

        with nc.Block() as block:

            @block.sync
            def _(sp):
                sp.dma_start(aw[:, :], d['gla_alpha_w']).then_inc(s["aw"], 16)
                for i in range(n):
                    dn.load(sp, i, i % 4, w_tile(d['w_in'], cols[i]), first=i < 4)

            @block.scalar
            def _(act):
                def alphas():
                    for u in range(6):
                        m, c = u // 3, slice(u % 3 * CH, (u % 3 + 1) * CH)
                        act.wait_ge(s["alpha"], u + 1)
                        nc.scalar.activation(gx[:, m, c], k.ps[:, 6 + u % 2, 0:CH], ACT.Identity, bias=k.vec[:, V_GAB + m:V_GAB + m + 1]).then_inc(s["x"], 1)

                def exps():
                    for m in range(2):
                        act.wait_ge(s["abs"], m + 1)
                        nc.scalar.activation(ki[:, m, :], ki[:, m, :], ACT.Exp, scale=-1.0).then_inc(s["exp"], 1)

                def logs():
                    for m in range(2):
                        act.wait_ge(s["exp"], m + 1)
                        nc.scalar.activation(ki[:, m, :], ki[:, m, :], ACT.Ln, bias=1.0).then_inc(s["ln"], 1)

                def decays(m):
                    act.wait_ge(s["cum"], 2 * m + 2)
                    nc.scalar.activation(gx[:, m, :], bc[:, m, :], ACT.Exp, scale=1 / 16).then_inc(s["e1"], 1)
                    nc.scalar.activation(ki[:, m, :], bc[:, m, :], ACT.Exp, scale=-1 / 16).then_inc(s["em"], 1)
                    nc.scalar.activation(kd[:, m, :], kd[:, m, :], ACT.Exp, scale=1 / 16).then_inc(s["ed"], 1)
                    nc.scalar.activation(dec[:, m, :], bc[:, m, GC - 1:SEQ:GC], ACT.Exp, scale=1 / 16)
                    nc.scalar.activation(dec_s[:, m::2], bc[:, m, SEQ + NS - 1::NS], ACT.Exp, scale=1 / 16)

                dn.start_evac(act)
                dn.split_hi(act, 0, 0, 0)
                for i in range(n):
                    if i + 1 < n:
                        dn.split_hi(act, i + 1, (i + 1) % 4, (i + 1) // 4)
                    dn.wait_tile(act, i)
                    ps = dense_out(k.ps, i % 2)
                    if i == 0:
                        ins = nc.scalar.activation(cols3(aT[:, :]), ps[0:16], ACT.Identity, bias=k.vec[0:16, VB_GA:VB_GA + 1], scale=1 / WS)
                    elif i < 9:
                        out = (q[:, 0], q[:, 1], kk[:, 0], kk[:, 1], vT[:, 0], vT[:, 1], vT[:, 2], vT[:, 3])[i - 1]
                        ins = nc.scalar.activation(cols3(out), ps, ACT.Identity, bias=k.vec[:, VB_GQ + i - 1:VB_GQ + i], scale=1 / WS)
                    else:
                        h = i - 9
                        ins = nc.scalar.activation(cols3(sg[:, h, :]), ps, ACT.Silu, bias=k.vec[:, VB_GG + h:VB_GG + h + 1], scale=1 / WS)
                    ins.then_inc(dn.evacuated, 1)
                    if i == 1:
                        alphas()
                    elif i == 2:
                        exps()
                    elif i == 3:
                        logs()
                    elif i in (6, 7):
                        decays(i - 6)

            @block.vector
            def _(dve):
                tt, stt = nc.vector.tensor_tensor, nc.vector.scalar_tensor_tensor

                def absolutes():
                    for m in range(2):
                        dve.wait_ge(s["x"], 3 * m + 3)
                        stt(ki[:, m, :], gx[:, m, :], -1.0, gx[:, m, :], ALU.mult, ALU.max).then_inc(s["abs"], 1)

                def cumulate(m):
                    dve.wait_ge(s["ln"], m + 1)
                    stt(gx[:, m, :], gx[:, m, :], 0.0, ki[:, m, :], ALU.min, ALU.subtract).then_inc(s["g"], 1)
                    dve.wait_ge(s["g"], m + 1)
                    nc.vector.tensor_tensor_scan(bc[:, m, :], reset[:, :], gx[:, m, :], 0.0, ALU.mult, ALU.add).then_inc(s["cum"], 1)
                    dve.wait_ge(s["cum"], 2 * m + 1)
                    for (whole, last), (out, _) in zip(chunks(bc[:, m, :]), chunks(kd[:, m, :])):
                        ins = stt(out, whole, -1.0, last.unsqueeze(2).broadcast_to(whole.shape), ALU.mult, ALU.add)
                    ins.then_inc(s["cum"], 1)

                def scale(m):
                    dve.wait_ge(dn.evacuated, 5 + 2)
                    dve.wait_ge(s["e1"], m + 1)
                    for u in range(2):
                        r = slice(u * GK, (u + 1) * GK)
                        ins = stt(q2[r, u, m, :], q[r, m, :], GK ** -0.5, gx[r, m, :], ALU.mult, ALU.mult)
                    ins.then_inc(s["q2"], 1)
                    dve.wait_ge(s["em"], m + 1)
                    tt(ki[:, m, :], kk[:, m, :], ki[:, m, :], ALU.mult)
                    dve.wait_ge(s["ed"], m + 1)
                    tt(kd[:, m, :], kk[:, m, :], kd[:, m, :], ALU.mult)

                nc.vector.memset(reset[:, :], 1.0).then_inc(s["init"], 1)
                dve.wait_ge(s["init"], 1)
                nc.vector.memset(reset[:, 0:SEQ:GC], 0.0)
                nc.vector.memset(reset[:, SEQ:T:NS], 0.0).then_inc(s["init"], 1)
                dve.wait_ge(s["init"], 2)
                for i in range(n):
                    dn.split_lo(dve, i, i % 4)
                    if i == 3:
                        absolutes()
                    elif i in (5, 6):
                        cumulate(i - 5)
                    elif i in (8, 9):
                        scale(i - 8)
                    elif i == 10:
                        dve.wait_ge(s["q2"], 2)
                        for u in range(2):
                            nc.vector.memset(q2[(1 - u) * GK:(2 - u) * GK, u], 0.0)

            @block.gpsimd
            def _(pool):
                for h in range(GH):
                    pool.wait_ge(dn.evacuated, 2 + 10 + h)
                    nc.gpsimd.tensor_scalar(sg[:, h, :], sg[:, h, :], k.vec[:, V_GNG + h:V_GNG + h + 1], None, ALU.mult)

            @block.tensor
            def _(pe):
                dn.start_pe(pe)
                for i in range(2):
                    dn.multiply(pe, i, i, k.hH, k.hL)
                pe.wait_ge(s["aw"], 16)
                pe.wait_ge(dn.evacuated, 1 + 2)
                for u in range(6):
                    m, c = u // 3, slice(u % 3 * CH, (u % 3 + 1) * CH)
                    if u >= 2:
                        pe.wait_ge(s["x"], u - 1)
                    nc.tensor.matmul(k.ps[:, 6 + u % 2, 0:CH], aw[:, m * P:(m + 1) * P], aT[:, c], start=True, stop=True).then_inc(s["alpha"], 1)
                with pe.Fori(1, n // 2) as j:
                    dn.multiply(pe, j * 2, 0, k.hH, k.hL)
                    dn.multiply(pe, j * 2 + 1, 1, k.hH, k.hL)
                dn.multiply(pe, n - 1, 0, k.hH, k.hL)

        rows = [P] * NT + [TS]
        vN, kN = sb("vN", [P, 3, 512]), sb("kN", [P, 3, 256])
        stat = sb("stat", [P, 2, 4])
        slots = k.w32[:, :, :, :].rearrange("p a b c -> p (a b c)")
        S = slots[:, 0:1024].rearrange("p (s m v) -> p s m v", s=4, m=2)
        sq, on = slots[:, 3072:3584], slots[:, 3584:4096]
        att, res = (w[:, :, :, :].rearrange("p a b c -> p (a b c)").bitcast(F32).rearrange("p (s n) -> p s n", s=2)
                    for w in (k.wH, k.wL))
        spare = kk[:, :, :].rearrange("p m t -> p (m t)")
        S0 = spare[:, 0:2048].rearrange("p (b m v) -> p b m v", b=NB, m=2)
        reset_f = reset[:, :]
        qm = reset_f[:, 0:1024].rearrange("p (u m b t) -> p u m b t", u=2, m=2, b=NB)
        kdm = slots[0:TS, 1024:3072].rearrange("p (b n) -> p b n", b=NB)
        BV, BK, BA, BD, BO, BT = 0, 1, 2, (3, 5), (4, 7), 6
        with nc.Block() as block:

            @block.sync
            def _(sp):
                for m in range(2):
                    sp.dma_start(S0[:, :, m, :], d['state_gla'].rearrange("b (m u) k v -> m (u k) b v", m=2)[m]).then_inc(s["s0"], 16)
                sp.wait_ge(s["state"], 1 + NC)
                sp.dma_start(d['out_gla_p'][0, 0].rearrange("(m u) k v -> (u k) m v", m=2), S[:, NC % 4]).then_inc(s["stored"], 16)
                sp.wait_ge(s["state"], 1 + NC + 2)
                for m in range(2):
                    sp.dma_start(d['out_gla_s'][0].rearrange("b (m u) k v -> m (u k) b v", m=2)[m], S0[:, :, m, :]).then_inc(s["stored"], 16)
                sp.wait_ge(s["stored"], 48)

            def hp(h):
                return slice(h % 2 * GK, h % 2 * GK + GK)

            def turn_out(pe, t):
                w = rows[t]
                pe.wait_ge(s["on"], t + 1)
                if t:
                    pe.wait_ge(s["res"], t)
                for h in range(GH):
                    ins = nc.tensor.transpose(k.ps[:, BT, h * P:h * P + w], on[0:w, h * P:(h + 1) * P], k.c('ident')[0:w, 0:w])
                ins.then_inc(s["ot"], 1)

            def heads(ap, w=P):
                return ap.rearrange("p (h n) -> p h n", h=GH)[:, :, 0:w]

            def copies(act, t):
                w = rows[t]
                act.wait_ge(s["tr"], t + 1)
                if t >= 3:
                    act.wait_ge(s["o"], t - 2)
                nc.scalar.copy(vN[0:w, t % 3, :], k.ps[0:w, BV, :]).then_inc(s["vout"], 1)
                nc.scalar.copy(kN[0:w, t % 3, :], k.ps[0:w, BK, 0:256]).then_inc(s["kout"], 1)

            def squares(act, t):
                w = rows[t]
                act.wait_ge(s["o"], t + 1)
                if t:
                    act.wait_ge(s["ms"], 2 * t)
                nc.scalar.activation(sq[0:w, :], k.ps[0:w, BO[t % 2], :], ACT.Square).then_inc(s["sq"], 1)
                act.wait_ge(s["ms"], 2 * t + 2)
                nc.scalar.activation(stat[0:w, t % 2, :], stat[0:w, t % 2, :], ACT.Sqrt).then_inc(s["root"], 1)

            def high(act, t):
                act.wait_ge(s["res"], t + 1)
                c = slice(t * P, t * P + rows[t])
                nc.scalar.copy(k.oH[:, 8:12, c], heads(res[:, t % 2, :], rows[t])).then_inc(s["hi"], 1)

            def mean_squares(dve, t):
                w = rows[t]
                st = stat[0:w, t % 2, :]
                dve.wait_ge(s["sq"], t + 1)
                nc.vector.tensor_reduce(st, heads(sq[0:w, :]), AX, ALU.add).then_inc(s["ms"], 1)
                dve.wait_ge(s["ms"], 2 * t + 1)
                nc.vector.tensor_scalar(st, st, 1.0 / GV, EPS, ALU.mult, ALU.add).then_inc(s["ms"], 1)

            def normed(dve, t):
                w = rows[t]
                st = stat[0:w, t % 2, :]
                dve.wait_ge(s["root"], t + 1)
                nc.vector.reciprocal(st, st).then_inc(s["step"], 1)
                dve.wait_ge(s["step"], t + 1)
                if t:
                    dve.wait_ge(s["ot"], t)
                nc.vector.tensor_tensor(heads(on[0:w, :]), heads(k.ps[0:w, BO[t % 2], :]), st.unsqueeze(2).broadcast_to([w, GH, GV]),
                                        ALU.mult).then_inc(s["on"], 1)

            def gated(dve, t):
                w, c = rows[t], slice(t * P, t * P + rows[t])
                dve.wait_ge(s["ot"], t + 1)
                if t >= 2:
                    dve.wait_ge(s["lo"], t - 1)
                nc.vector.tensor_tensor(heads(res[:, t % 2, :], w), heads(k.ps[:, BT, :], w), sg[:, :, c], ALU.mult).then_inc(s["res"], 1)

            @block.tensor
            def _(pe):
                def turn(t):
                    w, c = rows[t], slice(t * P, t * P + rows[t])
                    if t >= 1:
                        pe.wait_ge(s["vout"], t)
                        pe.wait_ge(s["kout"], t)
                    for h in range(GH):
                        nc.tensor.transpose(k.ps[0:w, BV, h * P:(h + 1) * P], vT[:, h, c], k.c('ident'))
                    for m in range(2):
                        ins = nc.tensor.transpose(k.ps[0:w, BK, m * P:(m + 1) * P], kd[:, m, c], k.c('ident'))
                    ins.then_inc(s["tr"], 1)

                def attend(t):
                    w, c = rows[t], slice(t * P, t * P + rows[t])
                    if t:
                        pe.wait_ge(s["attm"], t)
                    for h in range(GH):
                        ins = nc.tensor.matmul(k.ps[0:w, BA, h * P:h * P + w], ki[:, h // 2, c], q2[:, h % 2, h // 2, c], start=True, stop=True)
                    ins.then_inc(s["att"], 1)

                def states(t):
                    pe.wait_ge(s["vout"], t + 1)
                    pe.wait_ge(s["kout"], t + 1)
                    if t:
                        pe.wait_ge(s["state"], 1 + 2 * t)
                    for ch in range(2):
                        r = slice(ch * GC, (ch + 1) * GC)
                        for h in range(GH):
                            ins = nc.tensor.matmul(k.ps[hp(h), BD[ch], h // 2 * GV:(h // 2 + 1) * GV],
                                                   kN[r, t % 3, h * GK:(h + 1) * GK], vN[r, t % 3, h * GV:(h + 1) * GV], start=True, stop=True)
                    ins.then_inc(s["ds"], 1)

                def outputs(t):
                    w = rows[t]
                    pe.wait_ge(s["attm"], t + 1)
                    pe.wait_ge(s["vout"], t + 1)
                    if t >= 2:
                        pe.wait_ge(s["on"], t - 1)
                    for h in range(GH):
                        o = slice(h * GV, (h + 1) * GV)
                        nc.tensor.matmul(k.ps[0:w, BO[t % 2], o], att[0:w, t % 2, h * P:h * P + w], vN[0:w, t % 3, o],
                                         start=True, stop=False)
                        if t < NT:
                            for ch in range(2):
                                n_ch = 2 * t + ch
                                pe.wait_ge(s["state"], 1 + n_ch)
                                cc = slice(t * P + ch * GC, t * P + (ch + 1) * GC)
                                ins = nc.tensor.matmul(k.ps[ch * GC:(ch + 1) * GC, BO[t % 2], o], q2[:, h % 2, h // 2, cc],
                                                       S[:, n_ch % 4, h // 2, :], start=False, stop=True)
                        else:
                            pe.wait_ge(s["s0"], 32)
                            pe.wait_ge(s["qm"], 4)
                            for b in range(NB):
                                ins = nc.tensor.matmul(k.ps[0:w, BO[t % 2], o], qm[:, h % 2, h // 2, b, :], S0[:, b, h // 2, :],
                                                       start=False, stop=(b == NB - 1))
                    ins.then_inc(s["o"], 1)

                turn(0)
                for t in range(NT + 4):
                    if t <= NT:
                        attend(t)
                    if t < NT:
                        turn(t + 1)
                        states(t)
                    if 1 <= t <= NT + 1:
                        outputs(t - 1)
                    if t == NT + 1:
                        pe.wait_ge(s["kdm"], 1)
                        pe.wait_ge(s["attm"], NT + 1)
                        pe.wait_ge(s["state"], 1 + NC)
                        for b in range(NB):
                            for h in range(GH):
                                o = b % 2 * 256 + h // 2 * GV
                                ins = nc.tensor.matmul(k.ps[hp(h), b // 2, o:o + GV], kdm[:, b, h * GK:(h + 1) * GK], vN[0:TS, NT % 3, h * GV:(h + 1) * GV],
                                                       start=True, stop=True)
                        ins.then_inc(s["ds"], 1)
                    if t >= 3:
                        turn_out(pe, t - 3)

            @block.scalar
            def _(act):
                copies(act, 0)
                for t in range(NT + 5):
                    if 2 <= t <= NT + 2:
                        squares(act, t - 2)
                    if t < NT:
                        copies(act, t + 1)
                    if t >= 4:
                        high(act, t - 4)

            @block.gpsimd
            def _(pool):
                for t in range(NT + 1):
                    w, c = rows[t], slice(t * P, t * P + rows[t])
                    pool.wait_ge(s["hi"], t + 1)
                    nc.gpsimd.tensor_tensor(k.oL[:, 8:12, c], heads(res[:, t % 2, :], w), k.oH[:, 8:12, c], ALU.subtract).then_inc(s["lo"], 1)

            @block.vector
            def _(dve):
                tt, ts, stt = nc.vector.tensor_tensor, nc.vector.tensor_scalar, nc.vector.scalar_tensor_tensor
                nc.vector.memset(S[:, 0], 0.0).then_inc(s["state"], 1)
                for m in range(2):
                    for u in range(2):
                        tt(qm[:, u, m], k.c('seqcols').rearrange("p (b t) -> p b t", b=NB),
                           q2[:, u, m, SEQ:].unsqueeze(1).broadcast_to([P, NB, TS]), ALU.mult).then_inc(s["qm"], 1)
                for t in range(NT + 5):
                    if t <= NT:
                        w = rows[t]
                        dve.wait_ge(s["att"], t + 1)
                        if t >= 2:
                            dve.wait_ge(s["o"], t - 1)
                        mask = k.c('gmask') if t < NT else k.c('gmask_s', TS)
                        tt(heads(att[0:w, t % 2, :], w), heads(k.ps[0:w, BA, :], w),
                           mask.unsqueeze(1).broadcast_to([w, GH, w]), ALU.mult).then_inc(s["attm"], 1)
                    if t >= 4:
                        gated(dve, t - 4)
                    if 2 <= t <= NT + 2:
                        mean_squares(dve, t - 2)
                    if t < NT:
                        dve.wait_ge(s["ds"], t + 1)
                        for ch in range(2):
                            n_ch = 2 * t + ch
                            dve.wait_ge(s["state"], 1 + n_ch)
                            if n_ch >= 3:
                                dve.wait_ge(s["o"], (n_ch - 3) // 2 + 1)
                            for m in range(2):
                                ins = stt(S[:, (n_ch + 1) % 4, m, :], S[:, n_ch % 4, m, :], dec[:, m, n_ch:n_ch + 1],
                                          k.ps[:, BD[ch], m * GV:(m + 1) * GV], ALU.mult, ALU.add)
                            ins.then_inc(s["state"], 1)
                    elif t == NT:
                        dve.wait_ge(s["kout"], NT + 1)
                        tt(kdm[:, :, :], kN[0:TS, NT % 3, :].unsqueeze(1).broadcast_to([TS, NB, 256]),
                           k.c('seqrows', TS).unsqueeze(2).broadcast_to([TS, NB, 256]), ALU.mult).then_inc(s["kdm"], 1)
                    if 2 <= t <= NT + 2:
                        normed(dve, t - 2)
                    if t == NT + 2:
                        dve.wait_ge(s["ds"], NT + 1)
                        dve.wait_ge(s["s0"], 32)
                        flat_s0 = S0.rearrange("p b m v -> p (b m) v")
                        dve.wait_ge(s["o"], NT + 1)
                        tt(flat_s0, flat_s0, dec_s[:, :].unsqueeze(2).broadcast_to([P, 2 * NB, GV]), ALU.mult).then_inc(s["state"], 1)
                        dve.wait_ge(s["state"], 1 + NC + 1)
                        tt(S0.rearrange("p b m v -> p (b m v)"), S0.rearrange("p b m v -> p (b m v)"),
                           k.ps[:, 0:4, :].rearrange("p a n -> p (a n)"), ALU.add).then_inc(s["state"], 1)


def merge(k, nxt):
    nc, d = k.nc, k.d
    loaded = [k.sem(f"mg_w{i}") for i in range(3)]
    split_hi, split_lo = k.sem("mg_hi"), k.sem("mg_lo")
    gate_mult, used, gate_out, branch_out = k.sem("mg_gmult"), k.sem("mg_used"), k.sem("mg_gout"), k.sem("mg_bout")
    added, sum_hi, sum_lo = k.sem("mg_added"), k.sem("mg_sumhi"), k.sem("mg_sumlo")
    NU = 3 * KD
    with nc.sbuf_tensor("mgw", [P, 3, 12, P], F32) as w32, nc.sbuf_tensor("mgwH", [P, 2, 12, P], F16) as wH, \
            nc.sbuf_tensor("mgwL", [P, 2, 12, P], F16) as wL, nc.sbuf_tensor("mgsg", [P, 2, T], F32) as sg, \
            nc.sbuf_tensor("mgacc", [P, 2, T], F32) as acc, nc.sbuf_tensor("mgtmp", [P, T], F32) as tmp, \
            nc.Block() as block:

        def units(eng, body, lookahead):
            if lookahead:
                with eng.Fori(0, NU // 6 - 1) as it:
                    for u in range(6):
                        body(it * 6 + u, u, it * 2 + u // 3)
                for u in range(6):
                    body(NU - 6 + u, u, KD - 2 + u // 3)
            else:
                with eng.Fori(0, NU // 6) as it:
                    for u in range(6):
                        body(it * 6 + u, u, it * 2 + u // 3)

        @block.sync
        def _(sp):
            def load(u, dt):
                z, slot = u % 3, u % 3
                sp.dma_start(w32[:, slot, 0:8, :], w_tile(d['w_in'], COL['merge'] + z * D + dt * P)).then_inc(loaded[slot], 16)
                sp.dma_start(w32[:, slot, 8:12, :], d['w_branch'][z][:, bass.ds(dt * P, P)].rearrange("(kt p) n -> p kt n", p=P)).then_inc(loaded[slot], 16)

            for u in range(3):
                load(u, 0)
            with sp.Fori(1, KD) as dt:
                for u in range(3):
                    sp.wait_ge(split_lo, dt * 3 + (u - 2))
                    load(u, dt)
            nxt.load_ahead(sp)

        @block.tensor
        def _(pe):
            pe.sem_inc(used, 2)

            def unit(i, u, dt):
                s, z = u % 2, u % 3
                pe.wait_ge(split_lo, i + 1)
                pe.wait_ge(gate_out, i + 1)
                for kt in range(KD):
                    for w, x in ((wH, k.hH), (wH, k.hL), (wL, k.hH)):
                        for c in range(3):
                            ins = nc.tensor.matmul(k.ps[:, c, 0:CH], w[:, s, kt, :], x[:, kt, c * CH:(c + 1) * CH],
                                                   start=(kt == 0 and w is wH and x is k.hH), stop=(kt == KD - 1 and w is wL))
                ins.then_inc(gate_mult, 1)
                pe.wait_ge(branch_out, i + 2)
                for kt in range(4):
                    for w, x in ((wH, k.oH), (wH, k.oL), (wL, k.oH)):
                        for c in range(3):
                            ins = nc.tensor.matmul(k.ps[:, 3 + c, 0:CH], w[:, s, 8 + kt, :], x[:, 4 * z + kt, c * CH:(c + 1) * CH],
                                                   start=(kt == 0 and w is wH and x is k.oH), stop=(kt == 3 and w is wL))
                ins.then_inc(used, 1)

            units(pe, unit, False)

        @block.scalar
        def _(act):
            act.sem_inc(gate_out, 1)

            def split(i, u):
                act.wait_ge(used, i + 1)
                nc.scalar.activation(wH[:, u % 2, :, :], w32[:, u % 3, :, :], ACT.Copy, scale=WS).then_inc(split_hi, 1)

            def unit(i, u, dt):
                if not isinstance(i, int) or i + 1 < NU:
                    nxt = (u + 1) % 6
                    act.wait_ge(loaded[nxt % 3], (dt + (1 if nxt % 3 == 0 else 0)) * 32 + 32)
                    split(i + 1, nxt)
                act.wait_ge(gate_mult, i + 1)
                act.wait_ge(branch_out, i + 1)
                b = VB_MG + u % 3 * KD + dt
                nc.scalar.activation(cols3(sg[:, u % 2, :]), dense_out(k.ps, 0), ACT.Sigmoid, bias=k.vec[:, bass.ds(b, 1)],
                                     scale=1 / WS).then_inc(gate_out, 1)
                if u % 3 == 2:
                    act.wait_ge(added, dt * 2 + 3)
                    nc.scalar.copy(k.mH[:, bass.ds(dt, 1), :], acc[:, u // 3, :].unsqueeze(1)).then_inc(sum_hi, 1)

            act.wait_ge(loaded[0], 32)
            split(0, 0)
            units(act, unit, True)
            nxt.split_hi_ahead(act)

        @block.vector
        def _(dve):
            dve.sem_inc(branch_out, 2)
            dve.sem_inc(added, 1)

            def split(i, u):
                dve.wait_ge(split_hi, i + 1)
                nc.vector.scalar_tensor_tensor(wL[:, u % 2, :, :], w32[:, u % 3, :, :], WS, wH[:, u % 2, :, :],
                                               ALU.mult, ALU.subtract).then_inc(split_lo, 1)

            def unit(i, u, dt):
                if not isinstance(i, int) or i + 1 < NU:
                    split(i + 1, (u + 1) % 6)
                z, a = u % 3, u // 3
                if z == 0:
                    dve.wait_ge(sum_lo, dt + 1)
                else:
                    dve.wait_ge(added, dt * 2 + z)
                dve.wait_ge(gate_out, i + 2)
                dve.wait_ge(used, i + 3)
                out = acc[:, a, :] if z == 0 else tmp[:, :]
                nc.vector.scalar_tensor_tensor(cols3(out), ps_branch, 1 / WS, cols3(sg[:, u % 2, :]), ALU.mult, ALU.mult).then_inc(branch_out, 1)
                if z:
                    dve.wait_ge(branch_out, i + 3)
                    nc.vector.tensor_tensor(acc[:, a, :], acc[:, a, :], tmp[:, :], ALU.add).then_inc(added, 1)

            ps_branch = dense_out(k.ps, 1)
            split(0, 0)
            units(dve, unit, True)
            nxt.split_lo_ahead(dve)

        @block.gpsimd
        def _(pool):
            pool.sem_inc(sum_lo, 2)
            with pool.Fori(0, KD // 2) as it:
                for a in range(2):
                    dt = it * 2 + a
                    pool.wait_ge(sum_hi, dt + 1)
                    o = bass.ds(dt, 1)
                    nc.gpsimd.tensor_tensor(k.mL[:, o, :], acc[:, a, :].unsqueeze(1), k.mH[:, o, :], ALU.subtract).then_inc(sum_lo, 1)


def square(k, act, i, sq, squared, added):
    if i >= 3:
        act.wait_ge(added, i - 2)
    out = k.ssq[:, :] if i == 0 else sq[:, i % 2, :]
    k.nc.scalar.activation(out, k.xT[:, i, :], ACT.Square).then_inc(squared, 1)


def add_square(k, dve, i, sq, squared, added):
    dve.wait_ge(squared, i + 1)
    if i >= 2:
        dve.wait_ge(added, i - 1)
    k.nc.vector.tensor_tensor(k.ssq[:, :], k.ssq[:, :], sq[:, i % 2, :], ALU.add).then_inc(added, 1)


def w_out(k, dn):
    nc, d, xT = k.nc, k.d, k.xT
    x_back, squared, added = k.sem("wo_x"), k.sem("wo_sq"), k.sem("wo_added")
    with nc.sbuf_tensor("wosq", [P, 2, T], F32) as sq, nc.Block() as block:

        @block.sync
        def _(sp):
            for i in range(KD):
                dn.load(sp, i, i % 4, w_tile(d['w_out'], i * P), first=i < 4)
                if i == 3:
                    sp.dma_start(flat(xT[:, :, :]), k.xTd).then_inc(x_back, 16)

        @block.scalar
        def _(act):
            dn.split_hi(act, 0, 0, 0)
            for i in range(KD):
                if i + 1 < KD:
                    dn.split_hi(act, i + 1, (i + 1) % 4, (i + 1) // 4)
                act.wait_ge(dn.evacuated, i + 3)
                square(k, act, i, sq, squared, added)

        @block.vector
        def _(dve):
            dn.start_evac(dve)
            dn.split_lo(dve, 0, 0)
            dve.wait_ge(x_back, 16)
            for i in range(KD):
                if i + 1 < KD:
                    dn.split_lo(dve, i + 1, (i + 1) % 4)
                dn.wait_tile(dve, i)
                nc.vector.scalar_tensor_tensor(cols3(xT[:, i, :]), dense_out(k.ps, i % 2), 1 / WS, cols3(xT[:, i, :]),
                                               ALU.mult, ALU.add).then_inc(dn.evacuated, 1)
                if i >= 2:
                    add_square(k, dve, i - 1, sq, squared, added)
            add_square(k, dve, KD - 1, sq, squared, added)

        @block.tensor
        def _(pe):
            dn.multiply_all(pe, k.mH, k.mL)


def mlp(k, dn):
    nc, d, xT, aH, aL = k.nc, k.d, k.xT, k.mH, k.mL
    NG = FF // D
    assert dn.n == 2 * KD * NG
    hi_made, squared, lo_made = k.sem("mp_ahi"), k.sem("mp_sq"), k.sem("mp_alo")
    xsquared, xadded = k.sem("mp_xsq"), k.sem("mp_xadd")
    with nc.sbuf_tensor("mprelu", [P, 2, T], F32) as relu, nc.sbuf_tensor("mpxsq", [P, 2, T], F32) as xsq, nc.sbuf_tensor("mpsq", [P, T], F32) as sq, nc.Block() as block:

        def groups(eng, body):
            with eng.Fori(0, NG - 1) as g:
                for t in range(2 * KD):
                    body(g, t, g * 16 + t)
            for t in range(2 * KD):
                body(NG - 1, t, (NG - 1) * 16 + t)

        def last(i):
            return isinstance(i, int) and i + 1 == dn.n

        @block.sync
        def _(sp):
            def load(g, t, i):
                src = w_tile(d['mlp_w1'], g * D + t * P) if t < KD else \
                    d['mlp_w2'][bass.ds(g * D, D), (t - KD) * P:(t - KD + 1) * P].rearrange("(kt p) n -> p kt n", p=P)
                dn.load(sp, i, t % 4, src, first=isinstance(i, int) and i < 4)

            for t in range(2 * KD):
                load(0, t, t)
            with sp.Fori(1, NG) as g:
                for t in range(2 * KD):
                    load(g, t, g * 16 + t)

        @block.tensor
        def _(pe):
            dn.start_pe(pe)
            with pe.Fori(0, NG) as g:
                with pe.Fori(0, KD // 2) as j:
                    for u in range(2):
                        dn.multiply(pe, g * 16 + j * 2 + u, u, k.hH, k.hL)
                dn.multiply(pe, g * 16 + KD, 0, aH, aL, ready=lambda pe, kt: pe.wait_ge(lo_made, g * 8 + (kt + 3)))
                dn.multiply(pe, g * 16 + KD + 1, 1, aH, aL)
                with pe.Fori(1, KD // 2) as j:
                    for u in range(2):
                        dn.multiply(pe, g * 16 + j * 2 + (KD + u), u, aH, aL)

        @block.scalar
        def _(act):
            def tile(g, t, i):
                if not last(i):
                    nxt = (t + 1) % 16
                    dn.split_hi(act, i + 1, nxt % 4, g * 4 + (t + 1) // 4)
                if t < KD:
                    act.wait_ge(dn.evacuated, i + 3)
                    nc.scalar.activation(aH[:, t, :], relu[:, t % 2, :], ACT.Square).then_inc(hi_made, 1)
                elif isinstance(i, int):
                    act.wait_ge(dn.evacuated, i + 3)
                    square(k, act, t - KD, xsq, xsquared, xadded)

            dn.split_hi(act, 0, 0, 0)
            groups(act, tile)

        @block.vector
        def _(dve):
            def tile(g, t, i):
                if not last(i):
                    dn.split_lo(dve, i + 1, (t + 1) % 4)
                dn.wait_tile(dve, i)
                ps = dense_out(k.ps, t % 2)
                if t < KD:
                    dve.wait_ge(lo_made, g * 8 + (t + 1))
                    ins = nc.vector.tensor_scalar(cols3(relu[:, t % 2, :]), ps, 1 / WS, 0.0, ALU.mult, ALU.max)
                else:
                    dve.wait_ge(dn.evacuated, i + 2)
                    ins = nc.vector.scalar_tensor_tensor(cols3(xT[:, t - KD, :]), ps, 1 / WS, cols3(xT[:, t - KD, :]), ALU.mult, ALU.add)
                ins.then_inc(dn.evacuated, 1)
                if isinstance(i, int) and t >= KD + 2:
                    add_square(k, dve, t - KD - 1, xsq, xsquared, xadded)

            dn.start_evac(dve)
            dn.split_lo(dve, 0, 0)
            groups(dve, tile)
            add_square(k, dve, KD - 1, xsq, xsquared, xadded)

        @block.gpsimd
        def _(pool):
            pool.sem_inc(lo_made, 2)
            with pool.Fori(0, NG) as g:
                for t in range(KD):
                    n = g * 8 + t
                    pool.wait_ge(dn.evacuated, g * 16 + (t + 3))
                    pool.wait_ge(lo_made, n + 2)
                    nc.gpsimd.tensor_tensor(sq[:, :], relu[:, t % 2, :], relu[:, t % 2, :], ALU.mult).then_inc(squared, 1)
                    pool.wait_ge(squared, n + 1)
                    pool.wait_ge(hi_made, n + 1)
                    nc.gpsimd.tensor_tensor(aL[:, t, :], sq[:, :], aH[:, t, :], ALU.subtract).then_inc(lo_made, 1)


def final_norm(k):
    nc, d, xT = k.nc, k.d, k.xT
    summed, ms_ready, root_ready, step, scale_ready = (k.sem("y_" + n) for n in ("summed", "ms", "root", "step", "scale"))
    diag_ready, turned, out0, out1 = k.sem("y_diag"), k.sem("y_turned"), k.sem("y_out0"), k.sem("y_out1")
    stored = [k.sem(f"y_stored{i}") for i in range(2)]
    yp = d['out_y_prompt'].rearrange("b (n p) c -> (b n) p c", p=P)
    ys = d['out_y_sample'].rearrange("b t c -> (b t) c")
    NC = NT + 1
    with nc.sbuf_tensor("yn", [P, 2, D], F32) as yn, nc.sbuf_tensor("ydiag", [P, KD, P], F32) as diag, \
            nc.sbuf_tensor("yst", [P, 4, 16], F32) as st, nc.Block() as block:
        ms, root, y, t2 = (st[:, i, 0:NC] for i in range(4))

        @block.tensor
        def _(pe):
            for t in range(NC):
                w = P if t < NT else TS
                ins = nc.tensor.matmul(k.ps[0:w, 7, t:t + 1], k.ssq[:, t * P:t * P + w], k.c('ones')[:, 0:1], start=True, stop=True)
            ins.then_inc(summed, 1)
            pe.wait_ge(diag_ready, 1)
            for t in range(NC):
                w = P if t < NT else TS
                if t == 3:
                    pe.wait_ge(ms_ready, 3)
                if t >= 4:
                    pe.wait_ge(out0, t - 3)
                    pe.wait_ge(out1, t - 3)
                for kt in range(KD):
                    ins = nc.tensor.matmul(k.ps[0:w, 2 * (t % 4) + kt // 4, kt % 4 * P:(kt % 4 + 1) * P], xT[:, kt, t * P:t * P + w],
                                           diag[:, kt, :], start=True, stop=True)
                    if kt == 3:
                        ins.then_inc(turned, 1)
                ins.then_inc(turned, 1)

        @block.scalar
        def _(act):
            act.wait_ge(ms_ready, 3)
            nc.scalar.activation(root, ms, ACT.Sqrt).then_inc(root_ready, 1)
            act.wait_ge(scale_ready, 1)
            for t in range(NC):
                w = P if t < NT else TS
                act.wait_ge(turned, 2 * t + 1)
                if t >= 2:
                    act.wait_ge(stored[t % 2], 16 * (t // 2))
                nc.scalar.activation(yn[0:w, t % 2, 0:512], k.ps[0:w, 2 * (t % 4), :], ACT.Copy, scale=y[0:w, t:t + 1]).then_inc(out0, 1)

        @block.vector
        def _(dve):
            tt, ts = nc.vector.tensor_tensor, nc.vector.tensor_scalar
            tt(diag[:, :, :], k.c('ident').unsqueeze(1).broadcast_to([P, KD, P]),
               k.vec[:, VG3:VG3 + KD].unsqueeze(2).broadcast_to([P, KD, P]), ALU.mult).then_inc(diag_ready, 1)
            nc.vector.memset(ms, 1.0).then_inc(ms_ready, 1)
            dve.wait_ge(ms_ready, 1)
            dve.wait_ge(summed, 1)
            ts(ms[:, 0:NT], k.ps[:, 7, 0:NT], 1.0 / D, EPS, ALU.mult, ALU.add).then_inc(ms_ready, 1)
            ts(ms[0:TS, NT:NC], k.ps[0:TS, 7, NT:NC], 1.0 / D, EPS, ALU.mult, ALU.add).then_inc(ms_ready, 1)
            dve.wait_ge(root_ready, 1)
            made = [0]

            def settle(ins):
                made[0] += 1
                ins.then_inc(step, 1)
                dve.wait_ge(step, made[0])

            settle(nc.vector.reciprocal(y, root))
            settle(tt(t2, y, y, ALU.mult))
            settle(tt(t2, t2, ms, ALU.mult))
            settle(ts(t2, t2, -0.5, 1.5, ALU.mult, ALU.add))
            tt(y, y, t2, ALU.mult).then_inc(scale_ready, 1)
            dve.wait_ge(scale_ready, 1)
            for t in range(NC):
                w = P if t < NT else TS
                dve.wait_ge(turned, 2 * t + 2)
                if t >= 2:
                    dve.wait_ge(stored[t % 2], 16 * (t // 2))
                ts(yn[0:w, t % 2, 512:D], k.ps[0:w, 2 * (t % 4) + 1, :], y[0:w, t:t + 1], None, ALU.mult).then_inc(out1, 1)

        @block.sync
        def _(sp):
            for t in range(NC):
                sp.wait_ge(out0, t + 1)
                sp.wait_ge(out1, t + 1)
                if t < NT:
                    sp.dma_start(yp[t], yn[:, t % 2, :]).then_inc(stored[t % 2], 16)
                else:
                    sp.dma_start(ys, yn[0:TS, t % 2, :]).then_inc(stored[t % 2], 16)
            sp.wait_ge(stored[0], 16 * 5)
            sp.wait_ge(stored[1], 16 * 4)


def build(nc, d):
    k = Prog(nc, d)

    def in_tiles(*cols):
        return [w_tile(d['w_in'], c) for c in cols]

    with ExitStack() as ctx:
        sb = lambda n, s, t=F32: ctx.enter_context(nc.sbuf_tensor(n, s, t))
        k.cst = sb("cst", [P, CW])
        k.c = lambda n, rows=P: k.cst[0:rows, CN[n][0]:CN[n][0] + CN[n][1]]
        k.vec = sb("vec", [P, 256])
        k.hH, k.hL = sb("hH", [P, KD, T], F16), sb("hL", [P, KD, T], F16)
        k.oH, k.oL = sb("oH", [P, 12, T], F16), sb("oL", [P, 12, T], F16)
        k.w32 = sb("w32", [P, 4, KD, P])
        k.wH, k.wL = sb("wH", [P, 2, KD, P], F16), sb("wL", [P, 2, KD, P], F16)
        k.ps = ctx.enter_context(nc.psum_tensor("ps", [P, 8, 512], F32))
        k.xTd = nc.dram_tensor("xTd", (P, KD * T), F32, kind="Internal").ap()
        k.skew = nc.dram_tensor("skew", (H, P, 384), F32, kind="Internal").ap()
        k.sums = sb("sums", [P, NT + 1])
        k.ptab = sb("ptab", [1, NB * PAGES], I32)
        with nc.sbuf_tensor("xT", [P, KD, T], F32) as xT:
            k.xT = xT
            load(k)
            k.end_stage()
            cp = Dense(k, "cp", 2, ahead=in_tiles(COL['cmp'], COL['cmp'] + P))
            norm(k, "n1", VG1, cp, sums_by_token=True)
            k.end_stage()
        with ExitStack() as nsa:
            sb2 = lambda n, s, t=F32: nsa.enter_context(nc.sbuf_tensor(n, s, t))
            k.kcT = sb2("kcT", [P, 9, NCB])
            k.vcN = sb2("vcN", [NCB, 9, P])
            k.cmpT = sb2("cmpT", [P, 2, T])
            pn = Dense(k, "pn", 9, ahead=in_tiles(*(COL['q'] + m * P for m in range(4))))
            compress(k, cp, pn)
            k.end_stage()
            k.qT = sb2("qT", [P, HPG, T])
            k.kT = sb2("kT", [P, 2, T])
            k.vN = sb2("vN", [P, NT, 2, P])
            k.vS = sb2("vS", [NS, NB, 2, P])
            k.gN = sb2("gN", [P, NT + 1, 24])
            k.toep = sb2("toep", [P, H, 256])
            k.oTs = sb2("oTs", [P, 4, TS])
            k.key_in = [k.sem(f"sa_key{i}", keep=True) for i in range(3)]
            project_nsa(k, pn)
            k.end_stage()
            kparts = k.w32[:, :, :, :].rearrange("p a b c -> p (a b c)").bitcast(F16)
            k.kH, k.kL = (kparts[:, u * 4096:(u + 1) * 4096].rearrange("p (g z t) -> p g z t", g=G, z=2) for u in range(2))
            k.kcH, k.kcL = sb2("kcH", [P, G, NCB], F16), sb2("kcL", [P, G, NCB], F16)
            sample_attention(k)
            k.end_stage()
            lr = Dense(k, "lrp", 8, ahead=in_tiles(*(COL['lx'] + m * P for m in range(4))))
            prompt_attention(k, lr)
            k.end_stage()
        gl = Dense(k, "glp", 13, ahead=in_tiles(COL['ga'], COL['gq'], COL['gq'] + P, COL['gk']))
        lru(k, lr, gl)
        k.end_stage()
        gla(k, gl)
        k.end_stage()
        with ExitStack() as tail:
            k.mH = tail.enter_context(nc.sbuf_tensor("mH", [P, KD, T], F16))
            k.mL = tail.enter_context(nc.sbuf_tensor("mL", [P, KD, T], F16))
            wo = Dense(k, "wo", KD, ahead=[w_tile(d['w_out'], i * P) for i in range(4)])
            merge(k, wo)
            k.end_stage()
            k.xT = tail.enter_context(nc.sbuf_tensor("xT2", [P, KD, T], F32))
            k.ssq = tail.enter_context(nc.sbuf_tensor("ssq", [P, T], F32))
            w_out(k, wo)
            k.end_stage()
            mp = Dense(k, "mp", 2 * FF // P, ahead=[w_tile(d['mlp_w1'], i * P) for i in range(4)])
            norm(k, "n2", VG2, mp)
            k.end_stage()
            mlp(k, mp)
            k.end_stage()
            final_norm(k)


OUTS = [('y_prompt', (1, SEQ, D)), ('y_sample', (NB, NS, D)),
        ('cmp_p', (1, 1, SEQ, 2, G, DH)), ('cmp_s', (1, NB, NS, 2, G, DH)),
        ('sel_p', (1, 1, SEQ, 2, G, DH)), ('sel_s', (1, NB, NS, 2, G, DH)),
        ('win_p', (1, 1, WIN, 2, G, DH)), ('win_s', (1, NB, WIN, 2, G, DH)),
        ('conv_p', (1, 1, 3, R)), ('conv_s', (1, NB, 3, R)), ('h_p', (1, 1, R)), ('h_s', (1, NB, R)),
        ('gla_p', (1, 1, GH, GK, GV)), ('gla_s', (1, NB, GH, GK, GV))]
SQUEEZED = ('w_in', 'b_in', 'w_branch', 'w_out', 'mlp_w1', 'mlp_w2', 'cache_nsa_cmp_kv', 'cache_nsa_sel_kv',
            'state_nsa_win_kv', 'state_lru_conv', 'state_lru_h', 'state_gla', 'nsa_cmp_pe', 'nsa_cmp_w1',
            'nsa_cmp_w2', 'lru_gate_w', 'gla_alpha_w')


def kernel(**inputs):
    import concourse.bacc as bacc
    from concourse.bass_utils import run_bass_kernel_spmd

    nc = bacc.Bacc("TRN2", target_bir_lowering=False, num_devices=1)
    arrays, d = {}, {}
    for name, a in list(inputs.items()) + [('consts', shape_constants())]:
        a = np.ascontiguousarray(a)
        arrays[f"in_{name}"] = a
        ap = nc.dram_tensor(f"in_{name}", a.shape, mybir.dt.from_np(a.dtype), kind="ExternalInput").ap()
        d[name] = ap[0] if name in SQUEEZED else ap
    for name, shape in OUTS:
        d['out_' + name] = nc.dram_tensor(f"out_{name}", shape, F32, kind="ExternalOutput").ap()
    build(nc, d)
    r = run_bass_kernel_spmd(nc, [arrays], core_ids=[0])
    return tuple(r.results[0][f"out_{n}"] for n, _ in OUTS)
```
